# Optimizing a Trainium2 kernel written in Bass

```python
import functools
import jax, jax.numpy as jnp
from jax import lax
import numpy as np

D_MODEL = 1024
BATCH = 1
SEQ = 512
DEPTH = 1
DEC_BATCH = 8
DEC_SEQ = 1
PAST_LEN = 4096
PAGE_SIZE = 128

PLE_DIM = 256
N_HEADS = 16
QK_NOPE = 64
QK_ROPE = 32
V_HEAD = 64
Q_LORA = 384
KV_LORA = 256
ROPE_THETA = 10000.0
ATTN_SCALE = (QK_NOPE + QK_ROPE) ** -0.5
Q_BLOCK = 128
C_CONV = 512
CONV_WIDTH = 31
CONV_STATE = CONV_WIDTH - 1
N_GROUPS = 4
EXPERTS_PER_GROUP = 8
N_EXPERTS = N_GROUPS * EXPERTS_PER_GROUP
TOP_K = 2
D_EXPERT = 256
MOE_BLOCK = 128
DN_ALPHA = (2 * DEPTH) ** 0.25
DN_BETA = (8 * DEPTH) ** -0.25
LN_EPS = 1e-5
RMS_EPS = 1e-6
NEG_INF = -1e30
OFF_KV = Q_LORA
OFF_KR = OFF_KV + KV_LORA
OFF_CONV = OFF_KR + QK_ROPE
OFF_GA = OFF_CONV + 2 * C_CONV
OFF_GB = OFF_GA + D_MODEL
D_IN = OFF_GB + D_MODEL
IN_OFFSETS = (OFF_KV, OFF_KR, OFF_CONV, OFF_GA, OFF_GB)

kernel_name = "hybrid_conv_mla_hiermoe_deepnorm_step"

def layer_norm(x, g, b):
    xf = x.astype(jnp.float32)
    mu = jnp.mean(xf, axis=-1, keepdims=True)
    xc = xf - mu
    var = jnp.mean(xc * xc, axis=-1, keepdims=True)
    return (xc * lax.rsqrt(var + LN_EPS) * g + b).astype(x.dtype)

def rms_norm(x, g):
    xf = x.astype(jnp.float32)
    y = xf * lax.rsqrt(jnp.mean(xf * xf, axis=-1, keepdims=True) + RMS_EPS)
    return (y * g).astype(x.dtype)

def rope(x, pos):
    half = x.shape[-1] // 2
    inv = 1.0 / (ROPE_THETA ** (jnp.arange(half, dtype=jnp.float32) / half))
    ang = pos.astype(jnp.float32)[:, None] * inv[None, :]
    shp = (pos.shape[0],) + (1,) * (x.ndim - 3) + (half,)
    cos, sin = jnp.cos(ang).reshape(shp), jnp.sin(ang).reshape(shp)
    x1, x2 = x[..., :half], x[..., half:]
    return jnp.concatenate([x1 * cos - x2 * sin, x2 * cos + x1 * sin], axis=-1).astype(x.dtype)

def latent_scores(q_lat, q_rope, c_kv, k_rope):
    s = jnp.einsum('bqhl,bkl->bhqk', q_lat, c_kv, preferred_element_type=jnp.float32)
    s = s + jnp.einsum('bqhr,bkr->bhqk', q_rope, k_rope, preferred_element_type=jnp.float32)
    return s * ATTN_SCALE

def mla_prompt_attend(q_lat, q_rope, c_kv, k_rope):
    s_len = q_lat.shape[1]
    pos = jnp.arange(s_len)
    outs = []
    for i in range(s_len // Q_BLOCK):
        q0, q1 = i * Q_BLOCK, (i + 1) * Q_BLOCK
        s = latent_scores(q_lat[:, q0:q1], q_rope[:, q0:q1], c_kv[:, :q1], k_rope[:, :q1])
        mask = pos[None, :q1] <= pos[q0:q1, None]
        p = jax.nn.softmax(jnp.where(mask, s, NEG_INF), axis=-1).astype(c_kv.dtype)
        outs.append(jnp.einsum('bhqk,bkl->bqhl', p, c_kv[:, :q1]))
    return jnp.concatenate(outs, axis=1)

def mla_sample_attend(q_lat, q_rope, c_kv, k_rope, cache_ckv, cache_krope, page_table, layer):
    bd, n_pages = page_table.shape
    past = n_pages * PAGE_SIZE
    ckv_past = cache_ckv[layer, page_table].reshape(bd, past, KV_LORA).astype(c_kv.dtype)
    kr_past = cache_krope[layer, page_table].reshape(bd, past, QK_ROPE).astype(k_rope.dtype)
    q_len = q_lat.shape[1]
    s_past = latent_scores(q_lat, q_rope, ckv_past, kr_past)
    s_new = latent_scores(q_lat, q_rope, c_kv, k_rope)
    causal = jnp.tril(jnp.ones((q_len, q_len), dtype=bool))
    s_new = jnp.where(causal, s_new, NEG_INF)
    p = jax.nn.softmax(jnp.concatenate([s_past, s_new], axis=-1), axis=-1).astype(c_kv.dtype)
    return (jnp.einsum('bhqk,bkl->bqhl', p[..., :past], ckv_past)
            + jnp.einsum('bhqk,bkl->bqhl', p[..., past:], c_kv))

def hier_moe(x, w_group, w_router, w_gate, w_up, w_down):
    b, s, d = x.shape
    h = x.reshape(b * s, d)
    t = h.shape[0]
    lg = (h @ w_group).astype(jnp.float32)
    pg = jax.nn.softmax(lg, axis=-1)
    g_idx = jnp.argmax(lg, axis=-1)
    pg_sel = jnp.take_along_axis(pg, g_idx[:, None], axis=1)
    le = (h @ w_router).astype(jnp.float32).reshape(t, N_GROUPS, EXPERTS_PER_GROUP)
    le_sel = jnp.take_along_axis(le, g_idx[:, None, None], axis=1)[:, 0]
    top_v, top_i = lax.top_k(le_sel, TOP_K)
    gates = (pg_sel * jax.nn.softmax(top_v, axis=-1)).astype(x.dtype)
    eid = (g_idx[:, None] * EXPERTS_PER_GROUP + top_i).astype(jnp.int32)
    n_rows = t * TOP_K
    n_blocks = (n_rows + N_EXPERTS * (MOE_BLOCK - 1) + MOE_BLOCK - 1) // MOE_BLOCK
    e_flat = eid.reshape(n_rows)
    order = jnp.argsort(e_flat)
    e_sorted = e_flat[order]
    counts = jnp.bincount(e_flat, length=N_EXPERTS).astype(jnp.int32)
    starts = jnp.cumsum(counts) - counts
    pcounts = ((counts + MOE_BLOCK - 1) // MOE_BLOCK) * MOE_BLOCK
    pend = jnp.cumsum(pcounts)
    pstarts = pend - pcounts
    dest = pstarts[e_sorted] + (jnp.arange(n_rows, dtype=jnp.int32) - starts[e_sorted])
    rows = jnp.zeros((n_blocks * MOE_BLOCK, d), h.dtype).at[dest].set(h[order // TOP_K])
    block_start = jnp.arange(n_blocks, dtype=jnp.int32) * MOE_BLOCK
    block_expert = jnp.clip(jnp.searchsorted(pend, block_start, side='right'), 0, N_EXPERTS - 1)

    def block_ffn(args):
        xb, e = args
        return (jax.nn.silu(xb @ w_gate[e]) * (xb @ w_up[e])) @ w_down[e]

    yb = lax.map(block_ffn, (rows.reshape(n_blocks, MOE_BLOCK, d), block_expert))
    y_sorted = yb.reshape(n_blocks * MOE_BLOCK, d)[dest]
    y_assign = jnp.zeros((n_rows, d), yb.dtype).at[order].set(y_sorted)
    y = jnp.sum(y_assign.reshape(t, TOP_K, d) * gates[..., None], axis=1)
    return y.reshape(b, s, d).astype(x.dtype)

def trunk_layer(x, p, pos, conv_left, attend, lw):
    b, s, _ = x.shape
    h = x @ lw['w_in']
    cq, ckv, kr, conv_in, ga, gb = jnp.split(h, IN_OFFSETS, axis=-1)
    q = (rms_norm(cq, lw['q_norm_g']) @ lw['w_uq']).reshape(b, s, N_HEADS, QK_NOPE + QK_ROPE)
    q_nope = q[..., :QK_NOPE]
    q_rope = rope(q[..., QK_NOPE:], pos)
    c_kv = rms_norm(ckv, lw['kv_norm_g'])
    k_rope = rope(kr, pos)
    q_lat = jnp.einsum('bshn,lhn->bshl', q_nope, lw['w_uk'])
    o_lat = attend(q_lat, q_rope, c_kv, k_rope)
    o = jnp.einsum('bshl,lhv->bshv', o_lat, lw['w_uv']).reshape(b, s, N_HEADS * V_HEAD)
    branch_b = o @ lw['w_o_attn']
    ca, cb = jnp.split(conv_in, 2, axis=-1)
    u = ca * jax.nn.sigmoid(cb)
    ext = jnp.concatenate([conv_left.astype(u.dtype), u], axis=1)
    y = lax.conv_general_dilated(ext, lw['w_dw'][:, None, :].astype(ext.dtype), window_strides=(1,),
                                 padding='VALID', dimension_numbers=('NWC', 'WIO', 'NWC'),
                                 feature_group_count=C_CONV) + lw['b_dw']
    new_conv = ext[:, -CONV_STATE:]
    branch_a = jax.nn.silu(layer_norm(y, lw['conv_ln_g'], lw['conv_ln_b'])) @ lw['w_pw2']
    mix = (jax.nn.sigmoid(ga) * branch_a + jax.nn.sigmoid(gb) * branch_b) @ lw['w_out']
    x = layer_norm(DN_ALPHA * x + mix, lw['ln1_g'], lw['ln1_b'])
    ffn = hier_moe(x, lw['w_group'], lw['w_router'], lw['w_gate'], lw['w_up'], lw['w_down'])
    x = layer_norm(DN_ALPHA * x + ffn, lw['ln2_g'], lw['ln2_b'])
    ple = jax.nn.sigmoid(x @ lw['w_ple_gate']) * (p.astype(x.dtype) @ lw['w_ple_proj'])
    x = x + rms_norm(ple, lw['ple_norm_g'])
    return x, c_kv, k_rope, new_conv

def setup_inputs(seed: int = 0) -> dict:
    key = jax.random.key(seed)
    ks = iter(jax.random.split(key, 48))
    f32 = jnp.float32

    def nrm(shape, scale):
        return jax.random.normal(next(ks), shape, f32) * scale

    def gain(n):
        return 1.0 + nrm((DEPTH, n), 0.02)

    n_pages = PAST_LEN // PAGE_SIZE
    n_used = DEC_BATCH * n_pages
    n_pool = (5 * n_used) // 4
    d = D_MODEL
    out = {}
    out['x_prompt'] = nrm((BATCH, SEQ, d), 1.0)
    out['x_sample'] = nrm((DEC_BATCH, DEC_SEQ, d), 1.0)
    out['cache_ckv'] = nrm((DEPTH, n_pool, PAGE_SIZE, KV_LORA), 1.0)
    out['cache_krope'] = nrm((DEPTH, n_pool, PAGE_SIZE, QK_ROPE), 1.0)
    out['state_conv'] = nrm((DEPTH, DEC_BATCH, CONV_STATE, C_CONV), 0.5)
    out['page_table'] = jax.random.permutation(next(ks), n_pool)[:n_used].reshape(DEC_BATCH, n_pages).astype(jnp.int32)
    out['p_prompt'] = nrm((DEPTH, BATCH, SEQ, PLE_DIM), 1.0)
    out['p_sample'] = nrm((DEPTH, DEC_BATCH, DEC_SEQ, PLE_DIM), 1.0)
    out['w_in'] = nrm((DEPTH, d, D_IN), d ** -0.5)
    out['q_norm_g'] = gain(Q_LORA)
    out['w_uq'] = nrm((DEPTH, Q_LORA, N_HEADS * (QK_NOPE + QK_ROPE)), Q_LORA ** -0.5)
    out['kv_norm_g'] = gain(KV_LORA)
    out['w_uk'] = nrm((DEPTH, KV_LORA, N_HEADS, QK_NOPE), KV_LORA ** -0.5)
    out['w_uv'] = nrm((DEPTH, KV_LORA, N_HEADS, V_HEAD), KV_LORA ** -0.5)
    out['w_o_attn'] = nrm((DEPTH, N_HEADS * V_HEAD, d), (N_HEADS * V_HEAD) ** -0.5)
    out['w_dw'] = nrm((DEPTH, CONV_WIDTH, C_CONV), CONV_WIDTH ** -0.5)
    out['b_dw'] = nrm((DEPTH, C_CONV), 0.02)
    out['conv_ln_g'] = gain(C_CONV)
    out['conv_ln_b'] = nrm((DEPTH, C_CONV), 0.02)
    out['w_pw2'] = nrm((DEPTH, C_CONV, d), C_CONV ** -0.5)
    out['w_out'] = nrm((DEPTH, d, d), d ** -0.5 * DN_BETA)
    out['ln1_g'] = gain(d)
    out['ln1_b'] = nrm((DEPTH, d), 0.02)
    out['w_group'] = nrm((DEPTH, d, N_GROUPS), d ** -0.5)
    out['w_router'] = nrm((DEPTH, d, N_EXPERTS), d ** -0.5)
    out['w_gate'] = nrm((DEPTH, N_EXPERTS, d, D_EXPERT), d ** -0.5)
    out['w_up'] = nrm((DEPTH, N_EXPERTS, d, D_EXPERT), d ** -0.5)
    out['w_down'] = nrm((DEPTH, N_EXPERTS, D_EXPERT, d), D_EXPERT ** -0.5 * DN_BETA)
    out['ln2_g'] = gain(d)
    out['ln2_b'] = nrm((DEPTH, d), 0.02)
    out['w_ple_gate'] = nrm((DEPTH, d, d), d ** -0.5)
    out['w_ple_proj'] = nrm((DEPTH, PLE_DIM, d), PLE_DIM ** -0.5)
    out['ple_norm_g'] = gain(d)
    return out

def reference(x_prompt, x_sample, cache_ckv, cache_krope, state_conv, page_table, p_prompt, p_sample,
              w_in, q_norm_g, w_uq, kv_norm_g, w_uk, w_uv, w_o_attn, w_dw, b_dw, conv_ln_g, conv_ln_b,
              w_pw2, w_out, ln1_g, ln1_b, w_group, w_router, w_gate, w_up, w_down, ln2_g, ln2_b,
              w_ple_gate, w_ple_proj, ple_norm_g):
    past_len = page_table.shape[1] * PAGE_SIZE
    pos_prompt = jnp.arange(x_prompt.shape[1], dtype=jnp.int32)
    pos_sample = past_len + jnp.arange(x_sample.shape[1], dtype=jnp.int32)
    hp, hs = x_prompt, x_sample
    ckv_p, kr_p, conv_p, ckv_s, kr_s, conv_s = [], [], [], [], [], []
    for i in range(DEPTH):
        lw = dict(w_in=w_in[i], q_norm_g=q_norm_g[i], w_uq=w_uq[i], kv_norm_g=kv_norm_g[i],
                  w_uk=w_uk[i], w_uv=w_uv[i], w_o_attn=w_o_attn[i], w_dw=w_dw[i], b_dw=b_dw[i],
                  conv_ln_g=conv_ln_g[i], conv_ln_b=conv_ln_b[i], w_pw2=w_pw2[i], w_out=w_out[i],
                  ln1_g=ln1_g[i], ln1_b=ln1_b[i], w_group=w_group[i], w_router=w_router[i],
                  w_gate=w_gate[i], w_up=w_up[i], w_down=w_down[i], ln2_g=ln2_g[i], ln2_b=ln2_b[i],
                  w_ple_gate=w_ple_gate[i], w_ple_proj=w_ple_proj[i], ple_norm_g=ple_norm_g[i])
        zeros_left = jnp.zeros((hp.shape[0], CONV_STATE, C_CONV), hp.dtype)
        hp, c1, k1, v1 = trunk_layer(hp, p_prompt[i], pos_prompt, zeros_left, mla_prompt_attend, lw)
        sample_attend = functools.partial(mla_sample_attend, cache_ckv=cache_ckv, cache_krope=cache_krope,
                                          page_table=page_table, layer=i)
        hs, c2, k2, v2 = trunk_layer(hs, p_sample[i], pos_sample, state_conv[i], sample_attend, lw)
        ckv_p.append(c1); kr_p.append(k1); conv_p.append(v1)
        ckv_s.append(c2); kr_s.append(k2); conv_s.append(v2)
    return (hp, hs, jnp.stack(ckv_p), jnp.stack(kr_p), jnp.stack(conv_p),
            jnp.stack(ckv_s), jnp.stack(kr_s), jnp.stack(conv_s))


_drawn_inputs = setup_inputs


def setup_inputs(seed=0):
    import zlib

    import numpy as np

    out = dict(_drawn_inputs(seed))
    spreads = {}
    factors = {'cache_ckv': 8.0,
     'cache_krope': 8.0,
     'q_norm_g': 8.0,
     'kv_norm_g': 2.817,
     'b_dw': 8.0,
     'conv_ln_g': 8.0,
     'conv_ln_b': 8.0,
     'ln1_g': 3.089,
     'ln1_b': 3.184,
     'ln2_g': 11.232,
     'ln2_b': 11.931,
     'ple_norm_g': 14.034}
    for name, (base, spread) in spreads.items():
        noise = np.random.default_rng([zlib.crc32(name.encode()), seed]).standard_normal(out[name].shape)
        drawn = base * np.exp(spread * noise) if base else spread * noise
        out[name] = __import__('jax').numpy.asarray(drawn.astype(out[name].dtype))
    for name, factor in factors.items():
        out[name] = (out[name] * factor).astype(out[name].dtype)
    return out
```

```python
from contextlib import ExitStack

import numpy as np

import concourse.bass as bass
from concourse import mybir

F32 = mybir.dt.float32
I32 = mybir.dt.int32
U32 = mybir.dt.uint32
ALU = mybir.AluOpType
ACT = mybir.ActivationFunctionType
AX = mybir.AxisListType

P = 128
D = 1024
NPR = 512
NS = 8
T = NPR + NS
TH = T // 2
KD = D // P
QL, KVL, ROPE, NOPE, VH = 384, 256, 32, 64, 64
KQ, KKV = QL // P, KVL // P
HEADS = 16
PAIRS = HEADS // 2
CC = 512
KC = CC // P
CW = 31
NA = KKV + 1 + KQ + 2 * KC
B_CKV, B_KR, B_CQ, B_CA, B_CB = 0, KKV, KKV + 1, KKV + 1 + KQ, KKV + 1 + KQ + KC
PAIRW = 2 * KQ * P + 2 * KKV * P + 2 * KVL
PAGE, NPAGES = 128, 32
NPOOL = 5 * NS * NPAGES // 4
NEXP, NGRP, EPG, DE = 32, 4, 8, 256
CAP = 64
EPAIRS = NEXP // 2
OVB = 2 * T // CAP
SLOTS = (NEXP + OVB) * CAP
EW = KD * 2 * DE + 2 * D
TILES = 5
ROWS = [P, P, P, P, NS]
N_NRM, LN_STEPS, RND, FD = 10, 10, 9, 8
CONV_STEPS = KC * CW
N_INI = 6
R_EXP, R_EXP2, R_RANK, R_SLOT, R_STEPS = 12, 19, 29, 51, 57
H_X2, H_PLE, H_STEPS, HA_STEPS = 10, 11, 14, 6
SCALE = float((NOPE + ROPE) ** -0.5)
ALPHA = float(2.0 ** 0.25)
LN_EPS, RMS_EPS = 1e-5, 1e-6
BIG = 3.0e38
NEG = -1e30

CI, C1, CU, CM = 0, 128, 256, 384
CTHR = CM + 512
CGID = CTHR + 8
CEID = CGID + 32
CEB = CEID + 32
CM8 = CEB + 32
CTOK = CM8 + 16
CVAL = CTOK + 5
CBLK = CVAL + 5
CSEL = CBLK + 16
NCON = CSEL + 32
VQG, VKG, VBD, VLG, VLB, VDW = 0, 3, 5, 9, 13, 17
NVEC = VDW + KC * CW

A_MIX = 0
A_OT = 4160
A_XT = 8320
A_HT = 12480
A_SIGB = A_HT + B_CA * T
A_EXT = A_HT + NA * T
A_EXS = A_EXT + KC * (CW - 1 + NPR)
A_ACC = A_EXS + KC * NS * CW
A_TMP = A_ACC + KC * T + 80
A_PAIR = A_TMP + 3 * T + 8
A_QT = A_PAIR + 2 * PAIRW
A_KT = A_QT + 4 * T
A_V = A_KT + 4 * NPR
A_P = A_V + 2 * NPR
A_PT = A_P + 2 * 1280
A_KRING = A_PT + 2 * 2048
A_RQ = A_KRING + 2 * 3072
A_SML = A_RQ + T
A_END1 = A_SML + 2053
A_RC = A_PT + 80
A_RS = A_RC + T
A_ERING = A_PAIR
A_SG = A_ERING + 2 * 20 * P
A_S = A_SG + T
A_WUV = A_S + 4104
A_PC = A_WUV + 2048
A_PTS = A_PC + 512
A_OLAT = A_PTS + 512
A_OLT = A_OLAT + 256
A_WO = A_OLT + 512
A_WBIG = A_EXT
A_RT = A_WBIG + 8192
A_X1 = A_RT + 2048
A_LN = A_X1 + TILES * D
A_RW = A_LN + 2048
A_X1T = A_RW + 288
A_W0 = A_X1T + 1024
A_W1 = A_OT
A_XG = A_MIX
A_XGT = A_XG + 2048
A_HS = A_XGT + 1024
A_HTS = A_HS + 512
assert A_HTS + 256 <= A_OT
A_Y = A_W1 + 2 * EW
A_PLT = A_Y + 2048
assert A_PLT + 2 * T <= A_EXT
A_ROWS = A_LN
A_WPP = A_W1
A_PG = A_X1T
A_F = A_W0
ARENA = max(A_END1, A_W0 + 2 * EW)


def decoder_layer(nc, a, o):
    ctx = ExitStack()
    with ctx:
        def sb(name, shape, dt=F32):
            return ctx.enter_context(nc.sbuf_tensor(name, shape, dt))

        def sem(name):
            return ctx.enter_context(nc.semaphore(name))

        arena = sb("arena", [P, ARENA])
        ps = ctx.enter_context(nc.psum_tensor("ps", [P, 8, 512], F32))

        def at(off, n):
            return arena[:, off:off + n]

        con = sb("con", [P, NCON])
        vec = sb("vec", [P, NVEC])
        pages = sb("pages", [1, NS * NPAGES], I32)
        eps = sb("eps", [P, 2])
        ident, ones, utri, maskw = con[:, CI:CI + P], con[:, C1:C1 + P], con[:, CU:CU + P], con[:, CM:CM + 512]

        xT = at(A_XT, KD * T).rearrange("p (k t) -> p k t", k=KD)
        hT = at(A_HT, NA * T).rearrange("p (b t) -> p b t", b=NA)
        hTh = at(A_HT, NA * T).rearrange("p (b h t) -> p b h t", b=NA, h=2)
        w1 = at(A_KRING, 2 * KD * P).rearrange("p (s k m) -> p s k m", s=2, k=KD)
        ext = at(A_EXT, KC * (CW - 1 + NPR)).rearrange("p (c t) -> p c t", c=KC)
        exs = at(A_EXS, KC * NS * CW).rearrange("p (c b w) -> p c b w", c=KC, b=NS)
        aT = at(A_ACC, KC * T).rearrange("p (c t) -> p c t", c=KC)
        tmp = at(A_TMP, 3 * T).rearrange("p (c t) -> p c t", c=3)
        tmph = at(A_TMP, 3 * T).rearrange("p (c h t) -> p c h t", c=3, h=2)
        sq = at(A_P, 5 * T).rearrange("p (c t) -> p c t", c=5)
        exw = at(A_P, NS * CW)
        rq, rc, rsn = at(A_RQ, T), at(A_RC, T), at(A_RS, T)
        small = [A_SML]

        def take(n):
            small[0] += n
            return at(small[0] - n, n)

        mixT = at(A_MIX, KD * T).rearrange("p (k t) -> p k t", k=KD)
        mixh = at(A_MIX, KD * T).rearrange("p (k h t) -> p k h t", k=KD, h=2)
        oT = at(A_OT, KD * T).rearrange("p (k t) -> p k t", k=KD)
        sigB = at(A_SIGB, KD * T).rearrange("p (k t) -> p k t", k=KD)
        sigBh = at(A_SIGB, KD * T).rearrange("p (k h t) -> p k h t", k=KD, h=2)

        pw = at(A_PAIR, 2 * PAIRW).rearrange("p (s n) -> p s n", s=2)
        qT = at(A_QT, 4 * T).rearrange("p (s x t) -> p s x t", s=2, x=2)
        qTh = at(A_QT, 4 * T).rearrange("p (s x h t) -> p s x h t", s=2, x=2, h=2)
        kT = at(A_KT, 4 * NPR).rearrange("p (s x t) -> p s x t", s=2, x=2)
        vv = at(A_V, 2 * NPR).rearrange("p (s j v) -> p s j v", s=2, j=4)
        vf = at(A_V, 2 * NPR).rearrange("p (s n) -> p s n", s=2)
        prob = at(A_P, 2 * 1280).rearrange("p (x n) -> p x n", x=2)
        pT = at(A_PT, 2 * 2048).rearrange("p (x j q) -> p x j q", x=2, j=4)
        POFF = [0, 128, 384, 768]
        mx = sb("mx", [P, 2, 4])
        nb = sb("nb", [P, 2, 4])
        rs = sb("rs", [P, 2, 4])
        rr = sb("rr", [P, 2, 4])

        def sqc(c):
            return at(A_S + c * T, T)

        kring = at(A_KRING, 2 * 3072).rearrange("p (s n) -> p s n", s=2)
        qlat = take(KKV * NS * 32).rearrange("p (c b h) -> p c b h", c=KKV, b=NS)
        qrr = take(NS * HEADS).rearrange("p (b h) -> p b h", b=NS)
        qrs = take(NS * 32).rearrange("p (b h) -> p b h", b=NS)[0:32]
        qcur = take(KKV * 4 * 32).rearrange("p (c b h) -> p c b h", c=KKV, b=4)
        qrcur = take(4 * 32).rearrange("p (b h) -> p b h", b=4)[0:32]
        knew = sb("knew", [P, KKV, 4])
        krnew = sb("krnew", [32, 4])
        krs = sb("krs", [32, NS])
        S = at(A_S, 4104)
        wuv = at(A_WUV, 2048).rearrange("p (c n) -> p c n", c=KKV)
        pc = at(A_PC, 512).rearrange("p (s n) -> p s n", s=2)
        pts = at(A_PTS, 512).rearrange("p (s n) -> p s n", s=2)
        olat = at(A_OLAT, 256)
        olT = at(A_OLT, 512).rearrange("p (c r n) -> p c r n", c=KKV, r=2)
        ckvs = take(KVL)[0:NS]
        pnT = take(P)[0:NS]
        assert small[0] <= A_END1
        sm = sb("sm", [P, 8])
        rsum = sb("rsum", [P, 20])
        pnm = sb("pnm", [P, NS])
        er = at(A_ERING, 2 * 20 * P).rearrange("p (s k m) -> p s k m", s=2, k=20)
        sg = at(A_SG, T)
        sgh = at(A_SG, T).rearrange("p (h t) -> p h t", h=2)
        wo = at(A_WO, 2 * KD * P).rearrange("p (s k m) -> p s k m", s=2, k=KD)

        wbig = at(A_WBIG, KD * D).rearrange("p (k n) -> p k n", k=KD)
        wpp = at(A_WPP, 2 * D).rearrange("p (k n) -> p k n", k=2)
        x1 = at(A_X1, TILES * D).rearrange("p (t n) -> p t n", t=TILES)
        lnr = at(A_LN, 2 * D).rearrange("p (t n) -> p t n", t=2)
        rw = at(A_RW, KD * 36).rearrange("p (k n) -> p k n", k=KD)
        x1T = at(A_X1T, KD * P).rearrange("p (k n) -> p k n", k=KD)
        plT = at(A_PLT, 2 * T).rearrange("p (k t) -> p k t", k=2)
        bst = sb("bst", [P, 2, 6])
        mv = sb("mv", [P, 2])
        rstd = sb("rstd", [P, 2])
        rt = [A_RT]

        def route(n, dt=F32):
            rt[0] += n
            v = at(rt[0] - n, n)
            return v if dt == F32 else v.bitcast(dt)

        def by_tile(n, dt=F32):
            return route(TILES * n, dt).rearrange("p (t n) -> p t n", t=TILES)

        L = by_tile(40)
        gv, gi, ev, ei = by_tile(8), by_tile(8, U32), by_tile(8), by_tile(8, U32)
        gf = route(TILES)
        ms, ms2, ohs, pos, ef, gx, gg = (by_tile(n) for n in (32, 32, 32, 32, 2, 4, 4))
        oh = route(2 * TILES * 32).rearrange("p (k t e) -> p k t e", k=2, t=TILES)
        pf = route((TILES + 1) * 32).rearrange("p (t e) -> p t e", e=32)
        cmp8 = route(256).rearrange("p (e m) -> p e m", m=8)
        cnt, nov, oend, one32, dsl = (route(32) for _ in range(5))
        slotf = route(2 * TILES).rearrange("p (k t) -> p k t", k=2)
        assert rt[0] <= A_X1
        gates = sb("gates", [P, 2, TILES])
        slotu = sb("slotu", [P, 2, TILES], U32)
        ovf = sb("ovf", [1, 17])
        ovi = sb("ovi", [1, 17], I32)
        ovc = at(A_X1T, 512).rearrange("p (b e) -> p b e", b=16)[0:1]
        tokrow = at(A_X1T + 512, P)[0:SLOTS // P]
        idx = sb("idx", [P, SLOTS // P], U32)
        idc = sb("idc", [P, 2], U32)
        wx = [at(A_W0, 2 * EW).rearrange("p (x n) -> p x n", x=2), at(A_W1, 2 * EW).rearrange("p (x n) -> p x n", x=2)]
        xg = at(A_XG, 2 * D).rearrange("p (s n) -> p s n", s=2)
        xgT = at(A_XGT, KD * P).rearrange("p (k n) -> p k n", k=KD)
        sgE = at(A_HS, 256)
        hs = at(A_HS + 256, 256)
        htT = at(A_HTS, 256).rearrange("p (c n) -> p c n", c=2)
        yb = at(A_Y, 2 * D).rearrange("p (s n) -> p s n", s=2)
        ln2r = at(A_ROWS, 2 * D).rearrange("p (t n) -> p t n", t=2)
        pgr = at(A_PG, D)
        fb = at(A_F, 10 * D).rearrange("p (s n) -> p s n", s=10)
        fbT = at(A_F + 9 * D, D).rearrange("p (k n) -> p k n", k=KD)
        zrow = at(A_MIX, P)[0:SLOTS // P]

        x1d = nc.dram_tensor("x1_scratch", (T, D), F32, kind="Internal").ap()
        ybd = nc.dram_tensor("y_scratch", (SLOTS, D), F32, kind="Internal").ap()
        tokd = nc.dram_tensor("token_of_slot", (SLOTS, 1), F32, kind="Internal").ap()

        s_con = sem("s_con")
        s_x = sem("s_x")
        s_w1 = [sem("s_w1a"), sem("s_w1b")]
        s_ini = sem("s_ini")
        s_ha = sem("s_ha")
        s_ht = sem("s_ht")
        s_sq = sem("s_sq")
        s_ss = sem("s_ss")
        s_rt = sem("s_rt")
        s_kro = sem("s_kro")
        s_nrm = sem("s_nrm")
        s_u = sem("s_u")
        s_gl = sem("s_gl")
        s_cv = sem("s_cv")
        s_sc = sem("s_sc")
        s_ln = sem("s_ln")
        s_kf = sem("s_kf")
        s_sw = sem("s_sw")
        s_pw = [sem("s_pwa"), sem("s_pwb")]
        s_g = sem("s_g")
        s_ga = sem("s_ga")
        s_gd = sem("s_gd")
        s_s = sem("s_s")
        s_mx = sem("s_mx")
        s_nb = sem("s_nb")
        s_ex = sem("s_ex")
        s_rc = sem("s_rc")
        s_pr = sem("s_pr")
        s_tp = sem("s_tp")
        s_ta = sem("s_ta")
        s_td = sem("s_td")
        s_o = sem("s_o")
        s_ot = sem("s_ot")
        s_qs = sem("s_qs")
        s_qc = sem("s_qc")
        s_k = [sem("s_ka"), sem("s_kb")]
        s_wuv = sem("s_wuv")
        s_er = [sem("s_era"), sem("s_erb")]
        s_cm = sem("s_cm")
        s_sqc = sem("s_sqc")
        s_d = sem("s_d")
        s_da = sem("s_da")
        s_dd = sem("s_dd")
        s_sk = sem("s_sk")
        s_ske = sem("s_ske")
        s_rnd = sem("s_rnd")
        s_pcx = sem("s_pcx")
        s_pt = sem("s_pt")
        s_pte = sem("s_pte")
        s_ov = sem("s_ov")
        s_on = sem("s_on")
        s_os = sem("s_os")
        s_ose = sem("s_ose")
        s_wo = [sem("s_woa"), sem("s_wob")]
        s_b = sem("s_b")
        s_bt = sem("s_bt")
        s_mt = sem("s_mt")
        s_wb = sem("s_wb")
        s_f = sem("s_f")
        s_fd = sem("s_fd")
        s_fa = sem("s_fa")
        s_fx = sem("s_fx")
        s_fe = sem("s_fe")
        s_fl = sem("s_fl")
        s_x1 = sem("s_x1")
        s_r = sem("s_r")
        s_ra = sem("s_ra")
        s_rp = sem("s_rp")
        s_z = sem("s_z")
        s_tk = sem("s_tk")
        s_tl = sem("s_tl")
        s_out = sem("s_out")
        s_wx = [[sem("s_w00"), sem("s_w01")], [sem("s_w10"), sem("s_w11")]]
        s_plw = sem("s_plw")
        s_plg = sem("s_plg")
        s_gt = [[sem("s_gt00"), sem("s_gt01")], [sem("s_gt10"), sem("s_gt11")]]
        s_h = sem("s_h")
        s_hd = sem("s_hd")
        s_hsc = sem("s_hsc")
        s_yo = [sem("s_yoa"), sem("s_yob")]

        s_own = sem("s_own")

        class Moe:
            def __init__(self, n):
                self.ic = sem(n + "ic")
                self.xg = [sem(n + "xga"), sem(n + "xgb")]
                self.xt = sem(n + "xt")
                self.xa = sem(n + "xa")
                self.xd = sem(n + "xd")
                self.h = sem(n + "h")
                self.sg = sem(n + "sg")
                self.hs = sem(n + "hs")
                self.ht = sem(n + "ht")
                self.he = sem(n + "he")
                self.y = sem(n + "y")
                self.ya = sem(n + "ya")
                self.yd = sem(n + "yd")
                self.yw = [sem(n + "ywa"), sem(n + "ywb")]

        moe, ovm = Moe("m_"), Moe("o_")
        s_ovw = sem("s_ovw")
        s_ovr = sem("s_ovr")

        block = ctx.enter_context(nc.Block())

        @block.sync
        def _(sp):
            sp.dma_start(con[:], a["con"]).then_inc(s_con, 16)
            sp.dma_start(xT[:, 0:4], a["xT"][:, 0:4]).then_inc(s_x, 16)
            sp.dma_start(w1[:, 0], a["w1"][0]).then_inc(s_w1[0], 16)
            sp.dma_start(xT[:, 4:8], a["xT"][:, 4:8]).then_inc(s_x, 16)
            sp.dma_start(w1[:, 1], a["w1"][1]).then_inc(s_w1[1], 16)
            sp.dma_start(rq, a["rope"][0]).then_inc(s_con, 16)
            sp.dma_start(rc, a["rope"][1]).then_inc(s_con, 16)
            sp.dma_start(rsn, a["rope"][2]).then_inc(s_con, 16)
            sp.dma_start(vec[:], a["vec"]).then_inc(s_con, 16)
            sp.dma_start(pages[:], a["pages"]).then_inc(s_con, 16)
            sp.dma_start(exs[:], a["state"]).then_inc(s_con, 16)
            for s in range(2):
                sp.dma_start(pw[:, s], a["wpair"][s]).then_inc(s_pw[s], 16)
            with sp.Fori(1, NA // 2) as i:
                for s in range(2):
                    sp.wait_ge(s_ha, 2 * i + s - 1)
                    sp.dma_start(w1[:, s], a["w1"][bass.ds(2 * i + s, 1)].rearrange("a p k m -> (a p) k m")
                                 ).then_inc(s_w1[s], 16)
            sp.wait_ge(s_ini, 1)
            sp.dma_start(tokd.rearrange("(q p) o -> q (p o)", p=P), zrow[:]).then_inc(s_z, 16)
            with sp.Fori(1, PAIRS // 2) as i:
                for s in range(2):
                    sp.wait_ge(s_g, 4 * (2 * i + s - 1))
                    sp.dma_start(pw[:, s], a["wpair"][bass.ds(2 * i + s, 1)].rearrange("a p n -> (a p) n")
                                 ).then_inc(s_pw[s], 16)
            sp.wait_ge(s_nrm, N_NRM)
            sp.dma_start(o["ckv"], hT[:, B_CKV:B_CKV + KKV, :]).then_inc(s_out, 16)
            sp.dma_start(o["krope"], hT[64:96, B_KR, :]).then_inc(s_out, 16)
            sp.wait_ge(s_gl, 2 * KC)
            sp.dma_start(o["conv_p"], ext[:, :, NPR:NPR + CW - 1]).then_inc(s_out, 16)
            sp.dma_start(o["conv_s"], exs[:]).then_inc(s_out, 16)

            def page(r, bb, n):
                return sp.value_load(pages[0:1, bass.ds(4 * NPAGES * r + bb * NPAGES + n, 1)], min_val=0, max_val=NPOOL - 1)

            def k_pages(r, g, s):
                kk = kring[:, s, 0:2048].rearrange("p (b u n) -> p b u n", b=4, u=2)
                kr = kring[0:32, s, 2048:3072].rearrange("p (b u n) -> p b u n", b=4, u=2)
                for bb in range(4):
                    for u in range(2):
                        pg = page(r, bb, 2 * g + u)
                        sp.dma_start(kk[:, bb, u, :], a["kcT"][bass.ds(pg, 1)].rearrange("a p n -> (a p) n")
                                     ).then_inc(s_k[s], 16)
                        sp.dma_start(kr[:, bb, u, :], a["krT"][bass.ds(pg, 1)].rearrange("a p n -> (a p) n")
                                     ).then_inc(s_k[s], 16)

            def v_pages(r, g, s):
                kk = kring[:, s, 0:2048].rearrange("p (b u n) -> p b u n", b=4, u=2)
                for bb in range(4):
                    for u in range(2):
                        pg = page(r, bb, 2 * g + u)
                        sp.dma_start(kk[:, bb, u, :], a["vc"][bass.ds(pg, 1)].rearrange("a p n -> (a p) n")
                                     ).then_inc(s_k[s], 16)

            sp.wait_ge(s_con, 112)
            sp.wait_ge(s_ha, NA)
            sp.wait_ge(s_o, PAIRS)
            sp.wait_ge(s_z, 16)
            sp.dma_start(wuv[:], a["wuv"]).then_inc(s_wuv, 16)
            with sp.Fori(0, 2) as r:
                for g in range(2):
                    sp.wait_ge(s_ov, 2 + 17 * r - 1 + g)
                    k_pages(r, g, g)
                with sp.Fori(1, 8) as gg:
                    for s in range(2):
                        sp.wait_ge(s_sk, 17 * r + 2 * gg + s - 1)
                        k_pages(r, 2 * gg + s, s)
                for g in range(2):
                    sp.wait_ge(s_sk, 17 * r + 15 + g)
                    sp.sem_inc(s_own, 1)
                    v_pages(r, g, g)
                with sp.Fori(1, 8) as gg:
                    for s in range(2):
                        sp.wait_ge(s_ov, 2 + 17 * r + 2 * gg + s)
                        v_pages(r, 2 * gg + s, s)

            sp.wait_ge(s_d, 4 + 24)
            sp.wait_ge(s_os, 1)
            for s in range(2):
                sp.dma_start(wo[:, s], a["wo"][s]).then_inc(s_wo[s], 16)
            sp.wait_ge(s_out, 64)
            sp.dma_start(wbig[:], a["w_out"]).then_inc(s_wb, 16)
            sp.dma_start(rw[:], a["w_rt"]).then_inc(s_wb, 16)
            with sp.Fori(1, KD // 2) as i:
                for s in range(2):
                    sp.wait_ge(s_b, 2 * i + s - 1)
                    sp.dma_start(wo[:, s], a["wo"][bass.ds(2 * i + s, 1)].rearrange("a p k m -> (a p) k m")
                                 ).then_inc(s_wo[s], 16)
            sp.wait_ge(s_mt, KD)
            sp.dma_start(x1[:, 0:4], a["x"][0:NPR].rearrange("(t p) n -> p t n", p=P)).then_inc(s_wb, 16)
            sp.dma_start(x1[0:NS, 4], a["x"][NPR:T]).then_inc(s_wb, 16)
            sp.dma_start(lnr[:], a["lnrows"][:, 0:2]).then_inc(s_wb, 16)
            for x in range(2):
                sp.dma_start(wx[0][:, x], a["wexp"][x]).then_inc(s_wx[0][x], 16)
            for x in range(2):
                sp.dma_start(wx[1][:, x], a["wexp"][2 + x]).then_inc(s_wx[1][x], 16)
            for t in range(TILES):
                sp.wait_ge(s_fd, FD * (t + 1))
                sp.dma_start(x1d[t * P:t * P + ROWS[t]], x1[0:ROWS[t], t]).then_inc(s_x1, 16)
            sp.wait_ge(s_f, TILES)
            sp.dma_start(wbig[:], a["w_plg"]).then_inc(s_plg, 16)
            sp.dma_start(plT[:], a["plT"]).then_inc(s_plw, 16)
            sp.dma_start(ln2r[:], a["lnrows"][:, 2:4]).then_inc(s_plw, 16)
            sp.wait_ge(s_r, R_STEPS)
            sp.dma_start(pgr[:], a["lnrows"][:, 4]).then_inc(s_plw, 16)
            with sp.Fori(1, EPAIRS // 2) as i:
                for s in range(2):
                    sp.wait_ge(moe.y, 2 * i + s - 1)
                    for x in range(2):
                        sp.dma_start(wx[s][:, x], a["wexp"][bass.ds(4 * i + 2 * s + x, 1)].rearrange("a p n -> (a p) n")
                                     ).then_inc(s_wx[s][x], 16)
            sp.wait_ge(moe.y, EPAIRS)
            sp.dma_start(wpp[:], a["w_plp"]).then_inc(s_plw, 16)
            flag = sp.value_load(ovi[0:1, 16:17], min_val=0, max_val=OVB)
            with sp.If(flag > 0):
                with sp.Fori(0, OVB // 2) as i:
                    sp.wait_ge(s_ovr, i + 1)
                    sp.sem_inc(s_own, 1)
                    for x in range(2):
                        e = sp.value_load(ovi[0:1, bass.ds(2 * i + x, 1)], min_val=0, max_val=NEXP - 1)
                        sp.dma_start(wx[0][:, x], a["wexp"][bass.ds(e, 1)].rearrange("a p n -> (a p) n")
                                     ).then_inc(s_ovw, 16)
            with sp.Else():
                sp.wait_ge(moe.y, EPAIRS)
            for t in range(TILES):
                sp.wait_ge(s_hd, H_STEPS * (t + 1))
                sp.dma_start(o["y"][t * P:t * P + ROWS[t]], fb[0:ROWS[t], 6 + t % 2]).then_inc(s_yo[t % 2], 16)
            sp.wait_ge(s_yo[0], 48)
            sp.wait_ge(s_yo[1], 32)
            sp.wait_ge(s_out, 64)

        @block.tensor
        def _(pe):
            mm = nc.tensor.matmul
            tr = nc.tensor.transpose

            pe.wait_ge(s_x, 32)

            def a_block(b, s, n):
                pe.wait_ge(s_w1[s], 16 * n)
                if not (isinstance(b, int) and b < 2):
                    pe.wait_ge(s_ht, b - 1)
                for k in range(KD):
                    for h in range(2):
                        x = mm(ps[:, 2 * s + h, 0:TH], w1[:, s, k], xT[:, k, h * TH:(h + 1) * TH],
                               start=(k == 0), stop=(k == KD - 1))
                x.then_inc(s_ha, 1)

            for s in range(2):
                a_block(s, s, 1)
            with pe.Fori(1, NA // 2) as i:
                for s in range(2):
                    a_block(2 * i + s, s, i + 1)
            pe.wait_ge(s_con, 112)
            pe.wait_ge(s_sq, 1)
            for c in range(KKV):
                for h in range(2):
                    x = mm(ps[:, 4 + h, 0:TH], ones, sq[:, c, h * TH:(h + 1) * TH], start=(c == 0), stop=(c == KKV - 1))
            x.then_inc(s_ss, 1)
            pe.wait_ge(s_sq, 2)
            for c in range(KQ):
                for h in range(2):
                    x = mm(ps[:, 6 + h, 0:TH], ones, sq[:, KKV + c, h * TH:(h + 1) * TH], start=(c == 0),
                           stop=(c == KQ - 1))
            x.then_inc(s_ss, 1)

            WQ, WK, WV, WL = 0, 2 * KQ * P, 2 * KQ * P + KKV * P, 2 * KQ * P + 2 * KKV * P

            def gen_q(p, s, x, n):
                if x == 0:
                    pe.wait_ge(s_pw[s], 16 * n)
                    if isinstance(p, int) and p == 0:
                        pe.wait_ge(s_nrm, N_NRM)
                        pe.wait_ge(s_ht, NA)
                    else:
                        pe.wait_ge(s_gd, 6 * p)
                else:
                    pe.wait_ge(s_ga, 4 * p + 3)
                    pe.wait_ge(s_gd, 6 * p + 3)
                for k in range(KQ):
                    for h in range(2):
                        y = mm(ps[:, h, 0:TH], pw[:, s, WQ + (x * KQ + k) * P:WQ + (x * KQ + k + 1) * P],
                               hT[:, B_CQ + k, h * TH:(h + 1) * TH], start=(k == 0), stop=(k == KQ - 1))
                y.then_inc(s_g, 1)

            def gen_kv(p, s):
                pe.wait_ge(s_ga, 4 * p + 1)
                pe.wait_ge(s_gd, 6 * p + 2)
                for c in range(KKV):
                    mm(ps[:, 0, :], pw[:, s, WK + c * P:WK + (c + 1) * P], hT[:, B_CKV + c, 0:NPR],
                       start=(c == 0), stop=(c == KKV - 1))
                for j in range(4):
                    for c in range(KKV):
                        y = mm(ps[:, 1, j * P:(j + 1) * P], hT[:, B_CKV + c, j * P:(j + 1) * P],
                               pw[:, s, WV + c * P:WV + (c + 1) * P], start=(c == 0), stop=(c == KKV - 1))
                y.then_inc(s_g, 1)

            def gen_lat(p, s):
                pe.wait_ge(s_ga, 4 * p + 4)
                pe.wait_ge(s_gd, 6 * p + 5)
                for x in range(2):
                    for c in range(KKV):
                        y = mm(ps[:, 0, (2 * x + c) * NS:(2 * x + c + 1) * NS],
                               pw[0:64, s, WL + x * KVL + c * P:WL + x * KVL + (c + 1) * P],
                               qT[0:64, s, x, NPR:T], start=True, stop=True)
                y.then_inc(s_g, 1)

            def scores(p, s, x):
                hh = 2 * p + x
                if x == 0:
                    pe.wait_ge(s_gd, 6 * p + 5)
                    pe.wait_ge(s_ga, 4 * p + 4)
                    if isinstance(p, int) and p == 0:
                        pe.wait_ge(s_kf, 4)
                        pe.wait_ge(s_rt, 2)
                if not (isinstance(p, int) and hh == 0):
                    pe.wait_ge(s_mx, 4 * hh)
                for bank, tiles in ((2, (0, 2)), (3, (1,)), (4, (3,))):
                    for i in tiles:
                        c0 = P if i == 2 else 0
                        y = mm(ps[:, bank, c0:c0 + (i + 1) * P], qT[:, s, x, i * P:(i + 1) * P],
                               kT[:, s, x, 0:(i + 1) * P], start=True, stop=True)
                    y.then_inc(s_s, 1)

            def turn(p, s, x):
                hh = 2 * p + x
                for bank, tiles in ((5, (0, 2)), (7, (1,)), (6, (3,))):
                    pe.wait_ge(s_pr, 4 * hh + {5: 2, 7: 3, 6: 4}[bank])
                    if not (isinstance(p, int) and hh == 0):
                        if bank == 5:
                            pe.wait_ge(s_td, 2 * hh)
                        elif bank == 7:
                            pe.wait_ge(s_ta, 2 * hh)
                            if x == 0:
                                pe.wait_ge(s_ot, p)
                    for i in tiles:
                        c0 = P if i == 2 else 0
                        for j in range(i + 1):
                            y = tr(ps[:, bank, c0 + j * P:c0 + (j + 1) * P],
                                   prob[:, x, POFF[i] + j * P:POFF[i] + (j + 1) * P], ident)
                    y.then_inc(s_tp, 1)

            def values(p, s):
                pe.wait_ge(s_ta, 4 * (p + 1))
                pe.wait_ge(s_td, 4 * (p + 1))
                for j in range(4):
                    for x in range(2):
                        y = mm(ps[64 * x:64 * x + 64, 7, j * P:NPR], vv[:, s, j, 64 * x:64 * x + 64],
                               pT[:, x, j, j * P:NPR], start=(j == 0), stop=(j == 3))
                y.then_inc(s_o, 1)

            def pair(p, s, n, last=False):
                q = 1 - s
                scores(p, s, 0)
                if not last:
                    gen_q(p + 1, q, 0, n)
                    gen_kv(p + 1, q)
                turn(p, s, 0)
                scores(p, s, 1)
                if not last:
                    gen_q(p + 1, q, 1, n)
                    gen_lat(p + 1, q)
                turn(p, s, 1)
                values(p, s)

            gen_q(0, 0, 0, 1)
            gen_kv(0, 0)
            gen_q(0, 0, 1, 1)
            gen_lat(0, 0)
            pair(0, 0, 1)
            pair(1, 1, 2)
            with pe.Fori(1, PAIRS // 2 - 1) as i:
                pair(2 * i, 0, i + 1)
                pair(2 * i + 1, 1, i + 2)
            pair(PAIRS - 2, 0, PAIRS // 2)
            pair(PAIRS - 1, 1, PAIRS // 2, last=True)

            pe.wait_ge(s_gd, 6 * PAIRS)
            mm(ps[0:32, 0, 0:P], con[64:128, CSEL:CSEL + 32], qrr[64:128].rearrange("p b h -> p (b h)"),
               start=True, stop=True)
            for c in range(KKV):
                x = tr(ps[0:NS, 1, c * P:(c + 1) * P], hT[:, B_CKV + c, NPR:T], ident)
            x.then_inc(s_qs, 1)
            pe.wait_ge(s_cv, CONV_STEPS)
            pe.wait_ge(s_sc, 3 * KC)
            for c in range(KC):
                for h in range(2):
                    x = mm(ps[:, 2 + h, 0:TH], ones, aT[:, c, h * TH:(h + 1) * TH], start=(c == 0), stop=(c == KC - 1))
            x.then_inc(s_cm, 1)
            pe.wait_ge(s_sqc, KC)
            for c in range(KC):
                for h in range(2):
                    x = mm(ps[:, 4 + h, 0:TH], ones, sqc(c)[:, h * TH:(h + 1) * TH], start=(c == 0), stop=(c == KC - 1))
            x.then_inc(s_cm, 1)
            pe.wait_ge(s_qc, 3)
            pe.wait_ge(s_ln, LN_STEPS)
            pe.wait_ge(s_sqc, 2 * KC + 1)

            def unit(r, jj, u):
                s, slot = jj % 2, u % 2
                if u == 0:
                    pe.wait_ge(s_er[s], 32 * r + 16 * (jj // 2 + 1))
                    pe.wait_ge(s_da, 1 + 8 * r + 2 * jj)
                elif u == 1:
                    pe.wait_ge(s_dd, 1 + 4 * r + jj)
                else:
                    pe.wait_ge(s_da, 1 + 8 * r + 2 * jj + 1)
                w0, n = ((0, KD), (KD, KC), (KD + KC, KD))[u]
                for k in range(n):
                    for h in range(2):
                        mov = aT[:, k] if u == 1 else xT[:, k]
                        y = mm(ps[:, 2 * slot + h, 0:TH], er[:, s, w0 + k], mov[:, h * TH:(h + 1) * TH],
                               start=(k == 0), stop=(k == n - 1))
                y.then_inc(s_d, 1)

            def k_step(r, g):
                s = g % 2
                if g == 0:
                    pe.wait_ge(s_rnd, RND * r + 4)
                pe.wait_ge(s_ske, 1 + 17 * r + max(g - 1, 0))
                pe.wait_ge(s_k[s], 3072 * r + 256 * (g // 2 + 1))
                kk = kring[:, s, 0:2048].rearrange("p (b u c n) -> p b u c n", b=4, u=2, c=2)
                kr = kring[0:32, s, 2048:3072].rearrange("p (b n) -> p b n", b=4)
                for c in range(KKV):
                    for bb in range(4):
                        mm(ps[32 * bb:32 * bb + 32, 4 + s, 0:256], qcur[:, c, bb], kk[:, bb, :, c, :],
                           start=(c == 0), stop=False)
                for bb in range(4):
                    y = mm(ps[32 * bb:32 * bb + 32, 4 + s, 0:256], qrcur[:, bb], kr[:, bb],
                           start=False, stop=True)
                y.then_inc(s_sk, 1)

            def k_new(r):
                pe.wait_ge(s_ske, 1 + 17 * r + 15)
                for bb in range(4):
                    for c in range(KKV):
                        mm(ps[32 * bb:32 * bb + 32, 4, 0:1], qcur[:, c, bb], knew[:, c, bb:bb + 1],
                           start=(c == 0), stop=False)
                    y = mm(ps[32 * bb:32 * bb + 32, 4, 0:1], qrcur[:, bb], krnew[:, bb:bb + 1], start=False, stop=True)
                y.then_inc(s_sk, 1)

            def v_new(r):
                pe.wait_ge(s_rnd, RND * r + 7)
                pe.wait_ge(s_pte, 1 + 18 * r)
                tr(ps[0:NS, 6, 0:P], pnm[:, :], ident).then_inc(s_pt, 1)
                pe.wait_ge(s_pte, 1 + 18 * r + 1)
                pe.wait_ge(s_on, 1 + r)
                pe.sem_inc(s_own, 1)
                for bb in range(4):
                    y = mm(ps[32 * bb:32 * bb + 32, 7, 0:KVL], pnT[:, 32 * bb:32 * bb + 32], ckvs[:, :],
                           start=True, stop=False)
                y.then_inc(s_ov, 1)

            def v_step(r, g):
                s = g % 2
                pe.wait_ge(s_pcx, 17 * r + g + 2)
                pe.wait_ge(s_pte, 1 + 18 * r + g + 1)
                for u in range(2):
                    y = tr(ps[:, 6, u * P:(u + 1) * P], pc[:, s, u * P:(u + 1) * P], ident)
                y.then_inc(s_pt, 1)
                pe.wait_ge(s_pte, 1 + 18 * r + g + 2)
                pe.wait_ge(s_k[s], 3072 * r + 2048 + 128 * (g // 2 + 1))
                kk = kring[:, s, 0:2048].rearrange("p (b u n) -> p b u n", b=4, u=2)
                for u in range(2):
                    for bb in range(4):
                        y = mm(ps[32 * bb:32 * bb + 32, 7, 0:KVL], pts[:, s, u * P + 32 * bb:u * P + 32 * bb + 32],
                               kk[:, bb, u], start=False, stop=(g == 15 and u == 1))
                y.then_inc(s_ov, 1)

            def o_turn(r):
                pe.wait_ge(s_on, 1 + r + 1)
                for c in range(KKV):
                    y = tr(ps[:, 6, c * P:(c + 1) * P], olat[:, c * P:(c + 1) * P], ident)
                y.then_inc(s_pt, 1)

            def round_(r):
                for half in range(2):
                    for q in range(6):
                        unit(r, 2 * half + q // 3, q % 3)
                        lo, hi = (16 * q) // 6, (16 * (q + 1)) // 6
                        for g in range(lo, hi):
                            if half == 0:
                                k_step(r, g)
                            else:
                                if g == 0:
                                    v_new(r)
                                v_step(r, g)
                    if half == 0:
                        k_new(r)
                o_turn(r)

            pe.sem_inc(s_d, 4)
            pe.sem_inc(s_ov, 2)
            with pe.Fori(0, 2) as r:
                round_(r)

            pe.wait_ge(s_wuv, 16)
            pe.wait_ge(s_pte, 1 + 36)
            for hd in range(HEADS):
                x = hd % 2
                for c in range(KKV):
                    y = mm(ps[64 * x:64 * x + 64, 4, (hd // 2) * NS:(hd // 2 + 1) * NS],
                           wuv[:, c, hd * VH:(hd + 1) * VH],
                           olT[:, c].rearrange("p r (b h) -> p (r b) h", h=32)[:, :, hd],
                           start=(c == 0), stop=(c == KKV - 1))
            y.then_inc(s_os, 1)

            pe.wait_ge(s_ose, 1)
            pe.wait_ge(s_ot, PAIRS)

            def b_block(j, s, n):
                pe.wait_ge(s_wo[s], 16 * n)
                if isinstance(j, int) and j < 2:
                    pe.wait_ge(s_da, 1 + 16)
                    pe.wait_ge(s_dd, 1 + 8)
                else:
                    pe.wait_ge(s_bt, j - 1)
                for k in range(KD):
                    for h in range(2):
                        y = mm(ps[:, 2 * s + h, 0:TH], wo[:, s, k], oT[:, k, h * TH:(h + 1) * TH],
                               start=(k == 0), stop=(k == KD - 1))
                y.then_inc(s_b, 1)

            for s in range(2):
                b_block(s, s, 1)
            with pe.Fori(1, KD // 2) as i:
                for s in range(2):
                    b_block(2 * i + s, s, i + 1)

            def turn_x1(t):
                n = ROWS[t]
                pe.wait_ge(s_fd, FD * (t + 1))
                if t >= 1:
                    pe.wait_ge(s_fe, 2 * t)
                for k in range(KD):
                    y = tr(ps[:, 4 + k // 4, (k % 4) * P:(k % 4) * P + n], x1[0:n, t, k * P:(k + 1) * P], ident[0:n, 0:n])
                y.then_inc(s_fx, 1)
                pe.wait_ge(s_fe, 2 * (t + 1))
                if t >= 1:
                    pe.wait_ge(s_r, 2 * t)
                for k in range(KD):
                    y = mm(ps[0:n, 6, 0:36], x1T[:, k, 0:n], rw[:, k], start=(k == 0), stop=(k == KD - 1))
                y.then_inc(s_fl, 1)

            pe.wait_ge(s_wb, 80)
            pe.wait_ge(s_mt, KD)
            for t in range(TILES):
                n, s = ROWS[t], t % 2
                if t >= 2:
                    pe.wait_ge(s_fd, FD * (t - 2) + 1)
                for k in range(KD):
                    for h in range(2):
                        y = mm(ps[0:n, 2 * s + h, :], mixT[:, k, t * P:t * P + n], wbig[:, k, h * 512:(h + 1) * 512],
                               start=(k == 0), stop=(k == KD - 1))
                y.then_inc(s_f, 1)
                if t >= 1:
                    turn_x1(t - 1)
            turn_x1(TILES - 1)
            pe.wait_ge(s_r, R_RANK)
            flat = ohs[:].rearrange("p t e -> p (t e)")
            mm(ps[:, 7, 0:TILES * 32], utri, flat, start=True, stop=False)
            mm(ps[:, 7, 0:TILES * 32], ones, pf[:, 0:TILES].rearrange("p t e -> p (t e)"), start=False, stop=True)
            mm(ps[:, 7, 256:288], ones, pf[:, TILES], start=True, stop=True).then_inc(s_rp, 1)
            pe.wait_ge(s_tl, 16)
            tr(ps[:, 6, 0:SLOTS // P], tokrow[:, :], ident[0:SLOTS // P, 0:SLOTS // P]).then_inc(s_rp, 1)

            def experts(m, p, n, w, xslot, wwait, credit=0):
                pe.wait_ge(m.xg[xslot], 16 * n)
                if credit or not (isinstance(p, int) and p == 0):
                    pe.wait_ge(m.xa, p + credit)
                    pe.wait_ge(m.xd, p + credit)
                for k in range(KD):
                    y = tr(ps[:, k // 4, (k % 4) * P:(k % 4 + 1) * P], xg[:, xslot, k * P:(k + 1) * P], ident)
                y.then_inc(m.xt, 1)
                pe.wait_ge(m.xa, p + 1 + credit)
                pe.wait_ge(m.xd, p + 1 + credit)
                wwait()
                for k in range(KD):
                    for x in range(2):
                        y = mm(ps[64 * x:64 * x + 64, 2, :], xgT[:, k, 64 * x:64 * x + 64],
                               w[:, x, k * 512:(k + 1) * 512], start=(k == 0), stop=(k == KD - 1))
                y.then_inc(m.h, 1)
                pe.wait_ge(m.hs, p + 1)
                for c in range(2):
                    y = tr(ps[:, 4, c * P:(c + 1) * P], hs[:, c * P:(c + 1) * P], ident)
                y.then_inc(m.ht, 1)
                pe.wait_ge(m.he, p + 1)
                if credit or not (isinstance(p, int) and p == 0):
                    pe.wait_ge(m.ya, p + credit)
                    pe.wait_ge(m.yd, p + credit)
                for c in range(2):
                    for h in range(2):
                        for x in range(2):
                            o0 = KD * 512 + c * D + h * 512
                            y = mm(ps[64 * x:64 * x + 64, 6 + h, :], htT[:, c, 64 * x:64 * x + 64],
                                   w[:, x, o0:o0 + 512], start=(c == 0), stop=(c == 1))
                y.then_inc(m.y, 1)

            def main(p, s, n):
                def weights():
                    pe.wait_ge(s_wx[s][0], 16 * n)
                    pe.wait_ge(s_wx[s][1], 16 * n)
                experts(moe, p, n, wx[s], s, weights)

            pe.wait_ge(s_r, R_STEPS)
            for s in range(2):
                main(s, s, 1)
            with pe.Fori(1, EPAIRS // 2) as i:
                for s in range(2):
                    main(2 * i + s, s, i + 1)
            flag = pe.value_load(ovi[0:1, 16:17], min_val=0, max_val=OVB)
            with pe.If(flag > 0):
                pe.wait_ge(moe.ya, EPAIRS)
                pe.wait_ge(moe.yd, EPAIRS)
                with pe.Fori(0, OVB // 2) as i:
                    experts(ovm, i, i + 1, wx[0], 0, lambda: pe.wait_ge(s_ovw, 32 * i + 32), credit=1)
            with pe.Else():
                pe.wait_ge(moe.y, EPAIRS)

            for t in range(TILES):
                n = ROWS[t]
                if t == 0:
                    pe.wait_ge(s_plw, 64)
                    pe.wait_ge(s_plg, 16)
                else:
                    pe.wait_ge(s_hd, H_STEPS * (t - 1) + H_PLE)
                for k in range(2):
                    for h in range(2):
                        mm(ps[0:n, 2 + h, :], plT[:, k, t * P:t * P + n], wpp[:, k, h * 512:(h + 1) * 512],
                           start=(k == 0), stop=(k == 1))
                pe.wait_ge(s_hd, H_STEPS * t + H_X2)
                for k in range(KD):
                    y = tr(ps[:, 4 + k // 4, (k % 4) * P:(k % 4) * P + n], fb[0:n, 4, k * P:(k + 1) * P], ident[0:n, 0:n])
                y.then_inc(s_h, 1)
                pe.wait_ge(s_hsc, HA_STEPS * t + 3)
                for k in range(KD):
                    for h in range(2):
                        y = mm(ps[0:n, h, :], fbT[:, k, 0:n], wbig[:, k, h * 512:(h + 1) * 512],
                               start=(k == 0), stop=(k == KD - 1))
                y.then_inc(s_h, 1)

        @block.scalar
        def _(act):
            av = nc.scalar.activation
            for b in range(2):
                act.wait_ge(s_ha, b + 1)
                av(hTh[:, b], ps[:, 2 * b:2 * b + 2, 0:TH], ACT.Copy).then_inc(s_ht, 1)
            with act.Fori(1, NA // 2) as i:
                for s in range(2):
                    act.wait_ge(s_ha, 2 * i + s + 1)
                    av(hTh[:, bass.ds(2 * i + s, 1)].rearrange("p a h t -> p (a h) t"), ps[:, 2 * s:2 * s + 2, 0:TH],
                       ACT.Copy).then_inc(s_ht, 1)
            act.wait_ge(s_ht, NA)
            av(tmp[64:128, 0], hT[0:64, B_KR], ACT.Copy).then_inc(s_kro, 1)
            act.wait_ge(s_ini, N_INI)
            act.wait_ge(s_ss, 1)
            av(tmph[:, 1], ps[:, 4:6, 0:TH], ACT.Sqrt, bias=eps[:, 0:1], scale=1.0 / KVL).then_inc(s_rt, 1)
            act.wait_ge(s_ss, 2)
            av(tmph[:, 2], ps[:, 6:8, 0:TH], ACT.Sqrt, bias=eps[:, 0:1], scale=1.0 / QL).then_inc(s_rt, 1)
            for c in range(KC):
                av(hT[:, B_CB + c], hT[:, B_CB + c], ACT.Sigmoid).then_inc(s_u, 1)

            def out_q(p, s, x):
                act.wait_ge(s_g, 4 * p + 1 + 2 * x)
                av(qTh[0:64, s, x], ps[0:64, 0:2, 0:TH], ACT.Copy).then_inc(s_ga, 1)

            def out_k(p, s):
                act.wait_ge(s_g, 4 * p + 2)
                for x in range(2):
                    av(kT[0:64, s, x], ps[64 * x:64 * x + 64, 0, :], ACT.Copy).then_inc(s_ga, 1)

            def soft(p, x):
                hh = 2 * p + x
                for n, i in enumerate((0, 2, 1, 3)):
                    act.wait_ge(s_mx, 4 * hh + n + 1)
                    nc.scalar.mul(nb[:, x, i:i + 1], mx[:, x, i:i + 1], -SCALE).then_inc(s_nb, 1)
                    act.wait_ge(s_nb, 4 * hh + n + 1)
                    q = prob[:, x, POFF[i]:POFF[i] + (i + 1) * P]
                    av(q, q, ACT.Exp, bias=nb[:, x, i:i + 1], scale=SCALE, accum_out=rs[:, x, i:i + 1]).then_inc(s_ex, 1)

            def out_p(p, x):
                hh = 2 * p + x
                if not (isinstance(p, int) and p == 0):
                    act.wait_ge(s_o, p)
                for n, (bank, i) in enumerate(((7, 1), (6, 3))):
                    act.wait_ge(s_tp, 3 * hh + n + 2)
                    av(pT[:, x, 0:i + 1, i * P:(i + 1) * P], ps[:, bank, 0:(i + 1) * P].rearrange("p (j q) -> p j q", q=P),
                       ACT.Copy).then_inc(s_ta, 1)

            def pair(p, s, last=False):
                q = 1 - s
                soft(p, 0)
                if not last:
                    out_q(p + 1, q, 0)
                    out_k(p + 1, q)
                out_p(p, 0)
                soft(p, 1)
                if not last:
                    out_q(p + 1, q, 1)
                out_p(p, 1)
                act.wait_ge(s_o, p + 1)
                dst = oT[:, p, 0:NPR] if isinstance(p, int) else \
                    oT[:, bass.ds(p, 1), 0:NPR].rearrange("p a t -> p (a t)")
                av(dst, ps[:, 7, :], ACT.Copy).then_inc(s_ot, 1)

            out_q(0, 0, 0)
            out_k(0, 0)
            out_q(0, 0, 1)
            pair(0, 0)
            pair(1, 1)
            with act.Fori(1, PAIRS // 2 - 1) as i:
                pair(2 * i, 0)
                pair(2 * i + 1, 1)
            pair(PAIRS - 2, 0)
            pair(PAIRS - 1, 1, last=True)

            for c in range(KC):
                act.wait_ge(s_ln, 2 + c)
                av(sqc(c), aT[:, c], ACT.Square).then_inc(s_sqc, 1)
            act.wait_ge(s_cm, 2)
            av(tmph[:, 1], ps[:, 4:6, 0:TH], ACT.Sqrt, bias=eps[:, 1:2], scale=1.0 / CC).then_inc(s_sqc, 1)
            for c in range(KC):
                act.wait_ge(s_ln, 7 + c)
                av(aT[:, c], aT[:, c], ACT.Silu, bias=vec[:, VLB + c:VLB + c + 1],
                   scale=vec[:, VLG + c:VLG + c + 1]).then_inc(s_sqc, 1)

            act.sem_inc(s_da, 1)
            act.sem_inc(s_ske, 1)

            def gate(r, jj, u):
                act.wait_ge(s_d, 4 + 12 * r + 3 * jj + u + 1)
                if u == 0:
                    act.wait_ge(s_dd, 1 + 4 * r + jj)
                    av(sgh, ps[:, 0:2, 0:TH], ACT.Sigmoid).then_inc(s_da, 1)
                else:
                    av(sigBh[:, bass.ds(4 * r + jj, 1)].rearrange("p a h t -> p (a h) t"), ps[:, 0:2, 0:TH],
                       ACT.Sigmoid).then_inc(s_da, 1)

            with act.Fori(0, 2) as r:
                for half in range(2):
                    for q in range(6):
                        if q % 3 != 1:
                            gate(r, 2 * half + q // 3, q % 3)
                        for g in range((16 * q) // 6, (16 * (q + 1)) // 6):
                            if half == 0:
                                act.wait_ge(s_sk, 17 * r + g + 1)
                                av(S[:, g * 256:(g + 1) * 256], ps[:, 4 + g % 2, 0:256], ACT.Copy).then_inc(s_ske, 1)
                            else:
                                if g == 0:
                                    act.wait_ge(s_rnd, RND * r + 6)
                                    av(rsum[:, 16:17], S[:, 4096:4097], ACT.Exp, bias=sm[:, 1:2],
                                       scale=SCALE).then_inc(s_pcx, 1)
                                if g >= 2:
                                    act.wait_ge(s_pt, 18 * r + g)
                                av(pc[:, g % 2], S[:, g * 256:(g + 1) * 256], ACT.Exp, bias=sm[:, 1:2], scale=SCALE,
                                   accum_out=rsum[:, g:g + 1]).then_inc(s_pcx, 1)
                    if half == 0:
                        act.wait_ge(s_sk, 17 * r + 17)
                        av(S[:, 4096:4097], ps[:, 4, 0:1], ACT.Copy).then_inc(s_ske, 1)
            act.wait_ge(s_os, 1)
            av(oT[:, :, NPR:T], ps[:, 4, 0:PAIRS * NS].rearrange("p (k b) -> p k b", k=PAIRS), ACT.Copy).then_inc(s_ose, 1)

            def x1_out(t):
                n = ROWS[t]
                act.wait_ge(s_fx, t + 1)
                if t >= 1:
                    act.wait_ge(s_fl, t)
                for h in range(2):
                    av(x1T[:, 4 * h:4 * h + 4, 0:n], ps[:, 4 + h, :].rearrange("p (k n) -> p k n", k=4)[:, :, 0:n],
                       ACT.Copy).then_inc(s_fe, 1)

            for t in range(TILES):
                act.wait_ge(s_fd, FD * t + 4)
                av(rstd[0:ROWS[t], 0:1], mv[0:ROWS[t], 1:2], ACT.Sqrt, bias=eps[0:ROWS[t], 1:2]).then_inc(s_fa, 1)
                if t >= 1:
                    x1_out(t - 1)
            x1_out(TILES - 1)
            act.wait_ge(s_r, R_EXP)
            av(gg[:], gx[:], ACT.Exp).then_inc(s_ra, 1)
            act.wait_ge(s_r, R_EXP2)
            av(gf, gf, ACT.Exp).then_inc(s_ra, 1)

            def experts(m, p, xs, n, c=0):
                act.wait_ge(m.xt, p + 1 + c)
                av(xgT[:, 0:4], ps[:, 0, :].rearrange("p (k n) -> p k n", k=4), ACT.Copy).then_inc(m.xa, 1)
                act.wait_ge(m.h, p + 1)
                av(sgE, ps[:, 2, 0:DE], ACT.Silu).then_inc(m.sg, 1)
                act.wait_ge(m.y, p + 1)
                if not (isinstance(n, int) and n == 0):
                    act.wait_ge(m.yw[xs], 16 * n)
                av(yb[:, xs, 0:512], ps[:, 6, :], ACT.Copy).then_inc(m.ya, 1)
                act.wait_ge(m.ya, p + 1 + c)
                act.wait_ge(m.yd, p + 1 + c)
                q = p if c == 0 else EPAIRS + p
                rows = ybd[q * P:(q + 1) * P] if isinstance(q, int) else ybd[bass.ds(q * P, P)]
                act.dma_start(rows, yb[:, xs]).then_inc(m.yw[xs], 16)

            for s in range(2):
                experts(moe, s, s, 0)
            with act.Fori(1, EPAIRS // 2) as i:
                for s in range(2):
                    experts(moe, 2 * i + s, s, i)
            act.wait_ge(s_r, R_STEPS)
            flag = act.value_load(ovi[0:1, 16:17], min_val=0, max_val=OVB)
            with act.If(flag > 0):
                act.wait_ge(moe.yw[0], 16 * EPAIRS // 2)
                act.sem_inc(ovm.xa, 1)
                act.sem_inc(ovm.ya, 1)
                act.sem_inc(s_ovr, 1)
                with act.Fori(0, OVB // 2) as i:
                    experts(ovm, i, 0, 0, c=1)
                    act.wait_ge(ovm.yw[0], 16 * i + 16)
                    act.sem_inc(s_ovr, 1)
            with act.Else():
                act.wait_ge(moe.y, EPAIRS)

            for t in range(TILES):
                n = ROWS[t]
                act.wait_ge(s_hd, H_STEPS * t + 6)
                av(rstd[0:n, 0:1], mv[0:n, 1:2], ACT.Sqrt, bias=eps[0:n, 1:2]).then_inc(s_hsc, 1)
                act.wait_ge(s_h, 2 * t + 1)
                for h in range(2):
                    av(fbT[:, 4 * h:4 * h + 4, 0:n], ps[:, 4 + h, :].rearrange("p (k n) -> p k n", k=4)[:, :, 0:n],
                       ACT.Copy).then_inc(s_hsc, 1)
                act.wait_ge(s_h, 2 * t + 2)
                av(fb[0:n, 5], ps[0:n, 0:2, :].rearrange("p h n -> p (h n)"), ACT.Sigmoid).then_inc(s_hsc, 1)
                act.wait_ge(s_hd, H_STEPS * t + H_PLE)
                av(fb[0:n, 8], fb[0:n, 5], ACT.Square, accum_out=rstd[0:n, 0:1]).then_inc(s_hsc, 1)
                act.wait_ge(s_hsc, HA_STEPS * t + 5)
                av(rstd[0:n, 1:2], rstd[0:n, 0:1], ACT.Sqrt, bias=eps[0:n, 0:1], scale=1.0 / D).then_inc(s_hsc, 1)

        @block.vector
        def _(dve):
            v = nc.vector
            v.memset(zrow, 0.0).then_inc(s_ini, 1)
            v.memset(eps[:, 0:1], RMS_EPS).then_inc(s_ini, 1)
            v.memset(eps[:, 1:2], LN_EPS).then_inc(s_ini, 1)
            v.memset(ext[:, :, 0:CW - 1], 0.0).then_inc(s_ini, 1)
            v.memset(qlat, 0.0).then_inc(s_ini, 1)
            v.memset(qrs, 0.0).then_inc(s_ini, 1)
            dve.wait_ge(s_ht, KKV)
            h = hT[:, B_CKV:B_CKV + KKV]
            v.tensor_tensor(sq[:, 0:KKV], h, h, ALU.mult).then_inc(s_sq, 1)
            dve.wait_ge(s_ht, B_CQ + KQ)
            h = hT[:, B_CQ:B_CQ + KQ]
            v.tensor_tensor(sq[:, KKV:KKV + KQ], h, h, ALU.mult).then_inc(s_sq, 1)
            dve.wait_ge(s_con, 112)
            dve.wait_ge(s_kro, 1)
            kr = hT[64:128, B_KR]
            v.tensor_tensor(tmp[64:128, 0], tmp[64:128, 0], rsn[64:128], ALU.mult).then_inc(s_nrm, 1)
            v.tensor_tensor(kr, kr, rc[64:128], ALU.mult).then_inc(s_nrm, 1)
            dve.wait_ge(s_nrm, 2)
            v.tensor_tensor(kr, kr, tmp[64:128, 0], ALU.add).then_inc(s_nrm, 1)
            dve.wait_ge(s_rt, 1)
            v.reciprocal(tmp[:, 1], tmp[:, 1]).then_inc(s_nrm, 1)
            dve.wait_ge(s_nrm, 4)
            for c in range(KKV):
                h = hT[:, B_CKV + c]
                v.scalar_tensor_tensor(out=h, in0=h, scalar=vec[:, VKG + c:VKG + c + 1], in1=tmp[:, 1], op0=ALU.mult,
                                       op1=ALU.mult).then_inc(s_nrm, 1)
            dve.wait_ge(s_rt, 2)
            v.reciprocal(tmp[:, 2], tmp[:, 2]).then_inc(s_nrm, 1)
            dve.wait_ge(s_nrm, 7)
            for c in range(KQ):
                h = hT[:, B_CQ + c]
                v.scalar_tensor_tensor(out=h, in0=h, scalar=vec[:, VQG + c:VQG + c + 1], in1=tmp[:, 2], op0=ALU.mult,
                                       op1=ALU.mult).then_inc(s_nrm, 1)

            def glu():
                for c in range(KC):
                    dve.wait_ge(s_u, c + 1)
                    v.tensor_tensor(ext[:, c, CW - 1:CW - 1 + NPR], hT[:, B_CA + c, 0:NPR], hT[:, B_CB + c, 0:NPR],
                                    ALU.mult).then_inc(s_gl, 1)
                    v.tensor_tensor(exs[:, c, :, CW - 1], hT[:, B_CA + c, NPR:T], hT[:, B_CB + c, NPR:T],
                                    ALU.mult).then_inc(s_gl, 1)

            def conv_s():
                e3 = exw.rearrange("p (b w) -> p b w", b=NS)
                for c in range(KC):
                    w = vec[:, VDW + c * CW:VDW + (c + 1) * CW].unsqueeze(1).to_broadcast([P, NS, CW])
                    dve.wait_ge(s_gl, 2 * c + 2)
                    v.tensor_tensor(e3, exs[:, c], w, ALU.mult).then_inc(s_sc, 1)
                    dve.wait_ge(s_sc, 3 * c + 1)
                    v.tensor_reduce(aT[:, c, NPR:T], e3, AX.X, ALU.add).then_inc(s_sc, 1)
                    dve.wait_ge(s_sc, 3 * c + 2)
                    v.tensor_scalar(aT[:, c, NPR:T], aT[:, c, NPR:T], vec[:, VBD + c:VBD + c + 1], None,
                                    ALU.add).then_inc(s_sc, 1)

            def out_q(p, s, x):
                dve.wait_ge(s_g, 4 * p + 1 + 2 * x)
                v.tensor_tensor(qTh[64:128, s, x], ps[64:128, 0:2, 0:TH],
                                rq[64:128].rearrange("p (h t) -> p h t", h=2), ALU.mult).then_inc(s_gd, 1)
                dve.wait_ge(s_gd, 6 * p + 1 + 3 * x)
                dst = qrr[64:128, :, 2 * p + x] if isinstance(p, int) else \
                    qrr[64:128, :, bass.ds(2 * p + x, 1)].rearrange("p b a -> p (b a)")
                v.tensor_copy(dst, qT[64:128, s, x, NPR:T]).then_inc(s_gd, 1)

            def out_v(p, s):
                dve.wait_ge(s_g, 4 * p + 2)
                v.tensor_copy(vf[:, s], ps[:, 1, :]).then_inc(s_gd, 1)

            def out_lat(p):
                dve.wait_ge(s_g, 4 * p + 4)
                for x in range(2):
                    sl = slice(2 * p + x, 2 * p + x + 1) if isinstance(p, int) else bass.ds(2 * p + x, 1)
                    y = v.tensor_copy(qlat[:, :, :, sl].rearrange("p c b a -> p c (b a)"),
                                      ps[:, 0, 16 * x:16 * x + 16].rearrange("p (c b) -> p c b", b=NS))
                y.then_inc(s_gd, 1)

            def masks(p, x):
                hh = 2 * p + x
                if not (isinstance(p, int) and p == 0):
                    dve.wait_ge(s_tp, 3 * (hh - 1))
                for n, i in enumerate((0, 2, 1, 3)):
                    dve.wait_ge(s_s, 3 * hh + (1, 1, 2, 3)[n])
                    dve.sem_inc(s_own, 1)
                    bank, c0 = (2, 3, 2, 4)[i], P if i == 2 else 0
                    w = (i + 1) * P
                    v.tensor_tensor_reduce(prob[:, x, POFF[i]:POFF[i] + w], ps[:, bank, c0:c0 + w], maskw[:, 512 - w:512],
                                           1.0, -BIG, ALU.add, ALU.max, mx[:, x, i:i + 1]).then_inc(s_mx, 1)

            def scale(p, x):
                hh = 2 * p + x
                for n, i in enumerate((0, 2, 1, 3)):
                    dve.wait_ge(s_ex, 4 * hh + n + 1)
                    v.reciprocal(rr[:, x, i:i + 1], rs[:, x, i:i + 1]).then_inc(s_rc, 1)
                    dve.wait_ge(s_rc, 4 * hh + n + 1)
                    q = prob[:, x, POFF[i]:POFF[i] + (i + 1) * P]
                    v.tensor_scalar(q, q, rr[:, x, i:i + 1], None, ALU.mult).then_inc(s_pr, 1)

            def out_p(p, x):
                hh = 2 * p + x
                if not (isinstance(p, int) and p == 0):
                    dve.wait_ge(s_o, p)
                dve.wait_ge(s_tp, 3 * hh + 1)
                for i in (0, 2):
                    c0 = P if i == 2 else 0
                    v.tensor_copy(pT[:, x, 0:i + 1, i * P:(i + 1) * P],
                                  ps[:, 5, c0:c0 + (i + 1) * P].rearrange("p (j q) -> p j q", q=P)).then_inc(s_td, 1)

            def tap(p, n):
                w = 4 * p + n
                at_w = (lambda off, ln: slice(off + w, off + w + ln)) if isinstance(p, int) else \
                    (lambda off, ln: bass.ds(w + off, ln))
                for c in range(KC):
                    win, wt = ext[:, c, at_w(0, NPR)], vec[:, at_w(VDW + c * CW, 1)]
                    if isinstance(p, int) and w == 0:
                        dve.wait_ge(s_gl, 2 * c + 1)
                        y = v.tensor_scalar(aT[:, c, 0:NPR], win, wt, vec[:, VBD + c:VBD + c + 1], ALU.mult, ALU.add)
                    else:
                        dve.wait_ge(s_cv, KC * w - KC + c + 1)
                        y = v.scalar_tensor_tensor(out=aT[:, c, 0:NPR], in0=win, scalar=wt, in1=aT[:, c, 0:NPR],
                                                   op0=ALU.mult, op1=ALU.add)
                    y.then_inc(s_cv, 1)

            def pair(p, s, last=False):
                q = 1 - s
                masks(p, 0)
                if not last:
                    out_q(p + 1, q, 0)
                tap(p, 0)
                scale(p, 0)
                if not last:
                    out_v(p + 1, q)
                out_p(p, 0)
                tap(p, 1)
                masks(p, 1)
                if not last:
                    out_q(p + 1, q, 1)
                tap(p, 2)
                scale(p, 1)
                if not last:
                    out_lat(p + 1)
                out_p(p, 1)
                if not last:
                    tap(p, 3)

            out_q(0, 0, 0)
            out_v(0, 0)
            out_q(0, 0, 1)
            out_lat(0)
            glu()
            conv_s()
            pair(0, 0)
            pair(1, 1)
            with dve.Fori(1, PAIRS // 2 - 1) as i:
                pair(2 * i, 0)
                pair(2 * i + 1, 1)
            pair(PAIRS - 2, 0)
            pair(PAIRS - 1, 1, last=True)

            dve.wait_ge(s_qs, 1)
            v.tensor_copy(qrs[:, :, 0:HEADS], ps[0:32, 0, 0:P].rearrange("p (b h) -> p b h", b=NS)).then_inc(s_qc, 1)
            v.tensor_copy(ckvs, ps[0:NS, 1, 0:KVL]).then_inc(s_qc, 1)
            v.tensor_copy(krs[:], hT[64:96, B_KR, NPR:T]).then_inc(s_qc, 1)
            dve.wait_ge(s_cm, 1)
            v.tensor_scalar(tmph[:, 0], ps[:, 2:4, 0:TH], 1.0 / CC, None, ALU.mult).then_inc(s_ln, 1)
            dve.wait_ge(s_ln, 1)
            for c in range(KC):
                v.tensor_tensor(aT[:, c], aT[:, c], tmp[:, 0], ALU.subtract).then_inc(s_ln, 1)
            dve.wait_ge(s_sqc, KC + 1)
            v.reciprocal(tmp[:, 2], tmp[:, 1]).then_inc(s_ln, 1)
            dve.wait_ge(s_ln, 6)
            for c in range(KC):
                v.tensor_tensor(aT[:, c], aT[:, c], tmp[:, 2], ALU.mult).then_inc(s_ln, 1)

            dve.sem_inc(s_dd, 1)
            dve.sem_inc(s_on, 1)
            dve.sem_inc(s_pte, 1)
            dve.wait_ge(s_qc, 3)

            def gated(r, jj):
                dve.wait_ge(s_d, 4 + 12 * r + 3 * jj + 2)
                dve.wait_ge(s_da, 1 + 8 * r + 2 * jj + 1)
                v.tensor_tensor(mixh[:, bass.ds(4 * r + jj, 1)].rearrange("p a h t -> p (a h) t"),
                                ps[:, 2:4, 0:TH], sgh, ALU.mult).then_inc(s_dd, 1)

            with dve.Fori(0, 2) as r:
                v.tensor_copy(qcur, qlat[:, :, bass.ds(4 * r, 4), :]).then_inc(s_rnd, 1)
                v.tensor_copy(qrcur, qrs[:, bass.ds(4 * r, 4), :]).then_inc(s_rnd, 1)
                v.tensor_copy(knew[:], hT[:, B_CKV:B_CKV + KKV, bass.ds(NPR + 4 * r, 4)]).then_inc(s_rnd, 1)
                v.tensor_copy(krnew[:], krs[:, bass.ds(4 * r, 4)]).then_inc(s_rnd, 1)
                gated(r, 0)
                gated(r, 1)
                dve.wait_ge(s_ske, 1 + 17 * r + 17)
                v.tensor_reduce(sm[:, 0:1], S[:, 0:4097], AX.X, ALU.max).then_inc(s_rnd, 1)
                dve.wait_ge(s_rnd, RND * r + 5)
                v.tensor_scalar(sm[:, 1:2], sm[:, 0:1], -SCALE, None, ALU.mult).then_inc(s_rnd, 1)
                dve.wait_ge(s_pcx, 17 * r + 1)
                v.tensor_scalar(pnm[:], con[:, bass.ds(CM8 + NS * r, NS)], rsum[:, 16:17], None, ALU.mult).then_inc(s_rnd, 1)
                dve.wait_ge(s_pt, 18 * r + 1)
                v.tensor_copy(pnT, ps[0:NS, 6, 0:P]).then_inc(s_pte, 1)
                for g in range(16):
                    if g in (2, 10):
                        gated(r, 2 + (g == 10))
                    dve.wait_ge(s_pt, 18 * r + g + 2)
                    dve.wait_ge(s_ov, 2 + 17 * r + max(g - 1, 0))
                    v.tensor_copy(pts[:, g % 2], ps[:, 6, 0:256]).then_inc(s_pte, 1)
                dve.wait_ge(s_pcx, 17 * r + 17)
                v.tensor_reduce(sm[:, 3:4], rsum[:, 0:17], AX.X, ALU.add).then_inc(s_rnd, 1)
                dve.wait_ge(s_rnd, RND * r + 8)
                v.reciprocal(sm[:, 4:5], sm[:, 3:4]).then_inc(s_rnd, 1)
                dve.wait_ge(s_rnd, RND * r + 9)
                dve.wait_ge(s_ov, 2 + 17 * r + 17)
                v.tensor_scalar(olat, ps[:, 7, 0:KVL], sm[:, 4:5], None, ALU.mult).then_inc(s_on, 1)
                dve.wait_ge(s_pt, 18 * r + 18)
                v.tensor_copy(olT[:, :, bass.ds(r, 1)].rearrange("p c a n -> p c (a n)"),
                              ps[:, 6, 0:256].rearrange("p (c n) -> p c n", c=KKV)).then_inc(s_pte, 1)

            def b_block(j, s):
                dve.wait_ge(s_b, j + 1)
                sl = slice(j, j + 1) if isinstance(j, int) else bass.ds(j, 1)
                if not (isinstance(j, int) and j == 0):
                    dve.wait_ge(s_mt, j)
                v.tensor_tensor(sgh, ps[:, 2 * s:2 * s + 2, 0:TH],
                                sigBh[:, sl].rearrange("p a h t -> p (a h) t"), ALU.mult).then_inc(s_bt, 1)
                dve.wait_ge(s_bt, j + 1)
                m = mixT[:, sl].rearrange("p a t -> p (a t)")
                v.tensor_tensor(m, m, sg, ALU.add).then_inc(s_mt, 1)

            for s in range(2):
                b_block(s, s)
            with dve.Fori(1, KD // 2) as i:
                for s in range(2):
                    b_block(2 * i + s, s)

            def norm(n, x, stats_sem, base, root_sem, root_n, g, b):
                for hh in range(2):
                    v.bn_stats(bst[0:n, hh], x[:, hh * 512:(hh + 1) * 512]).then_inc(stats_sem, 1)
                dve.wait_ge(stats_sem, base + 2)
                v.bn_aggr(mv[0:n], bst[0:n].rearrange("p h s -> p (h s)")).then_inc(stats_sem, 1)
                dve.wait_ge(root_sem, root_n)
                v.reciprocal(rstd[0:n, 1:2], rstd[0:n, 0:1]).then_inc(stats_sem, 1)
                dve.wait_ge(stats_sem, base + 4)
                v.tensor_scalar(x, x, mv[0:n, 0:1], rstd[0:n, 1:2], ALU.subtract, ALU.mult).then_inc(stats_sem, 1)
                dve.wait_ge(stats_sem, base + 5)
                v.tensor_tensor(x, x, g[0:n], ALU.mult).then_inc(stats_sem, 1)
                dve.wait_ge(stats_sem, base + 6)
                v.tensor_tensor(x, x, b[0:n], ALU.add).then_inc(stats_sem, 1)

            def logits(t):
                n = ROWS[t]
                dve.wait_ge(s_fl, t + 1)
                v.tensor_copy(L[0:n, t, 0:4], ps[0:n, 6, 0:4]).then_inc(s_r, 1)
                v.tensor_copy(L[0:n, t, 8:40], ps[0:n, 6, 4:36]).then_inc(s_r, 1)

            v.memset(L, 0.0).then_inc(s_ini, 1)
            dve.wait_ge(s_ini, N_INI + 1)
            v.memset(L[:, :, 4:8], -BIG).then_inc(s_ini, 1)
            v.memset(one32, 1.0).then_inc(s_ini, 1)
            v.memset(pf[:, 0], 0.0).then_inc(s_ini, 1)
            dve.wait_ge(s_ini, N_INI + 4)
            dve.wait_ge(s_wb, 80)
            for t in range(TILES):
                n = ROWS[t]
                x = x1[0:n, t]
                dve.wait_ge(s_f, t + 1)
                v.scalar_tensor_tensor(out=x, in0=x, scalar=ALPHA,
                                       in1=ps[0:n, 2 * (t % 2):2 * (t % 2) + 2, :].rearrange("p h n -> p (h n)"),
                                       op0=ALU.mult, op1=ALU.add).then_inc(s_fd, 1)
                dve.wait_ge(s_fd, FD * t + 1)
                norm(n, x, s_fd, FD * t + 1, s_fa, t + 1, lnr[:, 0], lnr[:, 1])
                if t >= 1:
                    logits(t - 1)
            logits(TILES - 1)

            count = [2 * TILES]

            def step(ins):
                ins.then_inc(s_r, 1)
                count[0] += 1
                dve.wait_ge(s_r, count[0])

            dve.wait_ge(s_r, count[0])

            def b3(x, n):
                return x.unsqueeze(2).to_broadcast([P, TILES, n])

            def cb(off, n):
                return con[:, off:off + n].unsqueeze(1).to_broadcast([P, TILES, n])

            for t in range(TILES):
                v.max(gv[:, t], L[:, t, 0:8])
            step(v.tensor_copy(gx, L[:, :, 0:4]))
            for t in range(TILES):
                v.max_index(gi[:, t], gv[:, t], L[:, t, 0:8])
            step(v.tensor_tensor(gx, gx, b3(gv[:, :, 0], 4), ALU.subtract))
            assert count[0] == R_EXP
            step(v.tensor_copy(gf, gi[:, :, 0]))
            step(v.tensor_tensor(ms, cb(CGID, 32), b3(gf, 32), ALU.is_equal))
            step(v.tensor_scalar(ms2, ms, -1.0, BIG, ALU.add, ALU.mult))
            step(v.tensor_tensor(ms, ms, L[:, :, 8:40], ALU.mult))
            step(v.tensor_tensor(ms, ms, ms2, ALU.add))
            for t in range(TILES):
                v.max(ev[:, t], ms[:, t])
            step(v.tensor_copy(ms2, ms))
            for t in range(TILES):
                v.max_index(ei[:, t], ev[:, t], ms2[:, t])
            step(v.tensor_tensor(gf, ev[:, :, 1], ev[:, :, 0], ALU.subtract))
            assert count[0] == R_EXP2, count
            step(v.tensor_copy(ef, ei[:, :, 0:2]))
            for k in range(2):
                step(v.tensor_tensor(oh[:, k], cb(CEID, 32), b3(ef[:, :, k], 32), ALU.is_equal))
            step(v.tensor_tensor(ohs, oh[:, 0], oh[:, 1], ALU.add))
            step(v.tensor_tensor(ohs, ohs, b3(con[:, CVAL:CVAL + TILES], 32), ALU.mult))
            for t in range(TILES):
                step(v.tensor_tensor(pf[:, t + 1], pf[:, t], ohs[:, t], ALU.add))
            assert count[0] == R_RANK, count
            dve.wait_ge(s_ra, 1)
            step(v.tensor_reduce(gv[:, :, 0], gg, AX.X, ALU.add))
            step(v.reciprocal(gv[:, :, 1], gv[:, :, 0]))
            dve.wait_ge(s_ra, 2)
            step(v.tensor_scalar(gv[:, :, 2], gf, 1.0, None, ALU.add))
            step(v.reciprocal(gv[:, :, 3], gv[:, :, 2]))
            step(v.tensor_tensor(gates[:, 0], gv[:, :, 3], gv[:, :, 1], ALU.mult))
            step(v.tensor_tensor(gates[:, 1], gates[:, 0], gf, ALU.mult))
            dve.wait_ge(s_rp, 1)
            v.tensor_copy(cnt, ps[:, 7, 256:288])
            step(v.tensor_copy(pos, ps[:, 7, 0:TILES * 32].rearrange("p (t e) -> p t e", e=32)))
            step(v.tensor_tensor(cmp8, cnt.unsqueeze(2).to_broadcast([P, 32, 8]),
                                 con[:, CTHR:CTHR + 8].unsqueeze(1).to_broadcast([P, 32, 8]), ALU.is_gt))
            step(v.tensor_reduce(nov, cmp8, AX.X, ALU.add))
            step(v.tensor_tensor_scan(oend, one32, nov, 0.0, ALU.mult, ALU.add))
            step(v.tensor_tensor(dsl, oend, nov, ALU.subtract))
            step(v.tensor_scalar(dsl, dsl, float(CAP), float(CAP * (NEXP - 1)), ALU.mult, ALU.add))
            step(v.tensor_tensor(dsl, dsl, con[:, CEB:CEB + 32], ALU.subtract))
            step(v.tensor_scalar(ms, pos, float(CAP), None, ALU.is_ge))
            step(v.tensor_tensor(ms, ms, dsl.unsqueeze(1).to_broadcast([P, TILES, 32]), ALU.mult))
            step(v.tensor_tensor(pos, pos, cb(CEB, 32), ALU.add))
            step(v.tensor_tensor(pos, pos, ms, ALU.add))
            for k in range(2):
                step(v.tensor_tensor(ms, oh[:, k], pos, ALU.mult))
                step(v.tensor_reduce(slotf[:, k], ms, AX.X, ALU.add))
            step(v.tensor_copy(slotu[:], slotf))
            assert count[0] == R_SLOT, count
            step(v.tensor_tensor(ovc, oend[0:1].unsqueeze(1).to_broadcast([1, 16, 32]),
                                 con[0:1, CBLK:CBLK + 16].unsqueeze(2).to_broadcast([1, 16, 32]), ALU.is_le))
            step(v.tensor_reduce(ovf[:, 0:16], ovc, AX.X, ALU.add))
            step(v.tensor_scalar(ovf[:, 0:16], ovf[:, 0:16], float(NEXP - 1), None, ALU.min))
            step(v.tensor_copy(ovf[:, 16:17], oend[0:1, 31:32]))
            step(v.tensor_copy(ovi[:], ovf[:]))
            dve.wait_ge(s_rp, 2)
            step(v.tensor_copy(idx[:], ps[:, 6, 0:SLOTS // P]))
            assert count[0] == R_STEPS, count

            def experts(m, p, xs, n, c=0):
                dve.wait_ge(m.xt, p + 1 + c)
                v.tensor_copy(xgT[:, 4:8], ps[:, 1, :].rearrange("p (k n) -> p k n", k=4)).then_inc(m.xd, 1)
                dve.wait_ge(m.sg, p + 1)
                v.tensor_tensor(hs, ps[:, 2, DE:2 * DE], sgE, ALU.mult).then_inc(m.hs, 1)
                dve.wait_ge(m.ht, p + 1)
                v.tensor_copy(htT, ps[:, 4, 0:256].rearrange("p (c n) -> p c n", c=2)).then_inc(m.he, 1)
                dve.wait_ge(m.y, p + 1)
                if not (isinstance(n, int) and n == 0):
                    dve.wait_ge(m.yw[xs], 16 * n)
                v.tensor_copy(yb[:, xs, 512:1024], ps[:, 7, :]).then_inc(m.yd, 1)

            for s in range(2):
                experts(moe, s, s, 0)
            with dve.Fori(1, EPAIRS // 2) as i:
                for s in range(2):
                    experts(moe, 2 * i + s, s, i)
            flag = dve.value_load(ovi[0:1, 16:17], min_val=0, max_val=OVB)
            with dve.If(flag > 0):
                dve.wait_ge(moe.yw[0], 16 * EPAIRS // 2)
                dve.sem_inc(ovm.xd, 1)
                dve.sem_inc(ovm.yd, 1)
                with dve.Fori(0, OVB // 2) as i:
                    experts(ovm, i, 0, 0, c=1)
            with dve.Else():
                dve.wait_ge(moe.y, EPAIRS)

            dve.wait_ge(s_plw, 64)
            for t in range(TILES):
                n, b = ROWS[t], H_STEPS * t
                dve.wait_ge(s_gt[t % 2][0], 16 * (t // 2 + 1))
                v.tensor_scalar(fb[0:n, t % 2], fb[0:n, t % 2], gates[0:n, 0, t:t + 1], None, ALU.mult).then_inc(s_hd, 1)
                dve.wait_ge(s_hd, b + 1)
                dve.wait_ge(s_gt[t % 2][1], 16 * (t // 2 + 1))
                v.scalar_tensor_tensor(out=fb[0:n, 8], in0=fb[0:n, 2 + t % 2], scalar=gates[0:n, 1, t:t + 1],
                                       in1=fb[0:n, t % 2], op0=ALU.mult, op1=ALU.add).then_inc(s_hd, 1)
                dve.wait_ge(s_hd, b + 2)
                x = fb[0:n, 4]
                v.scalar_tensor_tensor(out=x, in0=x1[0:n, t], scalar=ALPHA, in1=fb[0:n, 8], op0=ALU.mult,
                                       op1=ALU.add).then_inc(s_hd, 1)
                dve.wait_ge(s_hd, b + 3)
                norm(n, x, s_hd, b + 3, s_hsc, HA_STEPS * t + 1, ln2r[:, 0], ln2r[:, 1])
                dve.wait_ge(s_hsc, HA_STEPS * t + 4)
                v.tensor_tensor(fb[0:n, 5], fb[0:n, 5], ps[0:n, 2:4, :].rearrange("p h n -> p (h n)"),
                                ALU.mult).then_inc(s_hd, 1)
                dve.wait_ge(s_hsc, HA_STEPS * t + 6)
                v.reciprocal(rstd[0:n, 1:2], rstd[0:n, 1:2]).then_inc(s_hd, 1)
                dve.wait_ge(s_hd, b + 12)
                if t >= 2:
                    dve.wait_ge(s_yo[t % 2], 16 * (t // 2))
                y = fb[0:n, 6 + t % 2]
                v.scalar_tensor_tensor(out=y, in0=fb[0:n, 5], scalar=rstd[0:n, 1:2], in1=pgr[0:n], op0=ALU.mult,
                                       op1=ALU.mult).then_inc(s_hd, 1)
                dve.wait_ge(s_hd, b + 13)
                v.tensor_tensor(y, y, x, ALU.add).then_inc(s_hd, 1)

        @block.gpsimd
        def _(pool):
            g = nc.gpsimd
            pool.wait_ge(s_nrm, 3)
            for s in range(2):
                for x in range(2):
                    g.tensor_copy(kT[64:128, s, x], hT[64:128, B_KR, 0:NPR]).then_inc(s_kf, 1)
            pool.wait_ge(s_o, PAIRS)
            with pool.Fori(0, KD // 2) as i:
                for s in range(2):
                    pool.wait_ge(s_d, 4 + 3 * (2 * i + s) - 3)
                    g.dma_start(er[:, s], a["wgate"][bass.ds(2 * i + s, 1)].rearrange("a p k m -> (a p) k m")
                                ).then_inc(s_er[s], 16)

            pool.wait_ge(s_z, 16)
            pool.wait_ge(s_r, R_SLOT)
            for t in range(TILES):
                n = ROWS[t]
                for k in range(2):
                    g.indirect_dma_start(tokd, bass.IndirectOffsetOnAxis(ap=slotu[0:n, k, t:t + 1], axis=0),
                                         con[0:n, CTOK + t:CTOK + t + 1], None).then_inc(s_tk, 16)
            pool.wait_ge(s_tk, 32 * TILES)
            pool.wait_ge(s_r, R_SLOT + 2)
            g.dma_start(tokrow, tokd.rearrange("(q p) o -> q (p o)", p=P)).then_inc(s_tl, 16)
            pool.wait_ge(s_r, R_STEPS)
            pool.wait_ge(s_x1, 16 * TILES)

            def gather(m, p, xs, c=0):
                q = p if c == 0 else EPAIRS + p
                sl = slice(q, q + 1) if isinstance(q, int) else bass.ds(q, 1)
                if c or not (isinstance(p, int) and p < 2):
                    pool.wait_ge(m.xt, p - 1 if c == 0 else p + 1)
                g.tensor_copy(idc[:, xs:xs + 1], idx[:, sl]).then_inc(m.ic, 1)
                pool.wait_ge(m.ic, p + 1)
                pool.sem_inc(s_own, 1)
                g.indirect_dma_start(xg[:, xs], None, x1d, bass.IndirectOffsetOnAxis(ap=idc[:, xs:xs + 1], axis=0)
                                     ).then_inc(m.xg[xs], 16)

            for s in range(2):
                gather(moe, s, s)
            with pool.Fori(1, EPAIRS // 2) as i:
                for s in range(2):
                    gather(moe, 2 * i + s, s)
            pool.wait_ge(moe.xt, EPAIRS)
            flag = pool.value_load(ovi[0:1, 16:17], min_val=0, max_val=OVB)
            with pool.If(flag > 0):
                pool.sem_inc(ovm.xt, 1)
                with pool.Fori(0, OVB // 2) as i:
                    gather(ovm, i, 0, c=1)
                pool.wait_ge(s_ovr, OVB // 2 + 1)
            with pool.Else():
                pool.wait_ge(moe.y, EPAIRS)
            pool.wait_ge(moe.yw[0], 16 * EPAIRS // 2)
            pool.wait_ge(moe.yw[1], 16 * EPAIRS // 2)
            for t in range(TILES):
                n = ROWS[t]
                if t >= 2:
                    pool.wait_ge(s_hd, H_STEPS * (t - 2) + 2)
                for k in range(2):
                    g.indirect_dma_start(fb[0:n, 2 * k + t % 2], None, ybd,
                                         bass.IndirectOffsetOnAxis(ap=slotu[0:n, k, t:t + 1], axis=0)
                                         ).then_inc(s_gt[t % 2][k], 16)


def constants():
    con = np.zeros((P, NCON), np.float32)
    q = np.arange(P)
    con[:, CI:CI + P] = np.eye(P)
    con[:, C1:C1 + P] = 1.0
    con[:, CU:CU + P] = q[:, None] < q[None, :]
    con[:, CM + 384:CM + 512] = np.where(q[None, :] <= q[:, None], 0.0, NEG)
    con[:, CTHR:CTHR + 8] = CAP * np.arange(1, 9)
    con[:, CGID:CGID + 32] = np.arange(32) // EPG
    con[:, CEID:CEID + 32] = np.arange(32)
    con[:, CEB:CEB + 32] = CAP * np.arange(32)
    for r in range(2):
        con[:, CM8 + NS * r:CM8 + NS * (r + 1)] = (4 * r + q // 32)[:, None] == np.arange(NS)[None, :]
    for t in range(TILES):
        con[:, CTOK + t] = np.minimum(t * P + q, T - 1)
        con[:, CVAL + t] = t * P + q < T
    con[:, CBLK:CBLK + 16] = np.arange(16)
    for r in range(ROPE):
        con[64 + r, CSEL + r] = con[96 + r, CSEL + r] = 1.0
    half = ROPE // 2
    inv = (1.0 / (10000.0 ** (np.arange(half, dtype=np.float32) / half))).astype(np.float32)
    pos = np.concatenate([np.arange(NPR), np.full(NS, PAGE * NPAGES)]).astype(np.float32)
    ang = (pos[None, :] * inv[:, None]).astype(np.float32)
    c, s = np.cos(ang), np.sin(ang)
    c2, s2 = np.concatenate([c, c]), np.concatenate([-s, s])
    rope = np.zeros((3, P, T), np.float32)
    rope[0, 64:96], rope[0, 96:128] = c2, s2
    rope[1, 64:96] = rope[1, 96:128] = c2
    rope[2, 64:96] = rope[2, 96:128] = s2
    return con, rope


def chunks(w, p=P):
    return w.reshape(-1, p, w.shape[-1]).transpose(1, 0, 2)


def laid_out(i):
    x = np.concatenate([i["x_prompt"].reshape(NPR, D), i["x_sample"].reshape(NS, D)])
    w_in = i["w_in"][0]
    o_kv, o_kr, o_cv = QL, QL + KVL, QL + KVL + ROPE
    o_ga = o_cv + 2 * CC
    kr = w_in[:, o_kr:o_kr + ROPE]
    krs = np.concatenate([kr[:, 16:], kr[:, :16]], 1)
    first = np.concatenate([w_in[:, o_kv:o_kv + KVL], krs, krs, kr, kr, w_in[:, :QL], w_in[:, o_cv:o_cv + 2 * CC]], 1)

    def blocks(w):
        return chunks(w).reshape(P, -1, w.shape[1] // P, P).transpose(2, 0, 1, 3)

    uq = i["w_uq"][0].reshape(QL, HEADS, NOPE + ROPE)
    uq = np.concatenate([uq[..., :NOPE], uq[..., NOPE:], uq[..., NOPE + 16:], uq[..., NOPE:NOPE + 16]], -1)
    uq = uq.reshape(KQ, P, HEADS, P).transpose(2, 1, 0, 3)
    uq = uq.reshape(PAIRS, 2, P, KQ * P).transpose(0, 2, 1, 3).reshape(PAIRS, P, 2 * KQ * P)
    uk, uv = i["w_uk"][0], i["w_uv"][0]

    def by_pair(w):
        return w.reshape(KKV, P, PAIRS, 2 * w.shape[-1]).transpose(2, 1, 0, 3).reshape(PAIRS, P, -1)

    ukt = np.zeros((PAIRS, P, 2, KVL), np.float32)
    ukt[:, :NOPE] = uk.transpose(2, 1, 0).reshape(NOPE, PAIRS, 2, KVL).transpose(1, 0, 2, 3)
    wpair = np.concatenate([uq, by_pair(uk), by_pair(uv), ukt.reshape(PAIRS, P, -1)], -1)
    gates = np.concatenate([blocks(w_in[:, o_ga:o_ga + D]), blocks(i["w_pw2"][0]), blocks(w_in[:, o_ga + D:])], 2)
    vec = np.concatenate([np.asarray(v).reshape(-1, P).T for v in
                          (i["q_norm_g"][0], i["kv_norm_g"][0], i["b_dw"][0], i["conv_ln_g"][0], i["conv_ln_b"][0])]
                         + [i["w_dw"][0].T.reshape(KC, P, CW).transpose(1, 0, 2).reshape(P, KC * CW)], 1)
    state = np.zeros((P, KC, NS, CW), np.float32)
    state[..., :CW - 1] = i["state_conv"][0].transpose(2, 0, 1).reshape(KC, P, NS, CW - 1).transpose(1, 0, 2, 3)
    ex = np.concatenate([i["w_gate"][0], i["w_up"][0]], -1).reshape(NEXP, KD, P, 2 * DE).transpose(0, 2, 1, 3)
    dn = i["w_down"][0].reshape(NEXP, 2, P, D).transpose(0, 2, 1, 3)
    con, rope = constants()
    rows = np.stack([i[n][0] for n in ("ln1_g", "ln1_b", "ln2_g", "ln2_b", "ple_norm_g")])
    ple = np.concatenate([i["p_prompt"][0].reshape(NPR, -1), i["p_sample"][0].reshape(NS, -1)])
    ckv = i["cache_ckv"][0]
    out = {
        "xT": chunks(x.T), "x": x, "w1": blocks(first), "wpair": wpair, "wgate": gates, "wo": blocks(i["w_o_attn"][0]),
        "wuv": chunks(uv.reshape(KVL, -1)), "w_out": chunks(i["w_out"][0]),
        "w_rt": chunks(np.concatenate([i["w_group"][0], i["w_router"][0]], 1)),
        "wexp": np.concatenate([ex.reshape(NEXP, P, -1), dn.reshape(NEXP, P, -1)], -1),
        "w_plg": chunks(i["w_ple_gate"][0]), "w_plp": chunks(i["w_ple_proj"][0]), "plT": chunks(ple.T),
        "kcT": ckv.transpose(0, 2, 1).reshape(NPOOL, KKV, P, PAGE).transpose(0, 2, 1, 3).reshape(NPOOL, P, -1),
        "krT": i["cache_krope"][0].transpose(0, 2, 1), "vc": ckv,
        "state": state, "vec": vec, "con": con, "rope": rope,
        "lnrows": np.broadcast_to(rows[None], (P, 5, D)), "pages": i["page_table"].reshape(1, -1),
    }
    return {n: np.ascontiguousarray(v) for n, v in out.items()}


OUTS = {"y": (T, D), "ckv": (P, KKV, T), "krope": (ROPE, T), "conv_p": (P, KC, CW - 1), "conv_s": (P, KC, NS, CW)}


def kernel(**inputs):
    import concourse.bacc as bacc
    from concourse.bass_utils import run_bass_kernel_spmd

    arrays = laid_out({n: np.asarray(v) for n, v in inputs.items()})
    nc = bacc.Bacc("TRN2", target_bir_lowering=False, num_devices=1)
    a = {n: nc.dram_tensor(f"in_{n}", v.shape, mybir.dt.from_np(v.dtype), kind="ExternalInput").ap()
         for n, v in arrays.items()}
    o = {n: nc.dram_tensor(f"out_{n}", s, F32, kind="ExternalOutput").ap() for n, s in OUTS.items()}
    decoder_layer(nc, a, o)
    r = run_bass_kernel_spmd(nc, [{f"in_{n}": v for n, v in arrays.items()}], core_ids=[0]).results[0]
    y, ckv, kr, cp, cs = (r[f"out_{n}"] for n in ("y", "ckv", "krope", "conv_p", "conv_s"))
    ckv = ckv.transpose(2, 1, 0).reshape(T, KVL)
    kr = kr.T
    cp = cp.transpose(2, 1, 0).reshape(CW - 1, CC)
    cs = cs[..., 1:].transpose(2, 3, 1, 0).reshape(NS, CW - 1, CC)
    return (y[:NPR].reshape(1, NPR, D), y[NPR:].reshape(NS, 1, D),
            ckv[:NPR].reshape(1, 1, NPR, KVL), kr[:NPR].reshape(1, 1, NPR, ROPE), cp.reshape(1, 1, CW - 1, CC),
            ckv[NPR:].reshape(1, NS, 1, KVL), kr[NPR:].reshape(1, NS, 1, ROPE), cs.reshape(1, NS, CW - 1, CC))
```

```python
from contextlib import ExitStack

import numpy as np

import concourse.bass as bass
from concourse import mybir

F32 = mybir.dt.float32
I32 = mybir.dt.int32
U32 = mybir.dt.uint32
ALU = mybir.AluOpType
ACT = mybir.ActivationFunctionType
AX = mybir.AxisListType

P = 128
D = 1024
NPR = 512
NS = 8
T = NPR + NS
TH = T // 2
KD = D // P
QL, KVL, ROPE, NOPE, VH = 384, 256, 32, 64, 64
KQ, KKV = QL // P, KVL // P
KR = (KVL + ROPE) // 3
HEADS = 16
PAIRS = HEADS // 2
CC = 512
KC = CC // P
CW = 31
NA = KKV + 1 + KQ + 2 * KC
B_CKV, B_KR, B_CQ, B_CA, B_CB = 0, KKV, KKV + 1, KKV + 1 + KQ, KKV + 1 + KQ + KC
PAIRW = 2 * KQ * P + 2 * KKV * P + 2 * KVL
PAGE, NPAGES = 128, 32
NPOOL = 5 * NS * NPAGES // 4
NEXP, NGRP, EPG, DE = 32, 4, 8, 256
CAP = 64
EPAIRS = NEXP // 2
OVB = 2 * T // CAP
SLOTS = (NEXP + OVB) * CAP
EW = KD * 2 * DE + 2 * D
TILES = 5
ROWS = [P, P, P, P, NS]
N_NRM, LN_STEPS, RND, FD = 10, 10, 13, 8
CONV_STEPS = KC * CW
N_INI = 6
R_EXP, R_EXP2, R_RANK, R_SLOT, R_STEPS = 12, 19, 29, 51, 57
H_X2, H_PLE, H_STEPS, HA_STEPS = 10, 11, 14, 6
SCALE = float((NOPE + ROPE) ** -0.5)
ALPHA = float(2.0 ** 0.25)
LN_EPS, RMS_EPS = 1e-5, 1e-6
BIG = 3.0e38
NEG = -1e30

CI, C1, CU, CM = 0, 128, 256, 384
CTHR = CM + 512
CGID = CTHR + 8
CEID = CGID + 32
CEB = CEID + 32
CM8 = CEB + 32
CTOK = CM8 + 16
CVAL = CTOK + 5
CBLK = CVAL + 5
CSEL = CBLK + 16
NCON = CSEL + 32
VQG, VKG, VBD, VLG, VLB, VDW = 0, 3, 5, 9, 13, 17
NVEC = VDW + KC * CW

A_MIX = 0
A_OT = 4160
A_XT = 8320
A_HT = 12480
A_SIGB = A_HT + B_CA * T
A_EXT = A_HT + NA * T
A_EXS = A_EXT + KC * (CW - 1 + NPR)
A_ACC = A_EXS + KC * NS * CW
A_TMP = A_ACC + KC * T + 80
A_PAIR = A_TMP + 3 * T + 8
A_QT = A_PAIR + 2 * PAIRW
A_KT = A_QT + 4 * T
A_V = A_KT + 4 * NPR
A_P = A_V + 2 * NPR
A_PT = A_P + 2 * 1280
A_KRING = A_PT + 2 * 2048
A_RQ = A_KRING + 2 * 3072
A_SML = A_RQ + T
A_END1 = A_SML + 2053
A_RC = A_PT + 80
A_RS = A_RC + T
A_ERING = A_PAIR
A_SG = A_ERING + 2 * 20 * P
A_S = A_SG + T
A_WUV = A_S + 4104
A_PC = A_WUV + 2048
A_PTS = A_PC + 512
A_OLAT = A_PTS + 512
A_OLT = A_OLAT + 256
A_WO = A_OLT + 512
A_WBIG = A_EXT
A_RT = A_WBIG + 8192
A_X1 = A_RT + 2048
A_LN = A_X1 + TILES * D
A_RW = A_LN + 2048
A_X1T = A_RW + 288
A_W0 = A_X1T + 1024
A_W1 = A_OT
A_XG = A_MIX
A_XGT = A_XG + 2048
A_HS = A_XGT + 1024
A_HTS = A_HS + 512
assert A_HTS + 256 <= A_OT
A_Y = A_W1 + 2 * EW
A_PLT = A_Y + 2048
assert A_PLT + 2 * T <= A_EXT
A_ROWS = A_LN
A_WPP = A_W1
A_PG = A_X1T
A_F = A_W0
ARENA = max(A_END1, A_W0 + 2 * EW)


def decoder_layer(nc, a, o):
    ctx = ExitStack()
    with ctx:
        def sb(name, shape, dt=F32):
            return ctx.enter_context(nc.sbuf_tensor(name, shape, dt))

        def sem(name):
            return ctx.enter_context(nc.semaphore(name))

        arena = sb("arena", [P, ARENA])
        ps = ctx.enter_context(nc.psum_tensor("ps", [P, 8, 512], F32))

        def at(off, n):
            return arena[:, off:off + n]

        con = sb("con", [P, NCON])
        vec = sb("vec", [P, NVEC])
        pages = sb("pages", [1, NS * NPAGES], I32)
        eps = sb("eps", [P, 2])
        ident, ones, utri, maskw = con[:, CI:CI + P], con[:, C1:C1 + P], con[:, CU:CU + P], con[:, CM:CM + 512]

        xT = at(A_XT, KD * T).rearrange("p (k t) -> p k t", k=KD)
        hT = at(A_HT, NA * T).rearrange("p (b t) -> p b t", b=NA)
        hTh = at(A_HT, NA * T).rearrange("p (b h t) -> p b h t", b=NA, h=2)
        w1 = at(A_KRING, 2 * KD * P).rearrange("p (s k m) -> p s k m", s=2, k=KD)
        ext = at(A_EXT, KC * (CW - 1 + NPR)).rearrange("p (c t) -> p c t", c=KC)
        exs = at(A_EXS, KC * NS * CW).rearrange("p (c b w) -> p c b w", c=KC, b=NS)
        aT = at(A_ACC, KC * T).rearrange("p (c t) -> p c t", c=KC)
        tmp = at(A_TMP, 3 * T).rearrange("p (c t) -> p c t", c=3)
        tmph = at(A_TMP, 3 * T).rearrange("p (c h t) -> p c h t", c=3, h=2)
        sq = at(A_P, 5 * T).rearrange("p (c t) -> p c t", c=5)
        exw = at(A_P, NS * CW)
        rq, rc, rsn = at(A_RQ, T), at(A_RC, T), at(A_RS, T)
        small = [A_SML]

        def take(n):
            small[0] += n
            return at(small[0] - n, n)

        mixT = at(A_MIX, KD * T).rearrange("p (k t) -> p k t", k=KD)
        mixh = at(A_MIX, KD * T).rearrange("p (k h t) -> p k h t", k=KD, h=2)
        oT = at(A_OT, KD * T).rearrange("p (k t) -> p k t", k=KD)
        sigB = at(A_SIGB, KD * T).rearrange("p (k t) -> p k t", k=KD)
        sigBh = at(A_SIGB, KD * T).rearrange("p (k h t) -> p k h t", k=KD, h=2)

        pw = at(A_PAIR, 2 * PAIRW).rearrange("p (s n) -> p s n", s=2)
        qT = at(A_QT, 4 * T).rearrange("p (s x t) -> p s x t", s=2, x=2)
        qTh = at(A_QT, 4 * T).rearrange("p (s x h t) -> p s x h t", s=2, x=2, h=2)
        kT = at(A_KT, 4 * NPR).rearrange("p (s x t) -> p s x t", s=2, x=2)
        vv = at(A_V, 2 * NPR).rearrange("p (s j v) -> p s j v", s=2, j=4)
        vf = at(A_V, 2 * NPR).rearrange("p (s n) -> p s n", s=2)
        prob = at(A_P, 2 * 1280).rearrange("p (x n) -> p x n", x=2)
        pT = at(A_PT, 2 * 2048).rearrange("p (x j q) -> p x j q", x=2, j=4)
        POFF = [0, 128, 384, 768]
        mx = sb("mx", [P, 2, 4])
        nb = sb("nb", [P, 2, 4])
        rs = sb("rs", [P, 2, 4])
        rr = sb("rr", [P, 2, 4])

        def sqc(c):
            return at(A_S + c * T, T)

        kring = at(A_KRING, 2 * 3072).rearrange("p (s n) -> p s n", s=2)
        qlat = take(KKV * NS * 32).rearrange("p (c b h) -> p c b h", c=KKV, b=NS)
        qrr = take(NS * HEADS).rearrange("p (b h) -> p b h", b=NS)
        qrs = take(NS * 32).rearrange("p (b h) -> p b h", b=NS)[0:32]
        qcur = take(3 * 4 * 32).rearrange("p (c b h) -> p c b h", c=3, b=4)[0:KR]
        knew = sb("knew", [KR, 3, 4])
        krs = sb("krs", [32, NS])
        S = at(A_S, 4104)
        wuv = at(A_WUV, 2048).rearrange("p (c n) -> p c n", c=KKV)
        pc = at(A_PC, 512).rearrange("p (s n) -> p s n", s=2)
        pts = at(A_PTS, 512).rearrange("p (s n) -> p s n", s=2)
        olat = at(A_OLAT, 256)
        olT = at(A_OLT, 512).rearrange("p (c r n) -> p c r n", c=KKV, r=2)
        ckvs = take(KVL)[0:NS]
        pnT = take(P)[0:NS]
        assert small[0] <= A_END1
        sm = sb("sm", [P, 8])
        rsum = sb("rsum", [P, 20])
        pnm = sb("pnm", [P, NS])
        er = at(A_ERING, 2 * 20 * P).rearrange("p (s k m) -> p s k m", s=2, k=20)
        sg = at(A_SG, T)
        sgh = at(A_SG, T).rearrange("p (h t) -> p h t", h=2)
        wo = at(A_WO, 2 * KD * P).rearrange("p (s k m) -> p s k m", s=2, k=KD)

        wbig = at(A_WBIG, KD * D).rearrange("p (k n) -> p k n", k=KD)
        wpp = at(A_WPP, 2 * D).rearrange("p (k n) -> p k n", k=2)
        x1 = at(A_X1, TILES * D).rearrange("p (t n) -> p t n", t=TILES)
        lnr = at(A_LN, 2 * D).rearrange("p (t n) -> p t n", t=2)
        rw = at(A_RW, KD * 36).rearrange("p (k n) -> p k n", k=KD)
        x1T = at(A_X1T, KD * P).rearrange("p (k n) -> p k n", k=KD)
        plT = at(A_PLT, 2 * T).rearrange("p (k t) -> p k t", k=2)
        bst = sb("bst", [P, 2, 6])
        mv = sb("mv", [P, 2])
        rstd = sb("rstd", [P, 2])
        rt = [A_RT]

        def route(n, dt=F32):
            rt[0] += n
            v = at(rt[0] - n, n)
            return v if dt == F32 else v.bitcast(dt)

        def by_tile(n, dt=F32):
            return route(TILES * n, dt).rearrange("p (t n) -> p t n", t=TILES)

        L = by_tile(40)
        gv, gi, ev, ei = by_tile(8), by_tile(8, U32), by_tile(8), by_tile(8, U32)
        gf = route(TILES)
        ms, ms2, ohs, pos, ef, gx, gg = (by_tile(n) for n in (32, 32, 32, 32, 2, 4, 4))
        oh = route(2 * TILES * 32).rearrange("p (k t e) -> p k t e", k=2, t=TILES)
        pf = route((TILES + 1) * 32).rearrange("p (t e) -> p t e", e=32)
        cmp8 = route(256).rearrange("p (e m) -> p e m", m=8)
        cnt, nov, oend, one32, dsl = (route(32) for _ in range(5))
        slotf = route(2 * TILES).rearrange("p (k t) -> p k t", k=2)
        assert rt[0] <= A_X1
        gates = sb("gates", [P, 2, TILES])
        slotu = sb("slotu", [P, 2, TILES], U32)
        ovf = sb("ovf", [1, 17])
        ovi = sb("ovi", [1, 17], I32)
        ovc = at(A_X1T, 512).rearrange("p (b e) -> p b e", b=16)[0:1]
        tokrow = at(A_X1T + 512, P)[0:SLOTS // P]
        idx = sb("idx", [P, SLOTS // P], U32)
        idc = sb("idc", [P, 2], U32)
        wx = [at(A_W0, 2 * EW).rearrange("p (x n) -> p x n", x=2), at(A_W1, 2 * EW).rearrange("p (x n) -> p x n", x=2)]
        xg = at(A_XG, 2 * D).rearrange("p (s n) -> p s n", s=2)
        xgT = at(A_XGT, KD * P).rearrange("p (k n) -> p k n", k=KD)
        sgE = at(A_HS, 256)
        hs = at(A_HS + 256, 256)
        htT = at(A_HTS, 256).rearrange("p (c n) -> p c n", c=2)
        yb = at(A_Y, 2 * D).rearrange("p (s n) -> p s n", s=2)
        ln2r = at(A_ROWS, 2 * D).rearrange("p (t n) -> p t n", t=2)
        pgr = at(A_PG, D)
        fb = at(A_F, 10 * D).rearrange("p (s n) -> p s n", s=10)
        fbT = at(A_F + 9 * D, D).rearrange("p (k n) -> p k n", k=KD)
        zeros = at(A_MIX, D)

        x1d = nc.dram_tensor("x1_scratch", (T, D), F32, kind="Internal").ap()
        ybd = nc.dram_tensor("y_scratch", (SLOTS, D), F32, kind="Internal").ap()
        tokd = nc.dram_tensor("token_of_slot", (SLOTS, 1), F32, kind="Internal").ap()

        s_con = sem("s_con")
        s_x = sem("s_x")
        s_w1 = [sem("s_w1a"), sem("s_w1b")]
        s_ini = sem("s_ini")
        s_ha = sem("s_ha")
        s_ht = sem("s_ht")
        s_sq = sem("s_sq")
        s_ss = sem("s_ss")
        s_rt = sem("s_rt")
        s_kro = sem("s_kro")
        s_nrm = sem("s_nrm")
        s_u = sem("s_u")
        s_gl = sem("s_gl")
        s_cv = sem("s_cv")
        s_sc = sem("s_sc")
        s_ln = sem("s_ln")
        s_kf = sem("s_kf")
        s_sw = sem("s_sw")
        s_pw = [sem("s_pwa"), sem("s_pwb")]
        s_g = sem("s_g")
        s_ga = sem("s_ga")
        s_gd = sem("s_gd")
        s_s = sem("s_s")
        s_mx = sem("s_mx")
        s_nb = sem("s_nb")
        s_ex = sem("s_ex")
        s_rc = sem("s_rc")
        s_pr = sem("s_pr")
        s_tp = sem("s_tp")
        s_ta = sem("s_ta")
        s_td = sem("s_td")
        s_o = sem("s_o")
        s_ot = sem("s_ot")
        s_qs = sem("s_qs")
        s_qc = sem("s_qc")
        s_k = [sem("s_ka"), sem("s_kb")]
        s_kp = [sem("s_kpa"), sem("s_kpb")]
        s_wuv = sem("s_wuv")
        s_er = [sem("s_era"), sem("s_erb")]
        s_cm = sem("s_cm")
        s_sqc = sem("s_sqc")
        s_d = sem("s_d")
        s_da = sem("s_da")
        s_dd = sem("s_dd")
        s_sk = sem("s_sk")
        s_ske = sem("s_ske")
        s_rnd = sem("s_rnd")
        s_pcx = sem("s_pcx")
        s_pt = sem("s_pt")
        s_pte = sem("s_pte")
        s_ov = sem("s_ov")
        s_on = sem("s_on")
        s_os = sem("s_os")
        s_ose = sem("s_ose")
        s_wo = [sem("s_woa"), sem("s_wob")]
        s_b = sem("s_b")
        s_bt = sem("s_bt")
        s_mt = sem("s_mt")
        s_wb = sem("s_wb")
        s_f = sem("s_f")
        s_fd = sem("s_fd")
        s_fa = sem("s_fa")
        s_fx = sem("s_fx")
        s_fe = sem("s_fe")
        s_fl = sem("s_fl")
        s_x1 = sem("s_x1")
        s_r = sem("s_r")
        s_ra = sem("s_ra")
        s_rp = sem("s_rp")
        s_z = sem("s_z")
        s_yz = sem("s_yz")
        s_tk = sem("s_tk")
        s_tl = sem("s_tl")
        s_out = sem("s_out")
        s_wx = [[sem("s_w00"), sem("s_w01")], [sem("s_w10"), sem("s_w11")]]
        s_plw = sem("s_plw")
        s_plg = sem("s_plg")
        s_gt = [[sem("s_gt00"), sem("s_gt01")], [sem("s_gt10"), sem("s_gt11")]]
        s_h = sem("s_h")
        s_hd = sem("s_hd")
        s_hsc = sem("s_hsc")
        s_yo = [sem("s_yoa"), sem("s_yob")]

        s_own = sem("s_own")

        class Moe:
            def __init__(self, n):
                self.ic = sem(n + "ic")
                self.xg = [sem(n + "xga"), sem(n + "xgb")]
                self.xt = sem(n + "xt")
                self.xa = sem(n + "xa")
                self.xd = sem(n + "xd")
                self.h = sem(n + "h")
                self.sg = sem(n + "sg")
                self.hs = sem(n + "hs")
                self.ht = sem(n + "ht")
                self.he = sem(n + "he")
                self.y = sem(n + "y")
                self.ya = sem(n + "ya")
                self.yd = sem(n + "yd")
                self.yw = [sem(n + "ywa"), sem(n + "ywb")]

        moe = Moe("m_")
        s_ovr = sem("s_ovr")

        def kpage(s, j):
            return kring[0:KR, s, j * 3 * P:(j + 1) * 3 * P]

        def vpage(s, j):
            return kring[:, s, j * KVL:(j + 1) * KVL]

        def overflow(eng, blocks, body):
            with eng.Fori(0, OVB // 4) as i:
                for s in range(2):
                    with eng.If(blocks > 4 * i + 2 * s):
                        body(EPAIRS + 2 * i + s, s, EPAIRS // 2 + i)

        block = ctx.enter_context(nc.Block())

        @block.sync
        def _(sp):
            sp.dma_start(con[:], a["con"]).then_inc(s_con, 16)
            sp.dma_start(xT[:, 0:4], a["xT"][:, 0:4]).then_inc(s_x, 16)
            sp.dma_start(w1[:, 0], a["w1"][0]).then_inc(s_w1[0], 16)
            sp.dma_start(xT[:, 4:8], a["xT"][:, 4:8]).then_inc(s_x, 16)
            sp.dma_start(w1[:, 1], a["w1"][1]).then_inc(s_w1[1], 16)
            sp.dma_start(rq, a["rope"][0]).then_inc(s_con, 16)
            sp.dma_start(rc, a["rope"][1]).then_inc(s_con, 16)
            sp.dma_start(rsn, a["rope"][2]).then_inc(s_con, 16)
            sp.dma_start(vec[:], a["vec"]).then_inc(s_con, 16)
            sp.dma_start(pages[:], a["pages"]).then_inc(s_con, 16)
            sp.dma_start(exs[:], a["state"]).then_inc(s_con, 16)
            for s in range(2):
                sp.dma_start(pw[:, s], a["wpair"][s]).then_inc(s_pw[s], 16)
            with sp.Fori(1, NA // 2) as i:
                for s in range(2):
                    sp.wait_ge(s_ha, 2 * i + s - 1)
                    sp.dma_start(w1[:, s], a["w1"][bass.ds(2 * i + s, 1)].rearrange("a p k m -> (a p) k m")
                                 ).then_inc(s_w1[s], 16)
            sp.wait_ge(s_ini, 1)
            sp.dma_start(tokd.rearrange("(q p) o -> q (p o)", p=P), zeros[0:SLOTS // P, 0:P]).then_inc(s_z, 16)
            sp.dma_start(ybd[NEXP * CAP:SLOTS].rearrange("(q p) n -> p q n", p=P),
                         zeros.unsqueeze(1).to_broadcast([P, OVB * CAP // P, D])).then_inc(s_yz, 16)
            with sp.Fori(1, PAIRS // 2) as i:
                for s in range(2):
                    sp.wait_ge(s_g, 4 * (2 * i + s - 1))
                    sp.dma_start(pw[:, s], a["wpair"][bass.ds(2 * i + s, 1)].rearrange("a p n -> (a p) n")
                                 ).then_inc(s_pw[s], 16)
            sp.wait_ge(s_nrm, N_NRM)
            sp.dma_start(o["ckv"], hT[:, B_CKV:B_CKV + KKV, :]).then_inc(s_out, 16)
            sp.dma_start(o["krope"], hT[64:96, B_KR, :]).then_inc(s_out, 16)
            sp.wait_ge(s_gl, 2 * KC)
            sp.dma_start(o["conv_p"], ext[:, :, NPR:NPR + CW - 1]).then_inc(s_out, 16)
            sp.dma_start(o["conv_s"], exs[:]).then_inc(s_out, 16)

            numbers = [sp.alloc_register(f"sp_page{j}") for j in range(4)]

            def k_pages(r, g, s):
                sp.load(numbers, pages[0:1, bass.ds(8 * (16 * r + g), 4)])
                for j in range(4):
                    pg = sp.snap(numbers[j], min_val=0, max_val=NPOOL - 1)
                    sp.dma_start(kpage(s, j), a["kT"][bass.ds(pg, 1)].rearrange("a p n -> (a p) n")).then_inc(s_k[s], 16)

            def v_pages(r, g, s):
                sp.load(numbers, pages[0:1, bass.ds(8 * (16 * r + g), 4)])
                for j in range(4):
                    pg = sp.snap(numbers[j], min_val=0, max_val=NPOOL - 1)
                    sp.dma_start(vpage(s, j), a["vc"][bass.ds(pg, 1)].rearrange("a p n -> (a p) n")).then_inc(s_k[s], 16)

            sp.wait_ge(s_con, 112)
            sp.wait_ge(s_ha, NA)
            sp.wait_ge(s_o, PAIRS)
            sp.wait_ge(s_z, 16)
            sp.dma_start(wuv[:], a["wuv"]).then_inc(s_wuv, 16)
            with sp.Fori(0, 2) as r:
                for g in range(2):
                    sp.wait_ge(s_ov, 2 + 17 * r - 1 + g)
                    sp.sem_inc(s_own, 1)
                    k_pages(r, g, g)
                with sp.Fori(1, 8) as gg:
                    for s in range(2):
                        sp.wait_ge(s_sk, 17 * r + 2 * gg + s - 1)
                        sp.sem_inc(s_own, 1)
                        k_pages(r, 2 * gg + s, s)
                for g in range(2):
                    sp.wait_ge(s_sk, 17 * r + 15 + g)
                    sp.sem_inc(s_own, 1)
                    v_pages(r, g, g)
                with sp.Fori(1, 8) as gg:
                    for s in range(2):
                        sp.wait_ge(s_ov, 2 + 17 * r + 2 * gg + s)
                        sp.sem_inc(s_own, 1)
                        v_pages(r, 2 * gg + s, s)

            sp.wait_ge(s_d, 4 + 24)
            sp.wait_ge(s_os, 1)
            for s in range(2):
                sp.dma_start(wo[:, s], a["wo"][s]).then_inc(s_wo[s], 16)
            sp.wait_ge(s_out, 64)
            sp.dma_start(wbig[:], a["w_out"]).then_inc(s_wb, 16)
            sp.dma_start(rw[:], a["w_rt"]).then_inc(s_wb, 16)
            with sp.Fori(1, KD // 2) as i:
                for s in range(2):
                    sp.wait_ge(s_b, 2 * i + s - 1)
                    sp.dma_start(wo[:, s], a["wo"][bass.ds(2 * i + s, 1)].rearrange("a p k m -> (a p) k m")
                                 ).then_inc(s_wo[s], 16)
            sp.wait_ge(s_mt, KD)
            sp.dma_start(x1[:, 0:4], a["x"][0:NPR].rearrange("(t p) n -> p t n", p=P)).then_inc(s_wb, 16)
            sp.dma_start(x1[0:NS, 4], a["x"][NPR:T]).then_inc(s_wb, 16)
            sp.dma_start(lnr[:], a["lnrows"][:, 0:2]).then_inc(s_wb, 16)
            for x in range(2):
                sp.dma_start(wx[0][:, x], a["wexp"][x]).then_inc(s_wx[0][x], 16)
            for x in range(2):
                sp.dma_start(wx[1][:, x], a["wexp"][2 + x]).then_inc(s_wx[1][x], 16)
            for t in range(TILES):
                sp.wait_ge(s_fd, FD * (t + 1))
                sp.dma_start(x1d[t * P:t * P + ROWS[t]], x1[0:ROWS[t], t]).then_inc(s_x1, 16)
            sp.wait_ge(s_f, TILES)
            sp.dma_start(wbig[:], a["w_plg"]).then_inc(s_plg, 16)
            sp.dma_start(plT[:], a["plT"]).then_inc(s_plw, 16)
            sp.dma_start(ln2r[:], a["lnrows"][:, 2:4]).then_inc(s_plw, 16)
            sp.wait_ge(s_r, R_STEPS)
            sp.dma_start(pgr[:], a["lnrows"][:, 4]).then_inc(s_plw, 16)
            with sp.Fori(1, EPAIRS // 2) as i:
                for s in range(2):
                    sp.wait_ge(moe.y, 2 * i + s - 1)
                    for x in range(2):
                        sp.dma_start(wx[s][:, x], a["wexp"][bass.ds(4 * i + 2 * s + x, 1)].rearrange("a p n -> (a p) n")
                                     ).then_inc(s_wx[s][x], 16)
            sp.wait_ge(s_r, R_STEPS)
            blocks = sp.value_load(ovi[0:1, 16:17], min_val=0, max_val=OVB)

            def weights(p, s, n):
                sp.wait_ge(moe.y, p - 1)
                sp.sem_inc(s_own, 1)
                for x in range(2):
                    e = sp.value_load(ovi[0:1, bass.ds(2 * (p - EPAIRS) + x, 1)], min_val=0, max_val=NEXP - 1)
                    sp.dma_start(wx[s][:, x], a["wexp"][bass.ds(e, 1)].rearrange("a p n -> (a p) n")
                                 ).then_inc(s_wx[s][x], 16)

            overflow(sp, blocks, weights)
            sp.wait_ge(s_ovr, 1)
            sp.dma_start(wpp[:], a["w_plp"]).then_inc(s_plw, 16)
            for t in range(TILES):
                sp.wait_ge(s_hd, H_STEPS * (t + 1))
                sp.dma_start(o["y"][t * P:t * P + ROWS[t]], fb[0:ROWS[t], 6 + t % 2]).then_inc(s_yo[t % 2], 16)
            sp.wait_ge(s_yo[0], 48)
            sp.wait_ge(s_yo[1], 32)
            sp.wait_ge(s_out, 64)

        @block.tensor
        def _(pe):
            mm = nc.tensor.matmul
            tr = nc.tensor.transpose

            pe.wait_ge(s_x, 32)

            def a_block(b, s, n):
                pe.wait_ge(s_w1[s], 16 * n)
                if not (isinstance(b, int) and b < 2):
                    pe.wait_ge(s_ht, b - 1)
                for k in range(KD):
                    for h in range(2):
                        x = mm(ps[:, 2 * s + h, 0:TH], w1[:, s, k], xT[:, k, h * TH:(h + 1) * TH],
                               start=(k == 0), stop=(k == KD - 1))
                x.then_inc(s_ha, 1)

            for s in range(2):
                a_block(s, s, 1)
            with pe.Fori(1, NA // 2) as i:
                for s in range(2):
                    a_block(2 * i + s, s, i + 1)
            pe.wait_ge(s_con, 112)
            pe.wait_ge(s_sq, 1)
            for c in range(KKV):
                for h in range(2):
                    x = mm(ps[:, 4 + h, 0:TH], ones, sq[:, c, h * TH:(h + 1) * TH], start=(c == 0), stop=(c == KKV - 1))
            x.then_inc(s_ss, 1)
            pe.wait_ge(s_sq, 2)
            for c in range(KQ):
                for h in range(2):
                    x = mm(ps[:, 6 + h, 0:TH], ones, sq[:, KKV + c, h * TH:(h + 1) * TH], start=(c == 0),
                           stop=(c == KQ - 1))
            x.then_inc(s_ss, 1)

            WQ, WK, WV, WL = 0, 2 * KQ * P, 2 * KQ * P + KKV * P, 2 * KQ * P + 2 * KKV * P

            def gen_q(p, s, x, n):
                if x == 0:
                    pe.wait_ge(s_pw[s], 16 * n)
                    if isinstance(p, int) and p == 0:
                        pe.wait_ge(s_nrm, N_NRM)
                        pe.wait_ge(s_ht, NA)
                    else:
                        pe.wait_ge(s_gd, 6 * p)
                else:
                    pe.wait_ge(s_ga, 4 * p + 3)
                    pe.wait_ge(s_gd, 6 * p + 3)
                for k in range(KQ):
                    for h in range(2):
                        y = mm(ps[:, h, 0:TH], pw[:, s, WQ + (x * KQ + k) * P:WQ + (x * KQ + k + 1) * P],
                               hT[:, B_CQ + k, h * TH:(h + 1) * TH], start=(k == 0), stop=(k == KQ - 1))
                y.then_inc(s_g, 1)

            def gen_kv(p, s):
                pe.wait_ge(s_ga, 4 * p + 1)
                pe.wait_ge(s_gd, 6 * p + 2)
                for c in range(KKV):
                    mm(ps[:, 0, :], pw[:, s, WK + c * P:WK + (c + 1) * P], hT[:, B_CKV + c, 0:NPR],
                       start=(c == 0), stop=(c == KKV - 1))
                for j in range(4):
                    for c in range(KKV):
                        y = mm(ps[:, 1, j * P:(j + 1) * P], hT[:, B_CKV + c, j * P:(j + 1) * P],
                               pw[:, s, WV + c * P:WV + (c + 1) * P], start=(c == 0), stop=(c == KKV - 1))
                y.then_inc(s_g, 1)

            def gen_lat(p, s):
                pe.wait_ge(s_ga, 4 * p + 4)
                pe.wait_ge(s_gd, 6 * p + 5)
                for x in range(2):
                    for c in range(KKV):
                        y = mm(ps[:, 0, (2 * x + c) * NS:(2 * x + c + 1) * NS],
                               pw[0:64, s, WL + x * KVL + c * P:WL + x * KVL + (c + 1) * P],
                               qT[0:64, s, x, NPR:T], start=True, stop=True)
                y.then_inc(s_g, 1)

            def scores(p, s, x):
                hh = 2 * p + x
                if x == 0:
                    pe.wait_ge(s_gd, 6 * p + 5)
                    pe.wait_ge(s_ga, 4 * p + 4)
                    if isinstance(p, int) and p == 0:
                        pe.wait_ge(s_kf, 4)
                        pe.wait_ge(s_rt, 2)
                if not (isinstance(p, int) and hh == 0):
                    pe.wait_ge(s_mx, 4 * hh)
                for bank, tiles in ((2, (0, 2)), (3, (1,)), (4, (3,))):
                    for i in tiles:
                        c0 = P if i == 2 else 0
                        y = mm(ps[:, bank, c0:c0 + (i + 1) * P], qT[:, s, x, i * P:(i + 1) * P],
                               kT[:, s, x, 0:(i + 1) * P], start=True, stop=True)
                    y.then_inc(s_s, 1)

            def turn(p, s, x):
                hh = 2 * p + x
                for bank, tiles in ((5, (0, 2)), (7, (1,)), (6, (3,))):
                    pe.wait_ge(s_pr, 4 * hh + {5: 2, 7: 3, 6: 4}[bank])
                    if not (isinstance(p, int) and hh == 0):
                        if bank == 5:
                            pe.wait_ge(s_td, 2 * hh)
                        elif bank == 7:
                            pe.wait_ge(s_ta, 2 * hh)
                            if x == 0:
                                pe.wait_ge(s_ot, p)
                    for i in tiles:
                        c0 = P if i == 2 else 0
                        for j in range(i + 1):
                            y = tr(ps[:, bank, c0 + j * P:c0 + (j + 1) * P],
                                   prob[:, x, POFF[i] + j * P:POFF[i] + (j + 1) * P], ident)
                    y.then_inc(s_tp, 1)

            def values(p, s):
                pe.wait_ge(s_ta, 4 * (p + 1))
                pe.wait_ge(s_td, 4 * (p + 1))
                for j in range(4):
                    for x in range(2):
                        y = mm(ps[64 * x:64 * x + 64, 7, j * P:NPR], vv[:, s, j, 64 * x:64 * x + 64],
                               pT[:, x, j, j * P:NPR], start=(j == 0), stop=(j == 3))
                y.then_inc(s_o, 1)

            def pair(p, s, n, first=False, last=False):
                q = 1 - s
                scores(p, s, 0)
                if not first:
                    turn(p - 1, q, 1)
                if not last:
                    gen_q(p + 1, q, 0, n)
                if not first:
                    values(p - 1, q)
                scores(p, s, 1)
                if not last:
                    gen_kv(p + 1, q)
                turn(p, s, 0)
                if not last:
                    gen_q(p + 1, q, 1, n)
                    gen_lat(p + 1, q)

            gen_q(0, 0, 0, 1)
            gen_kv(0, 0)
            gen_q(0, 0, 1, 1)
            gen_lat(0, 0)
            pair(0, 0, 1, first=True)
            pair(1, 1, 2)
            with pe.Fori(1, PAIRS // 2 - 1) as i:
                pair(2 * i, 0, i + 1)
                pair(2 * i + 1, 1, i + 2)
            pair(PAIRS - 2, 0, PAIRS // 2)
            pair(PAIRS - 1, 1, PAIRS // 2, last=True)
            turn(PAIRS - 1, 1, 1)
            values(PAIRS - 1, 1)

            pe.wait_ge(s_gd, 6 * PAIRS)
            mm(ps[0:32, 0, 0:P], con[64:128, CSEL:CSEL + 32], qrr[64:128].rearrange("p b h -> p (b h)"),
               start=True, stop=True)
            for c in range(KKV):
                x = tr(ps[0:NS, 1, c * P:(c + 1) * P], hT[:, B_CKV + c, NPR:T], ident)
            x.then_inc(s_qs, 1)
            pe.wait_ge(s_cv, CONV_STEPS)
            pe.wait_ge(s_sc, 3 * KC)
            for c in range(KC):
                for h in range(2):
                    x = mm(ps[:, 2 + h, 0:TH], ones, aT[:, c, h * TH:(h + 1) * TH], start=(c == 0), stop=(c == KC - 1))
            x.then_inc(s_cm, 1)
            pe.wait_ge(s_sqc, KC)
            for c in range(KC):
                for h in range(2):
                    x = mm(ps[:, 4 + h, 0:TH], ones, sqc(c)[:, h * TH:(h + 1) * TH], start=(c == 0), stop=(c == KC - 1))
            x.then_inc(s_cm, 1)
            pe.wait_ge(s_qc, 3)
            pe.wait_ge(s_ln, LN_STEPS)
            pe.wait_ge(s_sqc, 2 * KC + 1)

            def unit(r, jj, u):
                s, slot = jj % 2, u % 2
                if u == 0:
                    pe.wait_ge(s_er[s], 32 * r + 16 * (jj // 2 + 1))
                    pe.wait_ge(s_da, 1 + 8 * r + 2 * jj)
                elif u == 1:
                    pe.wait_ge(s_dd, 1 + 4 * r + jj)
                else:
                    pe.wait_ge(s_da, 1 + 8 * r + 2 * jj + 1)
                w0, n = ((0, KD), (KD, KC), (KD + KC, KD))[u]
                for k in range(n):
                    for h in range(2):
                        mov = aT[:, k] if u == 1 else xT[:, k]
                        y = mm(ps[:, 2 * slot + h, 0:TH], er[:, s, w0 + k], mov[:, h * TH:(h + 1) * TH],
                               start=(k == 0), stop=(k == n - 1))
                y.then_inc(s_d, 1)

            def k_step(r, g):
                s = g % 2
                if g == 0:
                    pe.wait_ge(s_rnd, RND * r + 8)
                pe.wait_ge(s_ske, 1 + 17 * r + max(g - 1, 0))
                pe.wait_ge(s_k[s], 1024 * r + 64 * (g // 2 + 1))
                pe.wait_ge(s_kp[s], 1024 * r + 64 * (g // 2 + 1))
                kk = kring[0:KR, s].rearrange("p (b u c n) -> p b u c n", b=4, u=2, c=3)
                for c in range(3):
                    for bb in range(4):
                        y = mm(ps[32 * bb:32 * bb + 32, 4 + s, 0:256], qcur[:, c, bb], kk[:, bb, :, c, :],
                               start=(c == 0), stop=(c == 2))
                y.then_inc(s_sk, 1)

            def k_new(r):
                pe.wait_ge(s_ske, 1 + 17 * r + 15)
                for bb in range(4):
                    for c in range(3):
                        y = mm(ps[32 * bb:32 * bb + 32, 4, 0:1], qcur[:, c, bb], knew[:, c, bb:bb + 1],
                               start=(c == 0), stop=(c == 2))
                y.then_inc(s_sk, 1)

            def v_new(r):
                pe.wait_ge(s_rnd, RND * r + 11)
                pe.wait_ge(s_pte, 1 + 18 * r)
                tr(ps[0:NS, 6, 0:P], pnm[:, :], ident).then_inc(s_pt, 1)
                pe.wait_ge(s_pte, 1 + 18 * r + 1)
                pe.wait_ge(s_on, 1 + r)
                pe.sem_inc(s_own, 1)
                for bb in range(4):
                    y = mm(ps[32 * bb:32 * bb + 32, 7, 0:KVL], pnT[:, 32 * bb:32 * bb + 32], ckvs[:, :],
                           start=True, stop=False)
                y.then_inc(s_ov, 1)

            def v_turn(r, g):
                s = g % 2
                pe.wait_ge(s_pcx, 17 * r + g + 2)
                if g == 0:
                    pe.wait_ge(s_ske, 1 + 17 * r + 17)
                elif g >= 2:
                    pe.wait_ge(s_pte, 1 + 18 * r + g)
                for u in range(2):
                    y = tr(ps[:, 4 + s, u * P:(u + 1) * P], pc[:, s, u * P:(u + 1) * P], ident)
                y.then_inc(s_pt, 1)

            def v_step(r, g):
                s = g % 2
                if g < 15:
                    v_turn(r, g + 1)
                pe.wait_ge(s_pte, 1 + 18 * r + g + 2)
                pe.wait_ge(s_k[s], 1024 * r + 512 + 64 * (g // 2 + 1))
                pe.wait_ge(s_kp[s], 1024 * r + 512 + 64 * (g // 2 + 1))
                kk = kring[:, s, 0:2048].rearrange("p (b u n) -> p b u n", b=4, u=2)
                for u in range(2):
                    for bb in range(4):
                        y = mm(ps[32 * bb:32 * bb + 32, 7, 0:KVL], pts[:, s, u * P + 32 * bb:u * P + 32 * bb + 32],
                               kk[:, bb, u], start=False, stop=(g == 15 and u == 1))
                y.then_inc(s_ov, 1)

            def o_turn(r):
                pe.wait_ge(s_on, 1 + r + 1)
                for c in range(KKV):
                    y = tr(ps[:, 6, c * P:(c + 1) * P], olat[:, c * P:(c + 1) * P], ident)
                y.then_inc(s_pt, 1)

            def round_(r):
                for half in range(2):
                    for q in range(6):
                        unit(r, 2 * half + q // 3, q % 3)
                        lo, hi = (16 * q) // 6, (16 * (q + 1)) // 6
                        for g in range(lo, hi):
                            if half == 0:
                                k_step(r, g)
                            else:
                                if g == 0:
                                    v_new(r)
                                    v_turn(r, 0)
                                v_step(r, g)
                    if half == 0:
                        k_new(r)
                o_turn(r)

            pe.sem_inc(s_d, 4)
            pe.sem_inc(s_ov, 2)
            with pe.Fori(0, 2) as r:
                round_(r)

            pe.wait_ge(s_wuv, 16)
            pe.wait_ge(s_pte, 1 + 36)
            for hd in range(HEADS):
                x = hd % 2
                for c in range(KKV):
                    y = mm(ps[64 * x:64 * x + 64, 4, (hd // 2) * NS:(hd // 2 + 1) * NS],
                           wuv[:, c, hd * VH:(hd + 1) * VH],
                           olT[:, c].rearrange("p r (b h) -> p (r b) h", h=32)[:, :, hd],
                           start=(c == 0), stop=(c == KKV - 1))
            y.then_inc(s_os, 1)

            pe.wait_ge(s_ose, 1)
            pe.wait_ge(s_ot, PAIRS)

            def b_block(j, s, n):
                pe.wait_ge(s_wo[s], 16 * n)
                if isinstance(j, int) and j < 2:
                    pe.wait_ge(s_da, 1 + 16)
                    pe.wait_ge(s_dd, 1 + 8)
                else:
                    pe.wait_ge(s_bt, j - 1)
                for k in range(KD):
                    for h in range(2):
                        y = mm(ps[:, 2 * s + h, 0:TH], wo[:, s, k], oT[:, k, h * TH:(h + 1) * TH],
                               start=(k == 0), stop=(k == KD - 1))
                y.then_inc(s_b, 1)

            for s in range(2):
                b_block(s, s, 1)
            with pe.Fori(1, KD // 2) as i:
                for s in range(2):
                    b_block(2 * i + s, s, i + 1)

            def turn_x1(t):
                n = ROWS[t]
                pe.wait_ge(s_fd, FD * (t + 1))
                if t >= 1:
                    pe.wait_ge(s_fe, 2 * t)
                for k in range(KD):
                    y = tr(ps[:, 4 + k // 4, (k % 4) * P:(k % 4) * P + n], x1[0:n, t, k * P:(k + 1) * P], ident[0:n, 0:n])
                y.then_inc(s_fx, 1)
                pe.wait_ge(s_fe, 2 * (t + 1))
                if t >= 1:
                    pe.wait_ge(s_r, 2 * t)
                for k in range(KD):
                    y = mm(ps[0:n, 6, 0:36], x1T[:, k, 0:n], rw[:, k], start=(k == 0), stop=(k == KD - 1))
                y.then_inc(s_fl, 1)

            pe.wait_ge(s_wb, 80)
            pe.wait_ge(s_mt, KD)
            for t in range(TILES):
                n, s = ROWS[t], t % 2
                if t >= 2:
                    pe.wait_ge(s_fd, FD * (t - 2) + 1)
                for k in range(KD):
                    for h in range(2):
                        y = mm(ps[0:n, 2 * s + h, :], mixT[:, k, t * P:t * P + n], wbig[:, k, h * 512:(h + 1) * 512],
                               start=(k == 0), stop=(k == KD - 1))
                y.then_inc(s_f, 1)
                if t >= 1:
                    turn_x1(t - 1)
            turn_x1(TILES - 1)
            pe.wait_ge(s_r, R_RANK)
            flat = ohs[:].rearrange("p t e -> p (t e)")
            mm(ps[:, 7, 0:TILES * 32], utri, flat, start=True, stop=False)
            mm(ps[:, 7, 0:TILES * 32], ones, pf[:, 0:TILES].rearrange("p t e -> p (t e)"), start=False, stop=True)
            mm(ps[:, 7, 256:288], ones, pf[:, TILES], start=True, stop=True).then_inc(s_rp, 1)
            pe.wait_ge(s_tl, 16)
            tr(ps[:, 6, 0:SLOTS // P], tokrow[:, :], ident[0:SLOTS // P, 0:SLOTS // P]).then_inc(s_rp, 1)

            def experts(m, p, xslot, n):
                w = wx[xslot]
                pe.wait_ge(m.xg[xslot], 16 * n)
                if not (isinstance(p, int) and p == 0):
                    pe.wait_ge(m.xa, p)
                    pe.wait_ge(m.xd, p)
                for k in range(KD):
                    y = tr(ps[:, k // 4, (k % 4) * P:(k % 4 + 1) * P], xg[:, xslot, k * P:(k + 1) * P], ident)
                y.then_inc(m.xt, 1)
                pe.wait_ge(m.xa, p + 1)
                pe.wait_ge(m.xd, p + 1)
                pe.wait_ge(s_wx[xslot][0], 16 * n)
                pe.wait_ge(s_wx[xslot][1], 16 * n)
                for k in range(KD):
                    for x in range(2):
                        y = mm(ps[64 * x:64 * x + 64, 2, :], xgT[:, k, 64 * x:64 * x + 64],
                               w[:, x, k * 512:(k + 1) * 512], start=(k == 0), stop=(k == KD - 1))
                y.then_inc(m.h, 1)
                pe.wait_ge(m.hs, p + 1)
                for c in range(2):
                    y = tr(ps[:, 4, c * P:(c + 1) * P], hs[:, c * P:(c + 1) * P], ident)
                y.then_inc(m.ht, 1)
                pe.wait_ge(m.he, p + 1)
                if not (isinstance(p, int) and p == 0):
                    pe.wait_ge(m.ya, p)
                    pe.wait_ge(m.yd, p)
                for c in range(2):
                    for h in range(2):
                        for x in range(2):
                            o0 = KD * 512 + c * D + h * 512
                            y = mm(ps[64 * x:64 * x + 64, 6 + h, :], htT[:, c, 64 * x:64 * x + 64],
                                   w[:, x, o0:o0 + 512], start=(c == 0), stop=(c == 1))
                y.then_inc(m.y, 1)

            pe.wait_ge(s_r, R_STEPS)
            for s in range(2):
                experts(moe, s, s, 1)
            with pe.Fori(1, EPAIRS // 2) as i:
                for s in range(2):
                    experts(moe, 2 * i + s, s, i + 1)
            blocks = pe.value_load(ovi[0:1, 16:17], min_val=0, max_val=OVB)
            overflow(pe, blocks, lambda p, s, n: experts(moe, p, s, n + 1))
            pe.wait_ge(s_ovr, 1)

            for t in range(TILES):
                n = ROWS[t]
                if t == 0:
                    pe.wait_ge(s_plw, 64)
                    pe.wait_ge(s_plg, 16)
                else:
                    pe.wait_ge(s_hd, H_STEPS * (t - 1) + H_PLE)
                for k in range(2):
                    for h in range(2):
                        mm(ps[0:n, 2 + h, :], plT[:, k, t * P:t * P + n], wpp[:, k, h * 512:(h + 1) * 512],
                           start=(k == 0), stop=(k == 1))
                pe.wait_ge(s_hd, H_STEPS * t + H_X2)
                for k in range(KD):
                    y = tr(ps[:, 4 + k // 4, (k % 4) * P:(k % 4) * P + n], fb[0:n, 4, k * P:(k + 1) * P], ident[0:n, 0:n])
                y.then_inc(s_h, 1)
                pe.wait_ge(s_hsc, HA_STEPS * t + 3)
                for k in range(KD):
                    for h in range(2):
                        y = mm(ps[0:n, h, :], fbT[:, k, 0:n], wbig[:, k, h * 512:(h + 1) * 512],
                               start=(k == 0), stop=(k == KD - 1))
                y.then_inc(s_h, 1)

        @block.scalar
        def _(act):
            av = nc.scalar.activation
            for b in range(2):
                act.wait_ge(s_ha, b + 1)
                av(hTh[:, b], ps[:, 2 * b:2 * b + 2, 0:TH], ACT.Copy).then_inc(s_ht, 1)
            with act.Fori(1, NA // 2) as i:
                for s in range(2):
                    act.wait_ge(s_ha, 2 * i + s + 1)
                    av(hTh[:, bass.ds(2 * i + s, 1)].rearrange("p a h t -> p (a h) t"), ps[:, 2 * s:2 * s + 2, 0:TH],
                       ACT.Copy).then_inc(s_ht, 1)
            act.wait_ge(s_ht, NA)
            av(tmp[64:128, 0], hT[0:64, B_KR], ACT.Copy).then_inc(s_kro, 1)
            act.wait_ge(s_ini, N_INI)
            act.wait_ge(s_ss, 1)
            av(tmph[:, 1], ps[:, 4:6, 0:TH], ACT.Sqrt, bias=eps[:, 0:1], scale=1.0 / KVL).then_inc(s_rt, 1)
            act.wait_ge(s_ss, 2)
            av(tmph[:, 2], ps[:, 6:8, 0:TH], ACT.Sqrt, bias=eps[:, 0:1], scale=1.0 / QL).then_inc(s_rt, 1)
            for c in range(KC):
                av(hT[:, B_CB + c], hT[:, B_CB + c], ACT.Sigmoid).then_inc(s_u, 1)

            def out_q(p, s, x):
                act.wait_ge(s_g, 4 * p + 1 + 2 * x)
                av(qTh[0:64, s, x], ps[0:64, 0:2, 0:TH], ACT.Copy).then_inc(s_ga, 1)

            def out_k(p, s):
                act.wait_ge(s_g, 4 * p + 2)
                for x in range(2):
                    av(kT[0:64, s, x], ps[64 * x:64 * x + 64, 0, :], ACT.Copy).then_inc(s_ga, 1)

            def soft(p, x):
                hh = 2 * p + x
                for n, i in enumerate((0, 2, 1, 3)):
                    act.wait_ge(s_mx, 4 * hh + n + 1)
                    nc.scalar.mul(nb[:, x, i:i + 1], mx[:, x, i:i + 1], -SCALE).then_inc(s_nb, 1)
                    act.wait_ge(s_nb, 4 * hh + n + 1)
                    q = prob[:, x, POFF[i]:POFF[i] + (i + 1) * P]
                    av(q, q, ACT.Exp, bias=nb[:, x, i:i + 1], scale=SCALE, accum_out=rs[:, x, i:i + 1]).then_inc(s_ex, 1)

            def out_p(p, x):
                hh = 2 * p + x
                if not (isinstance(p, int) and p == 0):
                    act.wait_ge(s_o, p)
                for n, (bank, i) in enumerate(((7, 1), (6, 3))):
                    act.wait_ge(s_tp, 3 * hh + n + 2)
                    av(pT[:, x, 0:i + 1, i * P:(i + 1) * P], ps[:, bank, 0:(i + 1) * P].rearrange("p (j q) -> p j q", q=P),
                       ACT.Copy).then_inc(s_ta, 1)

            def out_o(p):
                act.wait_ge(s_o, p + 1)
                dst = oT[:, p, 0:NPR] if isinstance(p, int) else \
                    oT[:, bass.ds(p, 1), 0:NPR].rearrange("p a t -> p (a t)")
                av(dst, ps[:, 7, :], ACT.Copy).then_inc(s_ot, 1)

            def pair(p, s, first=False, last=False):
                q = 1 - s
                if not first:
                    out_p(p - 1, 1)
                soft(p, 0)
                if not last:
                    out_q(p + 1, q, 0)
                if not first:
                    out_o(p - 1)
                if not last:
                    out_k(p + 1, q)
                soft(p, 1)
                out_p(p, 0)
                if not last:
                    out_q(p + 1, q, 1)

            out_q(0, 0, 0)
            out_k(0, 0)
            out_q(0, 0, 1)
            pair(0, 0, first=True)
            pair(1, 1)
            with act.Fori(1, PAIRS // 2 - 1) as i:
                pair(2 * i, 0)
                pair(2 * i + 1, 1)
            pair(PAIRS - 2, 0)
            pair(PAIRS - 1, 1, last=True)
            out_p(PAIRS - 1, 1)
            out_o(PAIRS - 1)

            for c in range(KC):
                act.wait_ge(s_ln, 2 + c)
                av(sqc(c), aT[:, c], ACT.Square).then_inc(s_sqc, 1)
            act.wait_ge(s_cm, 2)
            av(tmph[:, 1], ps[:, 4:6, 0:TH], ACT.Sqrt, bias=eps[:, 1:2], scale=1.0 / CC).then_inc(s_sqc, 1)
            for c in range(KC):
                act.wait_ge(s_ln, 7 + c)
                av(aT[:, c], aT[:, c], ACT.Silu, bias=vec[:, VLB + c:VLB + c + 1],
                   scale=vec[:, VLG + c:VLG + c + 1]).then_inc(s_sqc, 1)

            act.sem_inc(s_da, 1)
            act.sem_inc(s_ske, 1)
            act.wait_ge(s_o, PAIRS)
            for s in range(2):
                act.dma_start(er[:, s], a["wgate"][s]).then_inc(s_er[s], 16)

            def gate(r, jj, u):
                act.wait_ge(s_d, 4 + 12 * r + 3 * jj + u + 1)
                if u == 0:
                    act.wait_ge(s_dd, 1 + 4 * r + jj)
                    av(sgh, ps[:, 0:2, 0:TH], ACT.Sigmoid).then_inc(s_da, 1)
                else:
                    av(sigBh[:, bass.ds(4 * r + jj, 1)].rearrange("p a h t -> p (a h) t"), ps[:, 0:2, 0:TH],
                       ACT.Sigmoid).then_inc(s_da, 1)

            def next_block(s, j):
                act.dma_start(er[:, s], a["wgate"][j].rearrange("a p k m -> (a p) k m")
                              ).then_inc(s_er[s], 16)

            with act.Fori(0, 2) as r:
                for half in range(2):
                    for q in range(6):
                        if q % 3 != 1:
                            gate(r, 2 * half + q // 3, q % 3)
                        if q % 3 == 2:
                            s = q // 3
                            if half == 0:
                                next_block(s, bass.ds(4 * r + 2 + s, 1))
                            else:
                                with act.If(r < 1):
                                    next_block(s, slice(4 + s, 5 + s))
                        lo, hi = (16 * q) // 6, (16 * (q + 1)) // 6
                        if half == 1:
                            lo, hi = (lo + 1 if q else 0), min(hi + 1, 16)
                        for g in range(lo, hi):
                            if half == 0:
                                act.wait_ge(s_sk, 17 * r + g + 1)
                                av(S[:, g * 256:(g + 1) * 256], ps[:, 4 + g % 2, 0:256], ACT.Copy).then_inc(s_ske, 1)
                            else:
                                if g == 0:
                                    act.wait_ge(s_rnd, RND * r + 10)
                                    av(rsum[:, 16:17], S[:, 4096:4097], ACT.Exp, bias=sm[:, 1:2],
                                       scale=SCALE).then_inc(s_pcx, 1)
                                if g >= 2:
                                    act.wait_ge(s_pt, 18 * r + g)
                                av(pc[:, g % 2], S[:, g * 256:(g + 1) * 256], ACT.Exp, bias=sm[:, 1:2], scale=SCALE,
                                   accum_out=rsum[:, g:g + 1]).then_inc(s_pcx, 1)
                    if half == 0:
                        act.wait_ge(s_sk, 17 * r + 17)
                        av(S[:, 4096:4097], ps[:, 4, 0:1], ACT.Copy).then_inc(s_ske, 1)
            act.wait_ge(s_os, 1)
            av(oT[:, :, NPR:T], ps[:, 4, 0:PAIRS * NS].rearrange("p (k b) -> p k b", k=PAIRS), ACT.Copy).then_inc(s_ose, 1)

            def x1_out(t):
                n = ROWS[t]
                act.wait_ge(s_fx, t + 1)
                if t >= 1:
                    act.wait_ge(s_fl, t)
                for h in range(2):
                    av(x1T[:, 4 * h:4 * h + 4, 0:n], ps[:, 4 + h, :].rearrange("p (k n) -> p k n", k=4)[:, :, 0:n],
                       ACT.Copy).then_inc(s_fe, 1)

            for t in range(TILES):
                act.wait_ge(s_fd, FD * t + 4)
                av(rstd[0:ROWS[t], 0:1], mv[0:ROWS[t], 1:2], ACT.Sqrt, bias=eps[0:ROWS[t], 1:2]).then_inc(s_fa, 1)
                if t >= 1:
                    x1_out(t - 1)
            x1_out(TILES - 1)
            act.wait_ge(s_r, R_EXP)
            av(gg[:], gx[:], ACT.Exp).then_inc(s_ra, 1)
            act.wait_ge(s_r, R_EXP2)
            av(gf, gf, ACT.Exp).then_inc(s_ra, 1)

            def experts(m, p, xs, n):
                act.wait_ge(m.xt, p + 1)
                av(xgT[:, 0:4], ps[:, 0, :].rearrange("p (k n) -> p k n", k=4), ACT.Copy).then_inc(m.xa, 1)
                act.wait_ge(m.h, p + 1)
                av(sgE, ps[:, 2, 0:DE], ACT.Silu).then_inc(m.sg, 1)
                act.wait_ge(m.y, p + 1)
                if not (isinstance(n, int) and n == 0):
                    act.wait_ge(m.yw[xs], 16 * n)
                av(yb[:, xs, 0:512], ps[:, 6, :], ACT.Copy).then_inc(m.ya, 1)
                act.wait_ge(m.ya, p + 1)
                act.wait_ge(m.yd, p + 1)
                rows = ybd[p * P:(p + 1) * P] if isinstance(p, int) else ybd[bass.ds(p * P, P)]
                act.dma_start(rows, yb[:, xs]).then_inc(m.yw[xs], 16)

            for s in range(2):
                experts(moe, s, s, 0)
            with act.Fori(1, EPAIRS // 2) as i:
                for s in range(2):
                    experts(moe, 2 * i + s, s, i)
            act.wait_ge(s_r, R_STEPS)
            act.wait_ge(s_yz, 16)
            blocks = act.value_load(ovi[0:1, 16:17], min_val=0, max_val=OVB)

            def extra(p, s, n):
                experts(moe, p, s, n)
                act.wait_ge(moe.yw[s], 16 * n + 16)
                act.sem_inc(s_own, 1)

            overflow(act, blocks, extra)
            act.wait_ge(moe.yw[0], 16 * EPAIRS // 2)
            act.wait_ge(moe.yw[1], 16 * EPAIRS // 2)
            act.sem_inc(s_ovr, 1)

            for t in range(TILES):
                n = ROWS[t]
                act.wait_ge(s_hd, H_STEPS * t + 6)
                av(rstd[0:n, 0:1], mv[0:n, 1:2], ACT.Sqrt, bias=eps[0:n, 1:2]).then_inc(s_hsc, 1)
                act.wait_ge(s_h, 2 * t + 1)
                for h in range(2):
                    av(fbT[:, 4 * h:4 * h + 4, 0:n], ps[:, 4 + h, :].rearrange("p (k n) -> p k n", k=4)[:, :, 0:n],
                       ACT.Copy).then_inc(s_hsc, 1)
                act.wait_ge(s_h, 2 * t + 2)
                av(fb[0:n, 5], ps[0:n, 0:2, :].rearrange("p h n -> p (h n)"), ACT.Sigmoid).then_inc(s_hsc, 1)
                act.wait_ge(s_hd, H_STEPS * t + H_PLE)
                av(fb[0:n, 8], fb[0:n, 5], ACT.Square, accum_out=rstd[0:n, 0:1]).then_inc(s_hsc, 1)
                act.wait_ge(s_hsc, HA_STEPS * t + 5)
                av(rstd[0:n, 1:2], rstd[0:n, 0:1], ACT.Sqrt, bias=eps[0:n, 0:1], scale=1.0 / D).then_inc(s_hsc, 1)

        @block.vector
        def _(dve):
            v = nc.vector
            v.memset(zeros, 0.0).then_inc(s_ini, 1)
            v.memset(eps[:, 0:1], RMS_EPS).then_inc(s_ini, 1)
            v.memset(eps[:, 1:2], LN_EPS).then_inc(s_ini, 1)
            v.memset(ext[:, :, 0:CW - 1], 0.0).then_inc(s_ini, 1)
            v.memset(qlat, 0.0).then_inc(s_ini, 1)
            v.memset(qrs, 0.0).then_inc(s_ini, 1)
            dve.wait_ge(s_ht, KKV)
            h = hT[:, B_CKV:B_CKV + KKV]
            v.tensor_tensor(sq[:, 0:KKV], h, h, ALU.mult).then_inc(s_sq, 1)
            dve.wait_ge(s_ht, B_CQ + KQ)
            h = hT[:, B_CQ:B_CQ + KQ]
            v.tensor_tensor(sq[:, KKV:KKV + KQ], h, h, ALU.mult).then_inc(s_sq, 1)
            dve.wait_ge(s_con, 112)
            dve.wait_ge(s_kro, 1)
            kr = hT[64:128, B_KR]
            v.tensor_tensor(tmp[64:128, 0], tmp[64:128, 0], rsn[64:128], ALU.mult).then_inc(s_nrm, 1)
            v.tensor_tensor(kr, kr, rc[64:128], ALU.mult).then_inc(s_nrm, 1)
            dve.wait_ge(s_nrm, 2)
            v.tensor_tensor(kr, kr, tmp[64:128, 0], ALU.add).then_inc(s_nrm, 1)
            dve.wait_ge(s_rt, 1)
            v.reciprocal(tmp[:, 1], tmp[:, 1]).then_inc(s_nrm, 1)
            dve.wait_ge(s_nrm, 4)
            for c in range(KKV):
                h = hT[:, B_CKV + c]
                v.scalar_tensor_tensor(out=h, in0=h, scalar=vec[:, VKG + c:VKG + c + 1], in1=tmp[:, 1], op0=ALU.mult,
                                       op1=ALU.mult).then_inc(s_nrm, 1)
            dve.wait_ge(s_rt, 2)
            v.reciprocal(tmp[:, 2], tmp[:, 2]).then_inc(s_nrm, 1)
            dve.wait_ge(s_nrm, 7)
            for c in range(KQ):
                h = hT[:, B_CQ + c]
                v.scalar_tensor_tensor(out=h, in0=h, scalar=vec[:, VQG + c:VQG + c + 1], in1=tmp[:, 2], op0=ALU.mult,
                                       op1=ALU.mult).then_inc(s_nrm, 1)

            def glu():
                for c in range(KC):
                    dve.wait_ge(s_u, c + 1)
                    v.tensor_tensor(ext[:, c, CW - 1:CW - 1 + NPR], hT[:, B_CA + c, 0:NPR], hT[:, B_CB + c, 0:NPR],
                                    ALU.mult).then_inc(s_gl, 1)
                    v.tensor_tensor(exs[:, c, :, CW - 1], hT[:, B_CA + c, NPR:T], hT[:, B_CB + c, NPR:T],
                                    ALU.mult).then_inc(s_gl, 1)

            def conv_s():
                e3 = exw.rearrange("p (b w) -> p b w", b=NS)
                for c in range(KC):
                    w = vec[:, VDW + c * CW:VDW + (c + 1) * CW].unsqueeze(1).to_broadcast([P, NS, CW])
                    dve.wait_ge(s_gl, 2 * c + 2)
                    v.tensor_tensor(e3, exs[:, c], w, ALU.mult).then_inc(s_sc, 1)
                    dve.wait_ge(s_sc, 3 * c + 1)
                    v.tensor_reduce(aT[:, c, NPR:T], e3, AX.X, ALU.add).then_inc(s_sc, 1)
                    dve.wait_ge(s_sc, 3 * c + 2)
                    v.tensor_scalar(aT[:, c, NPR:T], aT[:, c, NPR:T], vec[:, VBD + c:VBD + c + 1], None,
                                    ALU.add).then_inc(s_sc, 1)

            def out_q(p, s, x):
                dve.wait_ge(s_g, 4 * p + 1 + 2 * x)
                v.tensor_tensor(qTh[64:128, s, x], ps[64:128, 0:2, 0:TH],
                                rq[64:128].rearrange("p (h t) -> p h t", h=2), ALU.mult).then_inc(s_gd, 1)
                dve.wait_ge(s_gd, 6 * p + 1 + 3 * x)
                dst = qrr[64:128, :, 2 * p + x] if isinstance(p, int) else \
                    qrr[64:128, :, bass.ds(2 * p + x, 1)].rearrange("p b a -> p (b a)")
                v.tensor_copy(dst, qT[64:128, s, x, NPR:T]).then_inc(s_gd, 1)

            def out_v(p, s):
                dve.wait_ge(s_g, 4 * p + 2)
                v.tensor_copy(vf[:, s], ps[:, 1, :]).then_inc(s_gd, 1)

            def out_lat(p):
                dve.wait_ge(s_g, 4 * p + 4)
                for x in range(2):
                    sl = slice(2 * p + x, 2 * p + x + 1) if isinstance(p, int) else bass.ds(2 * p + x, 1)
                    y = v.tensor_copy(qlat[:, :, :, sl].rearrange("p c b a -> p c (b a)"),
                                      ps[:, 0, 16 * x:16 * x + 16].rearrange("p (c b) -> p c b", b=NS))
                y.then_inc(s_gd, 1)

            def masks(p, x):
                hh = 2 * p + x
                if not (isinstance(p, int) and p == 0):
                    dve.wait_ge(s_tp, 3 * (hh - 1))
                for n, i in enumerate((0, 2, 1, 3)):
                    dve.wait_ge(s_s, 3 * hh + (1, 1, 2, 3)[n])
                    dve.sem_inc(s_own, 1)
                    bank, c0 = (2, 3, 2, 4)[i], P if i == 2 else 0
                    w = (i + 1) * P
                    v.tensor_tensor_reduce(prob[:, x, POFF[i]:POFF[i] + w], ps[:, bank, c0:c0 + w], maskw[:, 512 - w:512],
                                           1.0, -BIG, ALU.add, ALU.max, mx[:, x, i:i + 1]).then_inc(s_mx, 1)

            def scale(p, x):
                hh = 2 * p + x
                for n, i in enumerate((0, 2, 1, 3)):
                    dve.wait_ge(s_ex, 4 * hh + n + 1)
                    v.reciprocal(rr[:, x, i:i + 1], rs[:, x, i:i + 1]).then_inc(s_rc, 1)
                    dve.wait_ge(s_rc, 4 * hh + n + 1)
                    q = prob[:, x, POFF[i]:POFF[i] + (i + 1) * P]
                    v.tensor_scalar(q, q, rr[:, x, i:i + 1], None, ALU.mult).then_inc(s_pr, 1)

            def out_p(p, x):
                hh = 2 * p + x
                if not (isinstance(p, int) and p == 0):
                    dve.wait_ge(s_o, p)
                dve.wait_ge(s_tp, 3 * hh + 1)
                for i in (0, 2):
                    c0 = P if i == 2 else 0
                    v.tensor_copy(pT[:, x, 0:i + 1, i * P:(i + 1) * P],
                                  ps[:, 5, c0:c0 + (i + 1) * P].rearrange("p (j q) -> p j q", q=P)).then_inc(s_td, 1)

            def tap(p, n):
                w = 4 * p + n
                at_w = (lambda off, ln: slice(off + w, off + w + ln)) if isinstance(p, int) else \
                    (lambda off, ln: bass.ds(w + off, ln))
                for c in range(KC):
                    win, wt = ext[:, c, at_w(0, NPR)], vec[:, at_w(VDW + c * CW, 1)]
                    if isinstance(p, int) and w == 0:
                        dve.wait_ge(s_gl, 2 * c + 1)
                        y = v.tensor_scalar(aT[:, c, 0:NPR], win, wt, vec[:, VBD + c:VBD + c + 1], ALU.mult, ALU.add)
                    else:
                        dve.wait_ge(s_cv, KC * w - KC + c + 1)
                        y = v.scalar_tensor_tensor(out=aT[:, c, 0:NPR], in0=win, scalar=wt, in1=aT[:, c, 0:NPR],
                                                   op0=ALU.mult, op1=ALU.add)
                    y.then_inc(s_cv, 1)

            def pair(p, s, first=False, last=False):
                q = 1 - s
                masks(p, 0)
                if not first:
                    out_p(p - 1, 1)
                if not last:
                    out_q(p + 1, q, 0)
                tap(p, 0)
                scale(p, 0)
                masks(p, 1)
                if not last:
                    out_v(p + 1, q)
                tap(p, 1)
                out_p(p, 0)
                if not last:
                    out_q(p + 1, q, 1)
                tap(p, 2)
                scale(p, 1)
                if not last:
                    out_lat(p + 1)
                    tap(p, 3)

            out_q(0, 0, 0)
            out_v(0, 0)
            out_q(0, 0, 1)
            out_lat(0)
            glu()
            conv_s()
            pair(0, 0, first=True)
            pair(1, 1)
            with dve.Fori(1, PAIRS // 2 - 1) as i:
                pair(2 * i, 0)
                pair(2 * i + 1, 1)
            pair(PAIRS - 2, 0)
            pair(PAIRS - 1, 1, last=True)
            out_p(PAIRS - 1, 1)

            dve.wait_ge(s_qs, 1)
            v.tensor_copy(qrs[:, :, 0:HEADS], ps[0:32, 0, 0:P].rearrange("p (b h) -> p b h", b=NS)).then_inc(s_qc, 1)
            v.tensor_copy(ckvs, ps[0:NS, 1, 0:KVL]).then_inc(s_qc, 1)
            v.tensor_copy(krs[:], hT[64:96, B_KR, NPR:T]).then_inc(s_qc, 1)
            dve.wait_ge(s_cm, 1)
            v.tensor_scalar(tmph[:, 0], ps[:, 2:4, 0:TH], 1.0 / CC, None, ALU.mult).then_inc(s_ln, 1)
            dve.wait_ge(s_ln, 1)
            for c in range(KC):
                v.tensor_tensor(aT[:, c], aT[:, c], tmp[:, 0], ALU.subtract).then_inc(s_ln, 1)
            dve.wait_ge(s_sqc, KC + 1)
            v.reciprocal(tmp[:, 2], tmp[:, 1]).then_inc(s_ln, 1)
            dve.wait_ge(s_ln, 6)
            for c in range(KC):
                v.tensor_tensor(aT[:, c], aT[:, c], tmp[:, 2], ALU.mult).then_inc(s_ln, 1)

            dve.sem_inc(s_dd, 1)
            dve.sem_inc(s_on, 1)
            dve.sem_inc(s_pte, 1)
            dve.wait_ge(s_qc, 3)
            dve.wait_ge(s_z, 16)
            dve.wait_ge(s_yz, 16)

            def gated(r, jj):
                dve.wait_ge(s_d, 4 + 12 * r + 3 * jj + 2)
                dve.wait_ge(s_da, 1 + 8 * r + 2 * jj + 1)
                v.tensor_tensor(mixh[:, bass.ds(4 * r + jj, 1)].rearrange("p a h t -> p (a h) t"),
                                ps[:, 2:4, 0:TH], sgh, ALU.mult).then_inc(s_dd, 1)

            with dve.Fori(0, 2) as r:
                now, new = bass.ds(4 * r, 4), bass.ds(NPR + 4 * r, 4)
                ckv = hT[:, B_CKV:B_CKV + KKV]
                v.tensor_copy(qcur[:, 0:2], qlat[0:KR, :, now, :]).then_inc(s_rnd, 1)
                v.tensor_copy(qcur[0:32, 2], qrs[:, now, :]).then_inc(s_rnd, 1)
                v.tensor_copy(knew[:, 0:2], ckv[0:KR, :, new]).then_inc(s_rnd, 1)
                v.tensor_copy(knew[0:32, 2], krs[:, now]).then_inc(s_rnd, 1)
                for c in range(KKV):
                    v.tensor_copy(qcur[32 + 32 * c:64 + 32 * c, 2], qlat[KR:P, c, now, :]).then_inc(s_rnd, 1)
                    v.tensor_copy(knew[32 + 32 * c:64 + 32 * c, 2], ckv[KR:P, c, new]).then_inc(s_rnd, 1)
                gated(r, 0)
                gated(r, 1)
                dve.wait_ge(s_ske, 1 + 17 * r + 17)
                v.tensor_reduce(sm[:, 0:1], S[:, 0:4097], AX.X, ALU.max).then_inc(s_rnd, 1)
                dve.wait_ge(s_rnd, RND * r + 9)
                v.tensor_scalar(sm[:, 1:2], sm[:, 0:1], -SCALE, None, ALU.mult).then_inc(s_rnd, 1)
                dve.wait_ge(s_pcx, 17 * r + 1)
                v.tensor_scalar(pnm[:], con[:, bass.ds(CM8 + NS * r, NS)], rsum[:, 16:17], None, ALU.mult).then_inc(s_rnd, 1)
                dve.wait_ge(s_pt, 18 * r + 1)
                v.tensor_copy(pnT, ps[0:NS, 6, 0:P]).then_inc(s_pte, 1)
                for g in range(16):
                    if g in (2, 10):
                        gated(r, 2 + (g == 10))
                    dve.wait_ge(s_pt, 18 * r + g + 2)
                    dve.wait_ge(s_ov, 2 + 17 * r + (g if g >= 2 else 0))
                    v.tensor_copy(pts[:, g % 2], ps[:, 4 + g % 2, 0:256]).then_inc(s_pte, 1)
                dve.wait_ge(s_pcx, 17 * r + 17)
                v.tensor_reduce(sm[:, 3:4], rsum[:, 0:17], AX.X, ALU.add).then_inc(s_rnd, 1)
                dve.wait_ge(s_rnd, RND * r + 12)
                v.reciprocal(sm[:, 4:5], sm[:, 3:4]).then_inc(s_rnd, 1)
                dve.wait_ge(s_rnd, RND * r + 13)
                dve.wait_ge(s_ov, 2 + 17 * r + 17)
                v.tensor_scalar(olat, ps[:, 7, 0:KVL], sm[:, 4:5], None, ALU.mult).then_inc(s_on, 1)
                dve.wait_ge(s_pt, 18 * r + 18)
                v.tensor_copy(olT[:, :, bass.ds(r, 1)].rearrange("p c a n -> p c (a n)"),
                              ps[:, 6, 0:256].rearrange("p (c n) -> p c n", c=KKV)).then_inc(s_pte, 1)

            def b_block(j, s):
                dve.wait_ge(s_b, j + 1)
                sl = slice(j, j + 1) if isinstance(j, int) else bass.ds(j, 1)
                if not (isinstance(j, int) and j == 0):
                    dve.wait_ge(s_mt, j)
                v.tensor_tensor(sgh, ps[:, 2 * s:2 * s + 2, 0:TH],
                                sigBh[:, sl].rearrange("p a h t -> p (a h) t"), ALU.mult).then_inc(s_bt, 1)
                dve.wait_ge(s_bt, j + 1)
                m = mixT[:, sl].rearrange("p a t -> p (a t)")
                v.tensor_tensor(m, m, sg, ALU.add).then_inc(s_mt, 1)

            for s in range(2):
                b_block(s, s)
            with dve.Fori(1, KD // 2) as i:
                for s in range(2):
                    b_block(2 * i + s, s)

            def norm(n, x, stats_sem, base, root_sem, root_n, g, b):
                for hh in range(2):
                    v.bn_stats(bst[0:n, hh], x[:, hh * 512:(hh + 1) * 512]).then_inc(stats_sem, 1)
                dve.wait_ge(stats_sem, base + 2)
                v.bn_aggr(mv[0:n], bst[0:n].rearrange("p h s -> p (h s)")).then_inc(stats_sem, 1)
                dve.wait_ge(root_sem, root_n)
                v.reciprocal(rstd[0:n, 1:2], rstd[0:n, 0:1]).then_inc(stats_sem, 1)
                dve.wait_ge(stats_sem, base + 4)
                v.tensor_scalar(x, x, mv[0:n, 0:1], rstd[0:n, 1:2], ALU.subtract, ALU.mult).then_inc(stats_sem, 1)
                dve.wait_ge(stats_sem, base + 5)
                v.tensor_tensor(x, x, g[0:n], ALU.mult).then_inc(stats_sem, 1)
                dve.wait_ge(stats_sem, base + 6)
                v.tensor_tensor(x, x, b[0:n], ALU.add).then_inc(stats_sem, 1)

            def logits(t):
                n = ROWS[t]
                dve.wait_ge(s_fl, t + 1)
                v.tensor_copy(L[0:n, t, 0:4], ps[0:n, 6, 0:4]).then_inc(s_r, 1)
                v.tensor_copy(L[0:n, t, 8:40], ps[0:n, 6, 4:36]).then_inc(s_r, 1)

            v.memset(L, 0.0).then_inc(s_ini, 1)
            dve.wait_ge(s_ini, N_INI + 1)
            v.memset(L[:, :, 4:8], -BIG).then_inc(s_ini, 1)
            v.memset(one32, 1.0).then_inc(s_ini, 1)
            v.memset(pf[:, 0], 0.0).then_inc(s_ini, 1)
            dve.wait_ge(s_ini, N_INI + 4)
            dve.wait_ge(s_wb, 80)
            for t in range(TILES):
                n = ROWS[t]
                x = x1[0:n, t]
                dve.wait_ge(s_f, t + 1)
                v.scalar_tensor_tensor(out=x, in0=x, scalar=ALPHA,
                                       in1=ps[0:n, 2 * (t % 2):2 * (t % 2) + 2, :].rearrange("p h n -> p (h n)"),
                                       op0=ALU.mult, op1=ALU.add).then_inc(s_fd, 1)
                dve.wait_ge(s_fd, FD * t + 1)
                norm(n, x, s_fd, FD * t + 1, s_fa, t + 1, lnr[:, 0], lnr[:, 1])
                if t >= 1:
                    logits(t - 1)
            logits(TILES - 1)

            count = [2 * TILES]

            def step(ins):
                ins.then_inc(s_r, 1)
                count[0] += 1
                dve.wait_ge(s_r, count[0])

            dve.wait_ge(s_r, count[0])

            def b3(x, n):
                return x.unsqueeze(2).to_broadcast([P, TILES, n])

            def cb(off, n):
                return con[:, off:off + n].unsqueeze(1).to_broadcast([P, TILES, n])

            for t in range(TILES):
                v.max(gv[:, t], L[:, t, 0:8])
            step(v.tensor_copy(gx, L[:, :, 0:4]))
            for t in range(TILES):
                v.max_index(gi[:, t], gv[:, t], L[:, t, 0:8])
            step(v.tensor_tensor(gx, gx, b3(gv[:, :, 0], 4), ALU.subtract))
            assert count[0] == R_EXP
            step(v.tensor_copy(gf, gi[:, :, 0]))
            step(v.tensor_tensor(ms, cb(CGID, 32), b3(gf, 32), ALU.is_equal))
            step(v.tensor_scalar(ms2, ms, -1.0, BIG, ALU.add, ALU.mult))
            step(v.tensor_tensor(ms, ms, L[:, :, 8:40], ALU.mult))
            step(v.tensor_tensor(ms, ms, ms2, ALU.add))
            for t in range(TILES):
                v.max(ev[:, t], ms[:, t])
            step(v.tensor_copy(ms2, ms))
            for t in range(TILES):
                v.max_index(ei[:, t], ev[:, t], ms2[:, t])
            step(v.tensor_tensor(gf, ev[:, :, 1], ev[:, :, 0], ALU.subtract))
            assert count[0] == R_EXP2, count
            step(v.tensor_copy(ef, ei[:, :, 0:2]))
            for k in range(2):
                step(v.tensor_tensor(oh[:, k], cb(CEID, 32), b3(ef[:, :, k], 32), ALU.is_equal))
            step(v.tensor_tensor(ohs, oh[:, 0], oh[:, 1], ALU.add))
            step(v.tensor_tensor(ohs, ohs, b3(con[:, CVAL:CVAL + TILES], 32), ALU.mult))
            for t in range(TILES):
                step(v.tensor_tensor(pf[:, t + 1], pf[:, t], ohs[:, t], ALU.add))
            assert count[0] == R_RANK, count
            dve.wait_ge(s_ra, 1)
            step(v.tensor_reduce(gv[:, :, 0], gg, AX.X, ALU.add))
            step(v.reciprocal(gv[:, :, 1], gv[:, :, 0]))
            dve.wait_ge(s_ra, 2)
            step(v.tensor_scalar(gv[:, :, 2], gf, 1.0, None, ALU.add))
            step(v.reciprocal(gv[:, :, 3], gv[:, :, 2]))
            step(v.tensor_tensor(gates[:, 0], gv[:, :, 3], gv[:, :, 1], ALU.mult))
            step(v.tensor_tensor(gates[:, 1], gates[:, 0], gf, ALU.mult))
            dve.wait_ge(s_rp, 1)
            v.tensor_copy(cnt, ps[:, 7, 256:288])
            step(v.tensor_copy(pos, ps[:, 7, 0:TILES * 32].rearrange("p (t e) -> p t e", e=32)))
            step(v.tensor_tensor(cmp8, cnt.unsqueeze(2).to_broadcast([P, 32, 8]),
                                 con[:, CTHR:CTHR + 8].unsqueeze(1).to_broadcast([P, 32, 8]), ALU.is_gt))
            step(v.tensor_reduce(nov, cmp8, AX.X, ALU.add))
            step(v.tensor_tensor_scan(oend, one32, nov, 0.0, ALU.mult, ALU.add))
            step(v.tensor_tensor(dsl, oend, nov, ALU.subtract))
            step(v.tensor_scalar(dsl, dsl, float(CAP), float(CAP * (NEXP - 1)), ALU.mult, ALU.add))
            step(v.tensor_tensor(dsl, dsl, con[:, CEB:CEB + 32], ALU.subtract))
            step(v.tensor_scalar(ms, pos, float(CAP), None, ALU.is_ge))
            step(v.tensor_tensor(ms, ms, dsl.unsqueeze(1).to_broadcast([P, TILES, 32]), ALU.mult))
            step(v.tensor_tensor(pos, pos, cb(CEB, 32), ALU.add))
            step(v.tensor_tensor(pos, pos, ms, ALU.add))
            for k in range(2):
                step(v.tensor_tensor(ms, oh[:, k], pos, ALU.mult))
                step(v.tensor_reduce(slotf[:, k], ms, AX.X, ALU.add))
            step(v.tensor_copy(slotu[:], slotf))
            assert count[0] == R_SLOT, count
            step(v.tensor_tensor(ovc, oend[0:1].unsqueeze(1).to_broadcast([1, 16, 32]),
                                 con[0:1, CBLK:CBLK + 16].unsqueeze(2).to_broadcast([1, 16, 32]), ALU.is_le))
            step(v.tensor_reduce(ovf[:, 0:16], ovc, AX.X, ALU.add))
            step(v.tensor_scalar(ovf[:, 0:16], ovf[:, 0:16], float(NEXP - 1), None, ALU.min))
            step(v.tensor_copy(ovf[:, 16:17], oend[0:1, 31:32]))
            step(v.tensor_copy(ovi[:], ovf[:]))
            dve.wait_ge(s_rp, 2)
            step(v.tensor_copy(idx[:], ps[:, 6, 0:SLOTS // P]))
            assert count[0] == R_STEPS, count

            def experts(m, p, xs, n):
                dve.wait_ge(m.xt, p + 1)
                v.tensor_copy(xgT[:, 4:8], ps[:, 1, :].rearrange("p (k n) -> p k n", k=4)).then_inc(m.xd, 1)
                dve.wait_ge(m.sg, p + 1)
                v.tensor_tensor(hs, ps[:, 2, DE:2 * DE], sgE, ALU.mult).then_inc(m.hs, 1)
                dve.wait_ge(m.ht, p + 1)
                v.tensor_copy(htT, ps[:, 4, 0:256].rearrange("p (c n) -> p c n", c=2)).then_inc(m.he, 1)
                dve.wait_ge(m.y, p + 1)
                if not (isinstance(n, int) and n == 0):
                    dve.wait_ge(m.yw[xs], 16 * n)
                v.tensor_copy(yb[:, xs, 512:1024], ps[:, 7, :]).then_inc(m.yd, 1)

            for s in range(2):
                experts(moe, s, s, 0)
            with dve.Fori(1, EPAIRS // 2) as i:
                for s in range(2):
                    experts(moe, 2 * i + s, s, i)
            blocks = dve.value_load(ovi[0:1, 16:17], min_val=0, max_val=OVB)
            overflow(dve, blocks, lambda p, s, n: experts(moe, p, s, n))

            dve.wait_ge(s_plw, 64)
            for t in range(TILES):
                n, b = ROWS[t], H_STEPS * t
                dve.wait_ge(s_gt[t % 2][0], 16 * (t // 2 + 1))
                v.tensor_scalar(fb[0:n, t % 2], fb[0:n, t % 2], gates[0:n, 0, t:t + 1], None, ALU.mult).then_inc(s_hd, 1)
                dve.wait_ge(s_hd, b + 1)
                dve.wait_ge(s_gt[t % 2][1], 16 * (t // 2 + 1))
                v.scalar_tensor_tensor(out=fb[0:n, 8], in0=fb[0:n, 2 + t % 2], scalar=gates[0:n, 1, t:t + 1],
                                       in1=fb[0:n, t % 2], op0=ALU.mult, op1=ALU.add).then_inc(s_hd, 1)
                dve.wait_ge(s_hd, b + 2)
                x = fb[0:n, 4]
                v.scalar_tensor_tensor(out=x, in0=x1[0:n, t], scalar=ALPHA, in1=fb[0:n, 8], op0=ALU.mult,
                                       op1=ALU.add).then_inc(s_hd, 1)
                dve.wait_ge(s_hd, b + 3)
                norm(n, x, s_hd, b + 3, s_hsc, HA_STEPS * t + 1, ln2r[:, 0], ln2r[:, 1])
                dve.wait_ge(s_hsc, HA_STEPS * t + 4)
                v.tensor_tensor(fb[0:n, 5], fb[0:n, 5], ps[0:n, 2:4, :].rearrange("p h n -> p (h n)"),
                                ALU.mult).then_inc(s_hd, 1)
                dve.wait_ge(s_hsc, HA_STEPS * t + 6)
                v.reciprocal(rstd[0:n, 1:2], rstd[0:n, 1:2]).then_inc(s_hd, 1)
                dve.wait_ge(s_hd, b + 12)
                if t >= 2:
                    dve.wait_ge(s_yo[t % 2], 16 * (t // 2))
                y = fb[0:n, 6 + t % 2]
                v.scalar_tensor_tensor(out=y, in0=fb[0:n, 5], scalar=rstd[0:n, 1:2], in1=pgr[0:n], op0=ALU.mult,
                                       op1=ALU.mult).then_inc(s_hd, 1)
                dve.wait_ge(s_hd, b + 13)
                v.tensor_tensor(y, y, x, ALU.add).then_inc(s_hd, 1)

        @block.gpsimd
        def _(pool):
            gp = nc.gpsimd
            pool.wait_ge(s_nrm, 3)
            for s in range(2):
                for x in range(2):
                    gp.tensor_copy(kT[64:128, s, x], hT[64:128, B_KR, 0:NPR]).then_inc(s_kf, 1)
            numbers = [pool.alloc_register(f"pool_page{j}") for j in range(4)]

            def k_pages(r, g, s):
                pool.load(numbers, pages[0:1, bass.ds(8 * (16 * r + g) + 4, 4)])
                for j in range(4):
                    pg = pool.snap(numbers[j], min_val=0, max_val=NPOOL - 1)
                    pool.dma_start(kpage(s, 4 + j), a["kT"][bass.ds(pg, 1)].rearrange("a p n -> (a p) n")
                                   ).then_inc(s_kp[s], 16)

            def v_pages(r, g, s):
                pool.load(numbers, pages[0:1, bass.ds(8 * (16 * r + g) + 4, 4)])
                for j in range(4):
                    pg = pool.snap(numbers[j], min_val=0, max_val=NPOOL - 1)
                    pool.dma_start(vpage(s, 4 + j), a["vc"][bass.ds(pg, 1)].rearrange("a p n -> (a p) n")
                                   ).then_inc(s_kp[s], 16)

            pool.wait_ge(s_con, 112)
            pool.wait_ge(s_o, PAIRS)
            with pool.Fori(0, 2) as r:
                for g in range(2):
                    pool.wait_ge(s_ov, 2 + 17 * r - 1 + g)
                    pool.sem_inc(s_own, 1)
                    k_pages(r, g, g)
                with pool.Fori(1, 8) as gg:
                    for s in range(2):
                        pool.wait_ge(s_sk, 17 * r + 2 * gg + s - 1)
                        pool.sem_inc(s_own, 1)
                        k_pages(r, 2 * gg + s, s)
                for g in range(2):
                    pool.wait_ge(s_sk, 17 * r + 15 + g)
                    pool.sem_inc(s_own, 1)
                    v_pages(r, g, g)
                with pool.Fori(1, 8) as gg:
                    for s in range(2):
                        pool.wait_ge(s_ov, 2 + 17 * r + 2 * gg + s)
                        pool.sem_inc(s_own, 1)
                        v_pages(r, 2 * gg + s, s)


            pool.wait_ge(s_z, 16)
            pool.wait_ge(s_r, R_SLOT)
            for t in range(TILES):
                n = ROWS[t]
                for k in range(2):
                    gp.indirect_dma_start(tokd, bass.IndirectOffsetOnAxis(ap=slotu[0:n, k, t:t + 1], axis=0),
                                         con[0:n, CTOK + t:CTOK + t + 1], None).then_inc(s_tk, 16)
            pool.wait_ge(s_tk, 32 * TILES)
            pool.wait_ge(s_r, R_SLOT + 2)
            gp.dma_start(tokrow, tokd.rearrange("(q p) o -> q (p o)", p=P)).then_inc(s_tl, 16)
            pool.wait_ge(s_r, R_STEPS)
            pool.wait_ge(s_x1, 16 * TILES)

            def gather(m, p, xs):
                sl = slice(p, p + 1) if isinstance(p, int) else bass.ds(p, 1)
                if not (isinstance(p, int) and p < 2):
                    pool.wait_ge(m.xt, p - 1)
                gp.tensor_copy(idc[:, xs:xs + 1], idx[:, sl]).then_inc(m.ic, 1)
                pool.wait_ge(m.ic, p + 1)
                pool.sem_inc(s_own, 1)
                gp.indirect_dma_start(xg[:, xs], None, x1d, bass.IndirectOffsetOnAxis(ap=idc[:, xs:xs + 1], axis=0)
                                      ).then_inc(m.xg[xs], 16)

            for s in range(2):
                gather(moe, s, s)
            with pool.Fori(1, EPAIRS // 2) as i:
                for s in range(2):
                    gather(moe, 2 * i + s, s)
            blocks = pool.value_load(ovi[0:1, 16:17], min_val=0, max_val=OVB)
            overflow(pool, blocks, lambda p, s, n: gather(moe, p, s))
            pool.wait_ge(s_ovr, 1)
            for t in range(TILES):
                n = ROWS[t]
                if t >= 2:
                    pool.wait_ge(s_hd, H_STEPS * (t - 2) + 2)
                for k in range(2):
                    gp.indirect_dma_start(fb[0:n, 2 * k + t % 2], None, ybd,
                                         bass.IndirectOffsetOnAxis(ap=slotu[0:n, k, t:t + 1], axis=0)
                                         ).then_inc(s_gt[t % 2][k], 16)


def constants():
    con = np.zeros((P, NCON), np.float32)
    q = np.arange(P)
    con[:, CI:CI + P] = np.eye(P)
    con[:, C1:C1 + P] = 1.0
    con[:, CU:CU + P] = q[:, None] < q[None, :]
    con[:, CM + 384:CM + 512] = np.where(q[None, :] <= q[:, None], 0.0, NEG)
    con[:, CTHR:CTHR + 8] = CAP * np.arange(1, 9)
    con[:, CGID:CGID + 32] = np.arange(32) // EPG
    con[:, CEID:CEID + 32] = np.arange(32)
    con[:, CEB:CEB + 32] = CAP * np.arange(32)
    for r in range(2):
        con[:, CM8 + NS * r:CM8 + NS * (r + 1)] = (4 * r + q // 32)[:, None] == np.arange(NS)[None, :]
    for t in range(TILES):
        con[:, CTOK + t] = np.minimum(t * P + q, T - 1)
        con[:, CVAL + t] = t * P + q < T
    con[:, CBLK:CBLK + 16] = np.arange(16)
    for r in range(ROPE):
        con[64 + r, CSEL + r] = con[96 + r, CSEL + r] = 1.0
    half = ROPE // 2
    inv = (1.0 / (10000.0 ** (np.arange(half, dtype=np.float32) / half))).astype(np.float32)
    pos = np.concatenate([np.arange(NPR), np.full(NS, PAGE * NPAGES)]).astype(np.float32)
    ang = (pos[None, :] * inv[:, None]).astype(np.float32)
    c, s = np.cos(ang), np.sin(ang)
    c2, s2 = np.concatenate([c, c]), np.concatenate([-s, s])
    rope = np.zeros((3, P, T), np.float32)
    rope[0, 64:96], rope[0, 96:128] = c2, s2
    rope[1, 64:96] = rope[1, 96:128] = c2
    rope[2, 64:96] = rope[2, 96:128] = s2
    return con, rope


def chunks(w, p=P):
    return w.reshape(-1, p, w.shape[-1]).transpose(1, 0, 2)


def laid_out(i):
    x = np.concatenate([i["x_prompt"].reshape(NPR, D), i["x_sample"].reshape(NS, D)])
    w_in = i["w_in"][0]
    o_kv, o_kr, o_cv = QL, QL + KVL, QL + KVL + ROPE
    o_ga = o_cv + 2 * CC
    kr = w_in[:, o_kr:o_kr + ROPE]
    krs = np.concatenate([kr[:, 16:], kr[:, :16]], 1)
    first = np.concatenate([w_in[:, o_kv:o_kv + KVL], krs, krs, kr, kr, w_in[:, :QL], w_in[:, o_cv:o_cv + 2 * CC]], 1)

    def blocks(w):
        return chunks(w).reshape(P, -1, w.shape[1] // P, P).transpose(2, 0, 1, 3)

    uq = i["w_uq"][0].reshape(QL, HEADS, NOPE + ROPE)
    uq = np.concatenate([uq[..., :NOPE], uq[..., NOPE:], uq[..., NOPE + 16:], uq[..., NOPE:NOPE + 16]], -1)
    uq = uq.reshape(KQ, P, HEADS, P).transpose(2, 1, 0, 3)
    uq = uq.reshape(PAIRS, 2, P, KQ * P).transpose(0, 2, 1, 3).reshape(PAIRS, P, 2 * KQ * P)
    uk, uv = i["w_uk"][0], i["w_uv"][0]

    def by_pair(w):
        return w.reshape(KKV, P, PAIRS, 2 * w.shape[-1]).transpose(2, 1, 0, 3).reshape(PAIRS, P, -1)

    ukt = np.zeros((PAIRS, P, 2, KVL), np.float32)
    ukt[:, :NOPE] = uk.transpose(2, 1, 0).reshape(NOPE, PAIRS, 2, KVL).transpose(1, 0, 2, 3)
    wpair = np.concatenate([uq, by_pair(uk), by_pair(uv), ukt.reshape(PAIRS, P, -1)], -1)
    gates = np.concatenate([blocks(w_in[:, o_ga:o_ga + D]), blocks(i["w_pw2"][0]), blocks(w_in[:, o_ga + D:])], 2)
    vec = np.concatenate([np.asarray(v).reshape(-1, P).T for v in
                          (i["q_norm_g"][0], i["kv_norm_g"][0], i["b_dw"][0], i["conv_ln_g"][0], i["conv_ln_b"][0])]
                         + [i["w_dw"][0].T.reshape(KC, P, CW).transpose(1, 0, 2).reshape(P, KC * CW)], 1)
    state = np.zeros((P, KC, NS, CW), np.float32)
    state[..., :CW - 1] = i["state_conv"][0].transpose(2, 0, 1).reshape(KC, P, NS, CW - 1).transpose(1, 0, 2, 3)
    ex = np.concatenate([i["w_gate"][0], i["w_up"][0]], -1).reshape(NEXP, KD, P, 2 * DE).transpose(0, 2, 1, 3)
    dn = i["w_down"][0].reshape(NEXP, 2, P, D).transpose(0, 2, 1, 3)
    con, rope = constants()
    rows = np.stack([i[n][0] for n in ("ln1_g", "ln1_b", "ln2_g", "ln2_b", "ple_norm_g")])
    ple = np.concatenate([i["p_prompt"][0].reshape(NPR, -1), i["p_sample"][0].reshape(NS, -1)])
    ckv, ckr = i["cache_ckv"][0], i["cache_krope"][0]
    kT = np.concatenate([ckv[..., :KR], ckv[..., P:P + KR], ckr, ckv[..., KR:P], ckv[..., P + KR:]], 2).transpose(0, 2, 1)
    steps = i["page_table"].reshape(2, 4, NPAGES // 2, 2).transpose(0, 2, 1, 3)
    out = {
        "xT": chunks(x.T), "x": x, "w1": blocks(first), "wpair": wpair, "wgate": gates, "wo": blocks(i["w_o_attn"][0]),
        "wuv": chunks(uv.reshape(KVL, -1)), "w_out": chunks(i["w_out"][0]),
        "w_rt": chunks(np.concatenate([i["w_group"][0], i["w_router"][0]], 1)),
        "wexp": np.concatenate([ex.reshape(NEXP, P, -1), dn.reshape(NEXP, P, -1)], -1),
        "w_plg": chunks(i["w_ple_gate"][0]), "w_plp": chunks(i["w_ple_proj"][0]), "plT": chunks(ple.T),
        "kT": kT.reshape(NPOOL, 3, KR, PAGE).transpose(0, 2, 1, 3).reshape(NPOOL, KR, 3 * PAGE), "vc": ckv,
        "state": state, "vec": vec, "con": con, "rope": rope,
        "lnrows": np.broadcast_to(rows[None], (P, 5, D)), "pages": steps.reshape(1, -1),
    }
    return {n: np.ascontiguousarray(v) for n, v in out.items()}


OUTS = {"y": (T, D), "ckv": (P, KKV, T), "krope": (ROPE, T), "conv_p": (P, KC, CW - 1), "conv_s": (P, KC, NS, CW)}


def kernel(**inputs):
    import concourse.bacc as bacc
    from concourse.bass_utils import run_bass_kernel_spmd

    arrays = laid_out({n: np.asarray(v) for n, v in inputs.items()})
    nc = bacc.Bacc("TRN2", target_bir_lowering=False, num_devices=1)
    a = {n: nc.dram_tensor(f"in_{n}", v.shape, mybir.dt.from_np(v.dtype), kind="ExternalInput").ap()
         for n, v in arrays.items()}
    o = {n: nc.dram_tensor(f"out_{n}", s, F32, kind="ExternalOutput").ap() for n, s in OUTS.items()}
    decoder_layer(nc, a, o)
    r = run_bass_kernel_spmd(nc, [{f"in_{n}": v for n, v in arrays.items()}], core_ids=[0]).results[0]
    y, ckv, kr, cp, cs = (r[f"out_{n}"] for n in ("y", "ckv", "krope", "conv_p", "conv_s"))
    ckv = ckv.transpose(2, 1, 0).reshape(T, KVL)
    kr = kr.T
    cp = cp.transpose(2, 1, 0).reshape(CW - 1, CC)
    cs = cs[..., 1:].transpose(2, 3, 1, 0).reshape(NS, CW - 1, CC)
    return (y[:NPR].reshape(1, NPR, D), y[NPR:].reshape(NS, 1, D),
            ckv[:NPR].reshape(1, 1, NPR, KVL), kr[:NPR].reshape(1, 1, NPR, ROPE), cp.reshape(1, 1, CW - 1, CC),
            ckv[NPR:].reshape(1, NS, 1, KVL), kr[NPR:].reshape(1, NS, 1, ROPE), cs.reshape(1, NS, CW - 1, CC))
```

```python
from contextlib import ExitStack

import numpy as np

import concourse.bass as bass
from concourse import mybir

F32 = mybir.dt.float32
I32 = mybir.dt.int32
U32 = mybir.dt.uint32
ALU = mybir.AluOpType
ACT = mybir.ActivationFunctionType
AX = mybir.AxisListType

P = 128
D = 1024
NPR = 512
NS = 8
T = NPR + NS
TH = T // 2
KD = D // P
QL, KVL, ROPE, NOPE, VH = 384, 256, 32, 64, 64
KQ, KKV = QL // P, KVL // P
KR = (KVL + ROPE) // 3
SPN = 5
HEADS = 16
PAIRS = HEADS // 2
CC = 512
KC = CC // P
CW = 31
NA = KKV + 1 + KQ + 2 * KC
B_CKV, B_KR, B_CQ, B_CA, B_CB = 0, KKV, KKV + 1, KKV + 1 + KQ, KKV + 1 + KQ + KC
NCV = 2 * KC
PRE = CW - 3 * (PAIRS - 1)
PAIRW = 2 * KQ * P + 2 * KKV * P + 2 * KVL
PAGE, NPAGES = 128, 32
NPOOL = 5 * NS * NPAGES // 4
NEXP, NGRP, EPG, DE = 32, 4, 8, 256
CAP = 64
EPAIRS = NEXP // 2
OVB = 2 * T // CAP
SLOTS = (NEXP + OVB) * CAP
EW1 = KD * 2 * DE
EW = EW1 + 2 * D
TILES = 5
ROWS = [P, P, P, P, NS]
N_NRM, LN_STEPS, RND, FD = 10, 10, 17, 8
CONV_STEPS = KC * CW
N_INI = 6
R_EXP, R_EXP2, R_RANK, R_SLOT, R_STEPS = 12, 19, 29, 51, 57
HF_STEPS, HB_STEPS = 10, 4
SCALE = float((NOPE + ROPE) ** -0.5)
ALPHA = float(2.0 ** 0.25)
LN_EPS, RMS_EPS = 1e-5, 1e-6
BIG = 3.0e38
NEG = -1e30

CI, C1, CU, CM = 0, 128, 256, 384
CTHR = CM + 512
CGID = CTHR + 8
CEID = CGID + 32
CEB = CEID + 32
CM8 = CEB + 32
CTOK = CM8 + 16
CVAL = CTOK + 5
CBLK = CVAL + 5
CSEL = CBLK + 16
CSUM = CSEL + 32
NCON = CSUM + 16
VQG, VKG, VBD, VLG, VLB, VDW = 0, 3, 5, 9, 13, 17
NVEC = VDW + KC * CW

A_MIX = 0
A_OT = 4160
A_XT = 8320
A_HT = 12480
A_SIGB = A_HT + B_CA * T
A_EXT = A_HT + NA * T
A_EXS = A_EXT + KC * (CW - 1 + NPR)
A_ACC = A_EXS + KC * NS * CW
A_TMP = A_ACC + KC * T + 80
A_PAIR = A_TMP + 3 * T + 8
A_QT = A_PAIR + 2 * PAIRW
A_KT = A_QT + 4 * T
A_V = A_KT + 4 * NPR
A_P = A_V + 2 * NPR
A_PT = A_P + 2 * 1280
A_KRING = A_PT + 2 * 2048
A_RQ = A_KRING + 2 * 3072
A_SML = A_RQ + T
A_END1 = A_SML + 2053
A_RC = A_PT + 80
A_RS = A_RC + T
A_ERING = A_PAIR
A_SG = A_ERING + 2 * 20 * P
A_S = A_SG + T
A_WUV = A_S + 4104
A_PTS = A_WUV + 2048
A_OLAT = A_PTS + 512
A_OLT = A_OLAT + 256
A_SGB = A_XT
A_WO = A_XT + T
assert A_WO + 2 * D <= A_HT
A_WBIG = A_EXT
A_RT = A_WBIG + 8192
A_X1 = A_RT + 2048
A_LN = A_X1 + TILES * D
A_RW = A_LN + 2048
A_X1T = A_RW + 288
A_W0 = A_X1T + 1024
A_W1 = A_OT
A_XG = A_MIX
A_XGT = A_XG + 2048
A_HS = A_XGT + 1024
A_HTS = A_HS + 512
assert A_HTS + 256 <= A_OT
A_Y = A_W1 + 2 * EW
A_PLT = A_Y + 2048
assert A_PLT + 2 * T <= A_EXT and 12 * D <= 2 * EW
A_ROWS = A_LN
A_WPP = A_RT
A_PG = A_X1T
A_F = A_W0
ARENA = max(A_END1, A_W0 + 2 * EW)


def decoder_layer(nc, a, o):
    ctx = ExitStack()
    with ctx:
        def sb(name, shape, dt=F32):
            return ctx.enter_context(nc.sbuf_tensor(name, shape, dt))

        def sem(name):
            return ctx.enter_context(nc.semaphore(name))

        arena = sb("arena", [P, ARENA])
        ps = ctx.enter_context(nc.psum_tensor("ps", [P, 8, 512], F32))

        def at(off, n):
            return arena[:, off:off + n]

        con = sb("con", [P, NCON])
        vec = sb("vec", [P, NVEC])
        pages = sb("pages", [1, NS * NPAGES], I32)
        eps = sb("eps", [P, 2])
        ident, ones, utri, maskw = con[:, CI:CI + P], con[:, C1:C1 + P], con[:, CU:CU + P], con[:, CM:CM + 512]

        xT = at(A_XT, KD * T).rearrange("p (k t) -> p k t", k=KD)
        hT = at(A_HT, NA * T).rearrange("p (b t) -> p b t", b=NA)
        hTh = at(A_HT, NA * T).rearrange("p (b h t) -> p b h t", b=NA, h=2)
        w1 = at(A_KRING, 2 * KD * P).rearrange("p (s k m) -> p s k m", s=2, k=KD)
        ext = at(A_EXT, KC * (CW - 1 + NPR)).rearrange("p (c t) -> p c t", c=KC)
        exs = at(A_EXS, KC * NS * CW).rearrange("p (c b w) -> p c b w", c=KC, b=NS)
        aT = at(A_ACC, KC * T).rearrange("p (c t) -> p c t", c=KC)
        tmp = at(A_TMP, 3 * T).rearrange("p (c t) -> p c t", c=3)
        tmph = at(A_TMP, 3 * T).rearrange("p (c h t) -> p c h t", c=3, h=2)
        sq = at(A_P, 5 * T).rearrange("p (c t) -> p c t", c=5)
        exw = at(A_P, NS * CW)
        rq, rc, rsn = at(A_RQ, T), at(A_RC, T), at(A_RS, T)
        small = [A_SML]

        def take(n):
            small[0] += n
            return at(small[0] - n, n)

        mixT = at(A_MIX, KD * T).rearrange("p (k t) -> p k t", k=KD)
        mixh = at(A_MIX, KD * T).rearrange("p (k h t) -> p k h t", k=KD, h=2)
        oT = at(A_OT, KD * T).rearrange("p (k t) -> p k t", k=KD)
        sigB = at(A_SIGB, KD * T).rearrange("p (k t) -> p k t", k=KD)
        sigBh = at(A_SIGB, KD * T).rearrange("p (k h t) -> p k h t", k=KD, h=2)

        pw = at(A_PAIR, 2 * PAIRW).rearrange("p (s n) -> p s n", s=2)
        qT = at(A_QT, 4 * T).rearrange("p (s x t) -> p s x t", s=2, x=2)
        qTh = at(A_QT, 4 * T).rearrange("p (s x h t) -> p s x h t", s=2, x=2, h=2)
        kT = at(A_KT, 4 * NPR).rearrange("p (s x t) -> p s x t", s=2, x=2)
        vv = at(A_V, 2 * NPR).rearrange("p (s j v) -> p s j v", s=2, j=4)
        vf = at(A_V, 2 * NPR).rearrange("p (s n) -> p s n", s=2)
        prob = at(A_P, 2 * 1280).rearrange("p (x n) -> p x n", x=2)
        pT = at(A_PT, 2 * 2048).rearrange("p (x j q) -> p x j q", x=2, j=4)
        POFF = [0, 128, 384, 768]
        mx = sb("mx", [P, 2, 4])
        nb = sb("nb", [P, 2, 4])
        rs = sb("rs", [P, 2, 4])
        rr = sb("rr", [P, 2, 4])

        def sqc(c):
            return at(A_MIX + D + c * T, T)

        kring = at(A_KRING, 2 * 3072).rearrange("p (s n) -> p s n", s=2)
        vring = at(A_KRING, 3 * 2048).rearrange("p (s n) -> p s n", s=3)
        qlat = take(KKV * NS * 32).rearrange("p (c b h) -> p c b h", c=KKV, b=NS)
        qrr = take(NS * HEADS).rearrange("p (b h) -> p b h", b=NS)
        qrs = take(NS * 32).rearrange("p (b h) -> p b h", b=NS)[0:32]
        qcur = take(3 * 4 * 32).rearrange("p (c b h) -> p c b h", c=3, b=4)[0:KR]
        knew = sb("knew", [KR, 3, 4])
        krs = sb("krs", [32, NS])
        S = at(A_S, 4104)
        wuv = at(A_WUV, 2048).rearrange("p (c n) -> p c n", c=KKV)
        pts = at(A_PTS, 512).rearrange("p (s n) -> p s n", s=2)
        olat = at(A_OLAT, 256)
        olT = at(A_OLT, 512).rearrange("p (c r n) -> p c r n", c=KKV, r=2)
        ckvs = take(KVL)[0:NS]
        pnT = take(P)[0:NS]
        assert small[0] <= A_END1 and A_OLT + 512 <= A_KRING
        sm = sb("sm", [P, 8])
        smp = sb("smp", [P, 4])
        rsum = sb("rsum", [P, 5])
        pnm = sb("pnm", [P, NS])
        er = at(A_ERING, 2 * 20 * P).rearrange("p (s k m) -> p s k m", s=2, k=20)
        sg = at(A_SG, T)
        sgh = at(A_SG, T).rearrange("p (h t) -> p h t", h=2)
        sgb = at(A_SGB, T)
        sgbh = at(A_SGB, T).rearrange("p (h t) -> p h t", h=2)
        wo = at(A_WO, 2 * KD * P).rearrange("p (s k m) -> p s k m", s=2, k=KD)

        wbig = at(A_WBIG, KD * D).rearrange("p (k n) -> p k n", k=KD)
        wpp = at(A_WPP, 2 * D).rearrange("p (k n) -> p k n", k=2)
        x1 = at(A_X1, TILES * D).rearrange("p (t n) -> p t n", t=TILES)
        lnr = at(A_LN, 2 * D).rearrange("p (t n) -> p t n", t=2)
        rw = at(A_RW, KD * 36).rearrange("p (k n) -> p k n", k=KD)
        x1T = at(A_X1T, KD * P).rearrange("p (k n) -> p k n", k=KD)
        plT = at(A_PLT, 2 * T).rearrange("p (k t) -> p k t", k=2)
        bst = sb("bst", [P, 2, 6])
        mv = sb("mv", [P, 2])
        rstd = sb("rstd", [P, 2])
        rms = sb("rms", [P, 2])
        rt = [A_RT]

        def route(n, dt=F32):
            rt[0] += n
            v = at(rt[0] - n, n)
            return v if dt == F32 else v.bitcast(dt)

        def by_tile(n, dt=F32):
            return route(TILES * n, dt).rearrange("p (t n) -> p t n", t=TILES)

        L = by_tile(40)
        gv, gi, ev, ei = by_tile(8), by_tile(8, U32), by_tile(8), by_tile(8, U32)
        gf = route(TILES)
        ms, ms2, ohs, pos, ef, gx, gg = (by_tile(n) for n in (32, 32, 32, 32, 2, 4, 4))
        oh = route(2 * TILES * 32).rearrange("p (k t e) -> p k t e", k=2, t=TILES)
        pf = route((TILES + 1) * 32).rearrange("p (t e) -> p t e", e=32)
        cmp8 = route(256).rearrange("p (e m) -> p e m", m=8)
        cnt, nov, oend, one32, dsl = (route(32) for _ in range(5))
        slotf = route(2 * TILES).rearrange("p (k t) -> p k t", k=2)
        assert rt[0] <= A_X1
        gates = sb("gates", [P, 2, TILES])
        slotu = sb("slotu", [P, 2, TILES], U32)
        ovf = sb("ovf", [1, 17])
        ovi = sb("ovi", [1, 17], I32)
        ovc = at(A_X1T, 512).rearrange("p (b e) -> p b e", b=16)[0:1]
        tokrow = at(A_X1T + 512, P)[0:SLOTS // P]
        idx = sb("idx", [P, SLOTS // P], U32)
        idc = sb("idc", [P, 2], U32)
        wx = [at(A_W0, 2 * EW).rearrange("p (x n) -> p x n", x=2), at(A_W1, 2 * EW).rearrange("p (x n) -> p x n", x=2)]
        xg = at(A_XG, 2 * D).rearrange("p (s n) -> p s n", s=2)
        xgT = at(A_XGT, KD * P).rearrange("p (k n) -> p k n", k=KD)
        sgE = at(A_HS, 256)
        hs = at(A_HS + 256, 256)
        htT = at(A_HTS, 256).rearrange("p (c n) -> p c n", c=2)
        yb = at(A_Y, 2 * D).rearrange("p (s n) -> p s n", s=2)
        ln2r = at(A_ROWS, 2 * D).rearrange("p (t n) -> p t n", t=2)
        pgr = at(A_PG, D)
        fb = at(A_F, 12 * D).rearrange("p (s n) -> p s n", s=12)
        FX = (4, 10)
        fbT = at(A_F + 9 * D, D).rearrange("p (k n) -> p k n", k=KD)
        zeros = at(A_MIX, D)
        parts = at(A_MIX, D)

        x1d = nc.dram_tensor("x1_scratch", (T, D), F32, kind="Internal").ap()
        ybd = nc.dram_tensor("y_scratch", (SLOTS, D), F32, kind="Internal").ap()
        tokd = nc.dram_tensor("token_of_slot", (SLOTS, 1), F32, kind="Internal").ap()

        s_con = sem("s_con")
        s_x = sem("s_x")
        s_w1 = [sem("s_w1a"), sem("s_w1b")]
        s_ini = sem("s_ini")
        s_ha = sem("s_ha")
        s_ht = sem("s_ht")
        s_sq = sem("s_sq")
        s_ss = sem("s_ss")
        s_rt = sem("s_rt")
        s_kro = sem("s_kro")
        s_nrm = sem("s_nrm")
        s_u = sem("s_u")
        s_gl = sem("s_gl")
        s_cv = sem("s_cv")
        s_sc = sem("s_sc")
        s_ln = sem("s_ln")
        s_kf = sem("s_kf")
        s_sw = sem("s_sw")
        s_pw = [sem("s_pwa"), sem("s_pwb")]
        s_g = sem("s_g")
        s_ga = sem("s_ga")
        s_gd = sem("s_gd")
        s_s = sem("s_s")
        s_mx = sem("s_mx")
        s_nb = sem("s_nb")
        s_ex = sem("s_ex")
        s_rc = sem("s_rc")
        s_pr = sem("s_pr")
        s_tp = sem("s_tp")
        s_ta = sem("s_ta")
        s_td = sem("s_td")
        s_o = sem("s_o")
        s_ot = sem("s_ot")
        s_qs = sem("s_qs")
        s_qc = sem("s_qc")
        s_k = [sem("s_ka"), sem("s_kb")]
        s_kp = [sem("s_kpa"), sem("s_kpb")]
        s_v = [sem("s_v" + x) for x in "abc"]
        s_vp = [sem("s_vp" + x) for x in "abc"]
        s_wuv = sem("s_wuv")
        s_er = [sem("s_era"), sem("s_erb")]
        s_cm = sem("s_cm")
        s_sqc = sem("s_sqc")
        s_d = sem("s_d")
        s_da = sem("s_da")
        s_dd = sem("s_dd")
        s_sk = sem("s_sk")
        s_ske = sem("s_ske")
        s_rnd = sem("s_rnd")
        s_pcx = sem("s_pcx")
        s_pt = sem("s_pt")
        s_pte = sem("s_pte")
        s_ov = sem("s_ov")
        s_on = sem("s_on")
        s_os = sem("s_os")
        s_ose = sem("s_ose")
        s_wo = [sem("s_woa"), sem("s_wob")]
        s_b = sem("s_b")
        s_bt = sem("s_bt")
        s_mt = sem("s_mt")
        s_wb = sem("s_wb")
        s_fp = sem("s_fp")
        s_fc = sem("s_fc")
        s_f = sem("s_f")
        s_fd = sem("s_fd")
        s_fa = sem("s_fa")
        s_fx = sem("s_fx")
        s_fe = sem("s_fe")
        s_fl = sem("s_fl")
        s_x1 = sem("s_x1")
        s_r = sem("s_r")
        s_ra = sem("s_ra")
        s_rp = sem("s_rp")
        s_z = sem("s_z")
        s_yz = sem("s_yz")
        s_tk = sem("s_tk")
        s_tl = sem("s_tl")
        s_out = sem("s_out")
        s_wx = [[sem("s_w00"), sem("s_w01")], [sem("s_w10"), sem("s_w11")]]
        s_wd = [[sem("s_d00"), sem("s_d01")], [sem("s_d10"), sem("s_d11")]]
        s_plw = sem("s_plw")
        s_plg = sem("s_plg")
        s_gt = [[sem("s_gt00"), sem("s_gt01")], [sem("s_gt10"), sem("s_gt11")]]
        s_h = sem("s_h")
        s_hf = sem("s_hf")
        s_hr = sem("s_hr")
        s_hc = sem("s_hc")
        s_hg = sem("s_hg")
        s_hs = sem("s_hs")
        s_hb = sem("s_hb")
        s_yo = [sem("s_yoa"), sem("s_yob")]

        s_own = sem("s_own")

        class Moe:
            def __init__(self, n):
                self.ic = sem(n + "ic")
                self.xg = [sem(n + "xga"), sem(n + "xgb")]
                self.xt = sem(n + "xt")
                self.xa = sem(n + "xa")
                self.xd = sem(n + "xd")
                self.h = sem(n + "h")
                self.sg = sem(n + "sg")
                self.hs = sem(n + "hs")
                self.ht = sem(n + "ht")
                self.he = sem(n + "he")
                self.y = sem(n + "y")
                self.ya = sem(n + "ya")
                self.yd = sem(n + "yd")
                self.yw = [sem(n + "ywa"), sem(n + "ywb")]

        moe = Moe("m_")
        s_ovr = sem("s_ovr")

        def kpage(s, j):
            return kring[0:KR, s, j * 3 * P:(j + 1) * 3 * P]

        def vpage(s, j):
            return vring[:, s, j * KVL:(j + 1) * KVL]

        def narrow(bank, rows32, w):
            for k0 in (0, 4):
                for h in range(2):
                    for j in range(4):
                        y = nc.tensor.matmul(ps[32 * j:32 * j + 32, bank + h, :], rows32(k0 + j),
                                             w[:, k0 + j, h * 512:(h + 1) * 512], start=(k0 == 0), stop=(k0 == 4))
            return y

        def narrow_sum(bank, part, which):
            for h in range(2):
                y = nc.tensor.matmul(ps[0:NS, bank + h, :], con[:, CSUM + NS * which:CSUM + NS * (which + 1)],
                                     part[:, h * 512:(h + 1) * 512], start=True, stop=True)
            return y

        def overflow(eng, blocks, body):
            with eng.Fori(0, OVB // 4) as i:
                for s in range(2):
                    with eng.If(blocks > 4 * i + 2 * s):
                        body(EPAIRS + 2 * i + s, s, EPAIRS // 2 + i)

        block = ctx.enter_context(nc.Block())

        @block.sync
        def _(sp):
            sp.dma_start(xT[:, 0:4], a["xT"][:, 0:4]).then_inc(s_x, 16)
            sp.dma_start(w1[:, 0], a["w1"][0]).then_inc(s_w1[0], 16)
            sp.dma_start(xT[:, 4:8], a["xT"][:, 4:8]).then_inc(s_x, 16)
            sp.dma_start(w1[:, 1], a["w1"][1]).then_inc(s_w1[1], 16)
            sp.dma_start(con[:], a["con"]).then_inc(s_con, 16)
            sp.dma_start(rq, a["rope"][0]).then_inc(s_con, 16)
            sp.dma_start(rc, a["rope"][1]).then_inc(s_con, 16)
            sp.dma_start(rsn, a["rope"][2]).then_inc(s_con, 16)
            sp.dma_start(vec[:], a["vec"]).then_inc(s_con, 16)
            sp.dma_start(pages[:], a["pages"]).then_inc(s_con, 16)
            sp.dma_start(exs[:], a["state"]).then_inc(s_con, 16)
            for s in range(2):
                sp.dma_start(pw[:, s], a["wpair"][s]).then_inc(s_pw[s], 16)
            with sp.Fori(1, NA // 2) as i:
                for s in range(2):
                    sp.wait_ge(s_ha, 2 * i + s - 1)
                    sp.dma_start(w1[:, s], a["w1"][bass.ds(2 * i + s, 1)].rearrange("a p k m -> (a p) k m")
                                 ).then_inc(s_w1[s], 16)
            sp.wait_ge(s_ini, 1)
            sp.dma_start(tokd.rearrange("(q p) o -> q (p o)", p=P), zeros[0:SLOTS // P, 0:P]).then_inc(s_z, 16)
            sp.dma_start(ybd[NEXP * CAP:SLOTS].rearrange("(q p) n -> p q n", p=P),
                         zeros.unsqueeze(1).to_broadcast([P, OVB * CAP // P, D])).then_inc(s_yz, 16)
            with sp.Fori(1, PAIRS // 2) as i:
                for s in range(2):
                    sp.wait_ge(s_g, 4 * (2 * i + s - 1))
                    sp.dma_start(pw[:, s], a["wpair"][bass.ds(2 * i + s, 1)].rearrange("a p n -> (a p) n")
                                 ).then_inc(s_pw[s], 16)
            sp.wait_ge(s_nrm, N_NRM)
            sp.dma_start(o["ckv"], hT[:, B_CKV:B_CKV + KKV, :]).then_inc(s_out, 16)
            sp.dma_start(o["krope"], hT[64:96, B_KR, :]).then_inc(s_out, 16)
            sp.wait_ge(s_gl, 2 * KC)
            sp.dma_start(o["conv_p"], ext[:, :, NPR:NPR + CW - 1]).then_inc(s_out, 16)
            sp.dma_start(o["conv_s"], exs[:]).then_inc(s_out, 16)

            numbers = [sp.alloc_register(f"sp_page{j}") for j in range(SPN)]

            def step_pages(r, g):
                sp.load(numbers, pages[0:1, bass.ds(8 * (16 * r + g), SPN)])

            def k_pages(r, g, s):
                for j in range(SPN):
                    pg = sp.snap(numbers[j], min_val=0, max_val=NPOOL - 1)
                    sp.dma_start(kpage(s, j), a["kT"][bass.ds(pg, 1)].rearrange("a p n -> (a p) n")).then_inc(s_k[s], 16)

            def v_pages(r, g, s):
                for j in range(SPN):
                    pg = sp.snap(numbers[j], min_val=0, max_val=NPOOL - 1)
                    sp.dma_start(vpage(s, j), a["vc"][bass.ds(pg, 1)].rearrange("a p n -> (a p) n")).then_inc(s_v[s], 16)

            sp.wait_ge(s_con, 112)
            sp.wait_ge(s_ha, NA)
            with sp.Fori(0, 2) as r:
                for g in (1, 0):
                    step_pages(r, g)
                    sp.wait_ge(s_ov, 2 + 17 * r - g)
                    k_pages(r, g, g)
                with sp.Fori(1, 8) as gg:
                    for s in range(2):
                        step_pages(r, 2 * gg + s)
                        sp.wait_ge(s_sk, 17 * r + 2 * gg + s - 1)
                        k_pages(r, 2 * gg + s, s)
                for g in range(3):
                    step_pages(r, g)
                    sp.wait_ge(s_sk, 17 * r + (15 if g == 0 else 16))
                    v_pages(r, g, g)
                with sp.Fori(1, 5) as gg:
                    for s in range(3):
                        step_pages(r, 3 * gg + s)
                        sp.wait_ge(s_ov, 2 + 17 * r + 3 * gg + s - 1)
                        v_pages(r, 3 * gg + s, s)
                step_pages(r, 15)
                sp.wait_ge(s_ov, 2 + 17 * r + 14)
                v_pages(r, 15, 0)

            sp.wait_ge(s_d, 4 + 24)
            sp.wait_ge(s_os, 1)
            for s in range(2):
                sp.dma_start(wo[:, s], a["wo"][s]).then_inc(s_wo[s], 16)
            sp.wait_ge(s_out, 64)
            sp.dma_start(wbig[:, 0:2], a["w_out"][:, 0:2]).then_inc(s_wb, 16)
            sp.dma_start(rw[:], a["w_rt"]).then_inc(s_wb, 16)
            with sp.Fori(1, KD // 2) as i:
                for s in range(2):
                    sp.wait_ge(s_b, 2 * i + s - 1)
                    sp.dma_start(wo[:, s], a["wo"][bass.ds(2 * i + s, 1)].rearrange("a p k m -> (a p) k m")
                                 ).then_inc(s_wo[s], 16)
                sp.dma_start(wbig[:, bass.ds(2 * i, 2)], a["w_out"][:, bass.ds(2 * i, 2)]).then_inc(s_wb, 16)
            sp.wait_ge(s_ose, 1)
            sp.dma_start(x1[:, 0:4], a["x"][0:NPR].rearrange("(t p) n -> p t n", p=P)).then_inc(s_wb, 16)
            sp.dma_start(x1[0:NS, 4], a["x"][NPR:T]).then_inc(s_wb, 16)
            sp.dma_start(lnr[:], a["lnrows"][:, 0:2]).then_inc(s_wb, 16)

            def expert_weights(s, x, e, down):
                lo, hi, done = (EW1, EW, s_wd) if down else (0, EW1, s_wx)
                e = slice(e, e + 1) if isinstance(e, int) else bass.ds(e, 1)
                sp.dma_start(wx[s][:, x, lo:hi], a["wexp"][e, :, lo:hi].rearrange("a p n -> (a p) n")
                             ).then_inc(done[s][x], 16)

            for down in range(2):
                for x in range(2):
                    expert_weights(0, x, x, down)
            sp.wait_ge(s_mt, KD)
            for down in range(2):
                for x in range(2):
                    expert_weights(1, x, 2 + x, down)
            for t in range(TILES):
                sp.wait_ge(s_fd, FD * (t + 1))
                sp.dma_start(x1d[t * P:t * P + ROWS[t]], x1[0:ROWS[t], t]).then_inc(s_x1, 16)
            sp.wait_ge(s_f, TILES)
            sp.dma_start(wbig[:], a["w_plg"]).then_inc(s_plg, 16)
            sp.dma_start(plT[:], a["plT"]).then_inc(s_plw, 16)
            sp.dma_start(ln2r[:], a["lnrows"][:, 2:4]).then_inc(s_plw, 16)
            sp.wait_ge(s_r, R_STEPS)
            sp.dma_start(pgr[:], a["lnrows"][:, 4]).then_inc(s_plw, 16)
            sp.dma_start(wpp[:], a["w_plp"]).then_inc(s_plw, 16)
            with sp.Fori(1, EPAIRS // 2) as i:
                for s in range(2):
                    for down, used in ((0, moe.h), (1, moe.y)):
                        sp.wait_ge(used, 2 * i + s - 1)
                        for x in range(2):
                            expert_weights(s, x, 4 * i + 2 * s + x, down)
            sp.wait_ge(s_r, R_STEPS)
            blocks = sp.value_load(ovi[0:1, 16:17], min_val=0, max_val=OVB)

            def weights(p, s, n):
                sp.wait_ge(moe.y, p - 1)
                sp.sem_inc(s_own, 1)
                for x in range(2):
                    e = sp.value_load(ovi[0:1, bass.ds(2 * (p - EPAIRS) + x, 1)], min_val=0, max_val=NEXP - 1)
                    for down in range(2):
                        expert_weights(s, x, e, down)

            overflow(sp, blocks, weights)
            for t in range(TILES):
                sp.wait_ge(s_hb, HB_STEPS * (t + 1))
                sp.dma_start(o["y"][t * P:t * P + ROWS[t]], fb[0:ROWS[t], 6 + t % 2]).then_inc(s_yo[t % 2], 16)
            sp.wait_ge(s_yo[0], 48)
            sp.wait_ge(s_yo[1], 32)
            sp.wait_ge(s_out, 64)

        @block.tensor
        def _(pe):
            mm = nc.tensor.matmul
            tr = nc.tensor.transpose

            pe.sem_inc(s_d, 4)
            pe.sem_inc(s_ov, 2)

            pe.wait_ge(s_x, 32)

            def a_block(b, s, n):
                pe.wait_ge(s_w1[s], 16 * n)
                if not (isinstance(b, int) and b < 2):
                    pe.wait_ge(s_ht, b - 1)
                for k in range(KD):
                    for h in range(2):
                        x = mm(ps[:, 2 * s + h, 0:TH], w1[:, s, k], xT[:, k, h * TH:(h + 1) * TH],
                               start=(k == 0), stop=(k == KD - 1))
                x.then_inc(s_ha, 1)

            for s in range(2):
                a_block(s, s, 1)
            with pe.Fori(1, (NCV + KKV) // 2) as i:
                for s in range(2):
                    a_block(2 * i + s, s, i + 1)
            for b in range(NCV + KKV, NCV + KKV + 2):
                a_block(b, b % 2, b // 2 + 1)
            pe.wait_ge(s_con, 112)
            pe.wait_ge(s_sq, 1)
            for c in range(KKV):
                for h in range(2):
                    x = mm(ps[:, 4 + h, 0:TH], ones, sq[:, c, h * TH:(h + 1) * TH], start=(c == 0), stop=(c == KKV - 1))
            x.then_inc(s_ss, 1)
            for b in range(NCV + KKV + 2, NA):
                a_block(b, b % 2, b // 2 + 1)
            pe.wait_ge(s_sq, 2)
            for c in range(KQ):
                for h in range(2):
                    x = mm(ps[:, 6 + h, 0:TH], ones, sq[:, KKV + c, h * TH:(h + 1) * TH], start=(c == 0),
                           stop=(c == KQ - 1))
            x.then_inc(s_ss, 1)

            WQ, WK, WV, WL = 0, 2 * KQ * P, 2 * KQ * P + KKV * P, 2 * KQ * P + 2 * KKV * P

            def gen_q(p, s, x, n):
                if x == 0:
                    pe.wait_ge(s_pw[s], 16 * n)
                    if isinstance(p, int) and p == 0:
                        pe.wait_ge(s_nrm, N_NRM)
                        pe.wait_ge(s_ht, NA)
                    else:
                        pe.wait_ge(s_gd, 6 * p)
                else:
                    pe.wait_ge(s_ga, 4 * p + 3)
                    pe.wait_ge(s_gd, 6 * p + 3)
                for k in range(KQ):
                    for h in range(2):
                        y = mm(ps[:, h, 0:TH], pw[:, s, WQ + (x * KQ + k) * P:WQ + (x * KQ + k + 1) * P],
                               hT[:, B_CQ + k, h * TH:(h + 1) * TH], start=(k == 0), stop=(k == KQ - 1))
                y.then_inc(s_g, 1)

            def gen_kv(p, s):
                pe.wait_ge(s_ga, 4 * p + 1)
                pe.wait_ge(s_gd, 6 * p + 2)
                for c in range(KKV):
                    mm(ps[:, 0, :], pw[:, s, WK + c * P:WK + (c + 1) * P], hT[:, B_CKV + c, 0:NPR],
                       start=(c == 0), stop=(c == KKV - 1))
                for j in range(4):
                    for c in range(KKV):
                        y = mm(ps[:, 1, j * P:(j + 1) * P], hT[:, B_CKV + c, j * P:(j + 1) * P],
                               pw[:, s, WV + c * P:WV + (c + 1) * P], start=(c == 0), stop=(c == KKV - 1))
                y.then_inc(s_g, 1)

            def gen_lat(p, s):
                pe.wait_ge(s_ga, 4 * p + 4)
                pe.wait_ge(s_gd, 6 * p + 5)
                for x in range(2):
                    for c in range(KKV):
                        y = mm(ps[:, 0, (2 * x + c) * NS:(2 * x + c + 1) * NS],
                               pw[0:64, s, WL + x * KVL + c * P:WL + x * KVL + (c + 1) * P],
                               qT[0:64, s, x, NPR:T], start=True, stop=True)
                y.then_inc(s_g, 1)

            def scores(p, s, x):
                hh = 2 * p + x
                if x == 0:
                    pe.wait_ge(s_gd, 6 * p + 5)
                    pe.wait_ge(s_ga, 4 * p + 4)
                    if isinstance(p, int) and p == 0:
                        pe.wait_ge(s_kf, 4)
                        pe.wait_ge(s_rt, 2)
                if not (isinstance(p, int) and hh == 0):
                    pe.wait_ge(s_mx, 4 * hh)
                for bank, tiles in ((2, (0, 2)), (3, (1,)), (4, (3,))):
                    for i in tiles:
                        c0 = P if i == 2 else 0
                        y = mm(ps[:, bank, c0:c0 + (i + 1) * P], qT[:, s, x, i * P:(i + 1) * P],
                               kT[:, s, x, 0:(i + 1) * P], start=True, stop=True)
                    y.then_inc(s_s, 1)

            def turn(p, s, x):
                hh = 2 * p + x
                for bank, tiles in ((5, (0, 2)), (7, (1,)), (6, (3,))):
                    pe.wait_ge(s_pr, 4 * hh + {5: 2, 7: 3, 6: 4}[bank])
                    if not (isinstance(p, int) and hh == 0):
                        if bank == 5:
                            pe.wait_ge(s_td, 2 * hh)
                        elif bank == 7:
                            pe.wait_ge(s_ta, 2 * hh)
                            if x == 0:
                                pe.wait_ge(s_ot, p)
                    for i in tiles:
                        c0 = P if i == 2 else 0
                        for j in range(i + 1):
                            y = tr(ps[:, bank, c0 + j * P:c0 + (j + 1) * P],
                                   prob[:, x, POFF[i] + j * P:POFF[i] + (j + 1) * P], ident)
                    y.then_inc(s_tp, 1)

            def values(p, s):
                pe.wait_ge(s_ta, 4 * (p + 1))
                pe.wait_ge(s_td, 4 * (p + 1))
                for j in range(4):
                    for x in range(2):
                        y = mm(ps[64 * x:64 * x + 64, 7, j * P:NPR], vv[:, s, j, 64 * x:64 * x + 64],
                               pT[:, x, j, j * P:NPR], start=(j == 0), stop=(j == 3))
                y.then_inc(s_o, 1)

            def conv_sums(n, x):
                for c in range(KC):
                    for h in range(2):
                        y = mm(ps[:, h, 0:TH], ones, x(c)[:, h * TH:(h + 1) * TH], start=(c == 0), stop=(c == KC - 1))
                y.then_inc(s_cm, 1)

            def pair(p, s, n, first=False, last=False):
                q = 1 - s
                scores(p, s, 0)
                if not first:
                    turn(p - 1, q, 1)
                if not last:
                    gen_q(p + 1, q, 0, n)
                if not first:
                    values(p - 1, q)
                scores(p, s, 1)
                if last:
                    pe.wait_ge(s_gd, 6 * PAIRS)
                    pe.wait_ge(s_ga, 4 * PAIRS)
                    pe.wait_ge(s_cv, CONV_STEPS)
                    pe.wait_ge(s_sc, 3 * KC)
                    conv_sums(1, lambda c: aT[:, c])
                else:
                    gen_kv(p + 1, q)
                turn(p, s, 0)
                if not last:
                    gen_q(p + 1, q, 1, n)
                    gen_lat(p + 1, q)

            gen_q(0, 0, 0, 1)
            gen_kv(0, 0)
            gen_q(0, 0, 1, 1)
            gen_lat(0, 0)
            pair(0, 0, 1, first=True)
            pair(1, 1, 2)
            with pe.Fori(1, PAIRS // 2 - 1) as i:
                pair(2 * i, 0, i + 1)
                pair(2 * i + 1, 1, i + 2)
            pair(PAIRS - 2, 0, PAIRS // 2)
            pair(PAIRS - 1, 1, PAIRS // 2, last=True)
            turn(PAIRS - 1, 1, 1)
            pe.wait_ge(s_ln, 1)
            pe.wait_ge(s_sqc, KC)
            conv_sums(2, sqc)
            values(PAIRS - 1, 1)

            pe.wait_ge(s_mx, 4 * HEADS)
            mm(ps[0:32, 2, 0:P], con[64:128, CSEL:CSEL + 32], qrr[64:128].rearrange("p b h -> p (b h)"),
               start=True, stop=True)
            for c in range(KKV):
                x = tr(ps[0:NS, 3, c * P:(c + 1) * P], hT[:, B_CKV + c, NPR:T], ident)
            x.then_inc(s_qs, 1)
            pe.wait_ge(s_qc, 3)
            pe.wait_ge(s_ln, LN_STEPS)
            pe.wait_ge(s_sqc, 2 * KC + 1)
            pe.wait_ge(s_ot, PAIRS)

            def unit(r, jj, u, h):
                s, slot = jj % 2, u % 2
                if h == 1:
                    pass
                elif u == 0:
                    pe.wait_ge(s_er[s], 32 * r + 16 * (jj // 2 + 1))
                    pe.wait_ge(s_da, 1 + 8 * r + 2 * jj)
                elif u == 1:
                    pe.wait_ge(s_dd, 1 + 4 * r + jj)
                else:
                    pe.wait_ge(s_da, 1 + 8 * r + 2 * jj + 1)
                w0, n = ((0, KD), (KD, KC), (KD + KC, KD))[u]
                for k in range(n):
                    mov = aT[:, k] if u == 1 else xT[:, k]
                    y = mm(ps[:, 2 * slot + h, 0:TH], er[:, s, w0 + k], mov[:, h * TH:(h + 1) * TH],
                           start=(k == 0), stop=(k == n - 1))
                if h == 1:
                    y.then_inc(s_d, 1)

            def k_step(r, g):
                s = g % 2
                if g == 0:
                    pe.wait_ge(s_rnd, RND * r + 8)
                pe.wait_ge(s_ske, 1 + 17 * r + max(g - 1, 0))
                pe.wait_ge(s_k[s], 16 * SPN * (8 * r + g // 2 + 1))
                pe.wait_ge(s_kp[s], 16 * (8 - SPN) * (8 * r + g // 2 + 1))
                kk = kring[0:KR, s].rearrange("p (b u c n) -> p b u c n", b=4, u=2, c=3)
                for c in range(3):
                    for bb in range(4):
                        y = mm(ps[32 * bb:32 * bb + 32, 4 + s, 0:256], qcur[:, c, bb], kk[:, bb, :, c, :],
                               start=(c == 0), stop=(c == 2))
                y.then_inc(s_sk, 1)

            def k_new(r):
                pe.wait_ge(s_ske, 1 + 17 * r + 15)
                for bb in range(4):
                    for c in range(3):
                        y = mm(ps[32 * bb:32 * bb + 32, 4, 0:1], qcur[:, c, bb], knew[:, c, bb:bb + 1],
                               start=(c == 0), stop=(c == 2))
                y.then_inc(s_sk, 1)

            def v_new(r):
                pe.wait_ge(s_rnd, RND * r + 15)
                pe.wait_ge(s_pte, 1 + 18 * r)
                tr(ps[0:NS, 6, 0:P], pnm[:, :], ident).then_inc(s_pt, 1)
                pe.wait_ge(s_pte, 1 + 18 * r + 1)
                pe.wait_ge(s_on, 1 + r)
                pe.sem_inc(s_own, 1)
                for bb in range(4):
                    y = mm(ps[32 * bb:32 * bb + 32, 7, 0:KVL], pnT[:, 32 * bb:32 * bb + 32], ckvs[:, :],
                           start=True, stop=False)
                y.then_inc(s_ov, 1)

            def v_turn(r, g):
                s = g % 2
                pe.wait_ge(s_pcx, 5 * r + 2 + g // 4)
                if g == 0:
                    pe.wait_ge(s_ske, 1 + 17 * r + 17)
                elif g >= 2:
                    pe.wait_ge(s_pte, 1 + 18 * r + g)
                for u in range(2):
                    y = tr(ps[:, 4 + s, u * P:(u + 1) * P], S[:, g * 256 + u * P:g * 256 + (u + 1) * P], ident)
                y.then_inc(s_pt, 1)

            def v_step(r, g):
                s = g % 2
                if g < 15:
                    v_turn(r, g + 1)
                pe.wait_ge(s_pte, 1 + 18 * r + g + 2)
                j, n = g % 3, len(range(g % 3, 16, 3)) * r + g // 3 + 1
                pe.wait_ge(s_v[j], 16 * SPN * n)
                pe.wait_ge(s_vp[j], 16 * (8 - SPN) * n)
                kk = vring[:, j].rearrange("p (b u n) -> p b u n", b=4, u=2)
                for u in range(2):
                    for bb in range(4):
                        y = mm(ps[32 * bb:32 * bb + 32, 7, 0:KVL], pts[:, s, u * P + 32 * bb:u * P + 32 * bb + 32],
                               kk[:, bb, u], start=False, stop=(g == 15 and u == 1))
                y.then_inc(s_ov, 1)

            def o_turn(r):
                pe.wait_ge(s_on, 1 + r + 1)
                for c in range(KKV):
                    y = tr(ps[:, 6, c * P:(c + 1) * P], olat[:, c * P:(c + 1) * P], ident)
                y.then_inc(s_pt, 1)

            def round_(r):
                for half in range(2):
                    for q in range(12):
                        unit(r, 2 * half + q // 6, q // 2 % 3, q % 2)
                        lo, hi = (16 * q) // 12, (16 * (q + 1)) // 12
                        for g in range(lo, hi):
                            if half == 0:
                                k_step(r, g)
                            else:
                                if g == 0:
                                    v_new(r)
                                    v_turn(r, 0)
                                v_step(r, g)
                    if half == 0:
                        k_new(r)
                o_turn(r)

            with pe.Fori(0, 2) as r:
                round_(r)

            pe.wait_ge(s_wuv, 16)
            pe.wait_ge(s_pte, 1 + 36)
            for hd in range(HEADS):
                x = hd % 2
                for c in range(KKV):
                    y = mm(ps[64 * x:64 * x + 64, 4, (hd // 2) * NS:(hd // 2 + 1) * NS],
                           wuv[:, c, hd * VH:(hd + 1) * VH],
                           olT[:, c].rearrange("p r (b h) -> p (r b) h", h=32)[:, :, hd],
                           start=(c == 0), stop=(c == KKV - 1))
            y.then_inc(s_os, 1)

            pe.wait_ge(s_ose, 1)
            pe.wait_ge(s_ot, PAIRS)

            def b_block(j, s, n):
                pe.wait_ge(s_wo[s], 16 * n)
                if isinstance(j, int) and j < 2:
                    pe.wait_ge(s_da, 1 + 16)
                    pe.wait_ge(s_dd, 1 + 8)
                else:
                    pe.wait_ge(s_bt, j - 1)
                for k in range(KD):
                    for h in range(2):
                        y = mm(ps[:, 2 * s + h, 0:TH], wo[:, s, k], oT[:, k, h * TH:(h + 1) * TH],
                               start=(k == 0), stop=(k == KD - 1))
                y.then_inc(s_b, 1)

            for s in range(2):
                b_block(s, s, 1)
            with pe.Fori(1, KD // 2) as i:
                for s in range(2):
                    b_block(2 * i + s, s, i + 1)

            def turn_x1(t):
                n = ROWS[t]
                pe.wait_ge(s_fd, FD * (t + 1))
                if t >= 1:
                    pe.wait_ge(s_fe, 2 * t)
                for k in range(KD):
                    y = tr(ps[:, 4 + k // 4, (k % 4) * P:(k % 4) * P + n], x1[0:n, t, k * P:(k + 1) * P], ident[0:n, 0:n])
                y.then_inc(s_fx, 1)

            def logits_x1(t):
                n = ROWS[t]
                pe.wait_ge(s_fe, 2 * (t + 1))
                if t >= 1:
                    pe.wait_ge(s_r, 2 * t)
                for k in range(KD):
                    y = mm(ps[0:n, 6, 0:36], x1T[:, k, 0:n], rw[:, k], start=(k == 0), stop=(k == KD - 1))
                y.then_inc(s_fl, 1)

            pe.wait_ge(s_wb, 128)
            pe.wait_ge(s_mt, KD)
            for t in range(TILES):
                n, s = ROWS[t], t % 2
                if t >= 2:
                    pe.wait_ge(s_fd, FD * (t - 2) + 1)
                if t < TILES - 1:
                    for k in range(KD):
                        for h in range(2):
                            y = mm(ps[0:n, 2 * s + h, :], mixT[:, k, t * P:t * P + n],
                                   wbig[:, k, h * 512:(h + 1) * 512], start=(k == 0), stop=(k == KD - 1))
                    y.then_inc(s_f, 1)
                else:
                    narrow(0, lambda k: mixT[:, k, T - 32:T], wbig).then_inc(s_fp, 1)
                if t >= 2:
                    logits_x1(t - 2)
                if t == TILES - 1:
                    pe.wait_ge(s_fc, 1)
                    pe.wait_ge(s_fd, FD * (t - 1) + 1)
                    narrow_sum(2, parts, 0).then_inc(s_f, 1)
                if t >= 1:
                    turn_x1(t - 1)
            logits_x1(TILES - 2)
            turn_x1(TILES - 1)
            logits_x1(TILES - 1)
            pe.wait_ge(s_r, R_RANK)
            flat = ohs[:].rearrange("p t e -> p (t e)")
            mm(ps[:, 7, 0:TILES * 32], utri, flat, start=True, stop=False)
            mm(ps[:, 7, 0:TILES * 32], ones, pf[:, 0:TILES].rearrange("p t e -> p (t e)"), start=False, stop=True)
            mm(ps[:, 7, 256:288], ones, pf[:, TILES], start=True, stop=True).then_inc(s_rp, 1)
            pe.wait_ge(s_tl, 16)
            tr(ps[:, 6, 0:SLOTS // P], tokrow[:, :], ident[0:SLOTS // P, 0:SLOTS // P]).then_inc(s_rp, 1)

            def experts(m, p, xslot, n):
                w = wx[xslot]
                pe.wait_ge(m.xg[xslot], 16 * n)
                if not (isinstance(p, int) and p == 0):
                    pe.wait_ge(m.xa, p)
                    pe.wait_ge(m.xd, p)
                for k in range(KD):
                    y = tr(ps[:, k // 4, (k % 4) * P:(k % 4 + 1) * P], xg[:, xslot, k * P:(k + 1) * P], ident)
                y.then_inc(m.xt, 1)
                pe.wait_ge(m.xa, p + 1)
                pe.wait_ge(m.xd, p + 1)
                pe.wait_ge(s_wx[xslot][0], 16 * n)
                pe.wait_ge(s_wx[xslot][1], 16 * n)
                for k in range(KD):
                    for x in range(2):
                        y = mm(ps[64 * x:64 * x + 64, 2, :], xgT[:, k, 64 * x:64 * x + 64],
                               w[:, x, k * 512:(k + 1) * 512], start=(k == 0), stop=(k == KD - 1))
                y.then_inc(m.h, 1)
                pe.wait_ge(m.hs, p + 1)
                for c in range(2):
                    y = tr(ps[:, 4, c * P:(c + 1) * P], hs[:, c * P:(c + 1) * P], ident)
                y.then_inc(m.ht, 1)
                pe.wait_ge(m.he, p + 1)
                if not (isinstance(p, int) and p == 0):
                    pe.wait_ge(m.ya, p)
                    pe.wait_ge(m.yd, p)
                pe.wait_ge(s_wd[xslot][0], 16 * n)
                pe.wait_ge(s_wd[xslot][1], 16 * n)
                for c in range(2):
                    for h in range(2):
                        for x in range(2):
                            o0 = EW1 + c * D + h * 512
                            y = mm(ps[64 * x:64 * x + 64, 6 + h, :], htT[:, c, 64 * x:64 * x + 64],
                                   w[:, x, o0:o0 + 512], start=(c == 0), stop=(c == 1))
                y.then_inc(m.y, 1)

            pe.wait_ge(s_r, R_STEPS)
            for s in range(2):
                experts(moe, s, s, 1)
            with pe.Fori(1, EPAIRS // 2) as i:
                for s in range(2):
                    experts(moe, 2 * i + s, s, i + 1)
            blocks = pe.value_load(ovi[0:1, 16:17], min_val=0, max_val=OVB)
            overflow(pe, blocks, lambda p, s, n: experts(moe, p, s, n + 1))
            pe.wait_ge(s_ovr, 1)

            pe.wait_ge(s_plw, 64)
            pe.wait_ge(s_plg, 16)
            for t in range(TILES):
                n, b = ROWS[t], 2 + 4 * (t % 2)
                if t >= 2:
                    pe.wait_ge(s_hb, HB_STEPS * (t - 2) + 1)
                for k in range(2):
                    for h in range(2):
                        mm(ps[0:n, b + h, :], plT[:, k, t * P:t * P + n], wpp[:, k, h * 512:(h + 1) * 512],
                           start=(k == 0), stop=(k == 1))
                pe.wait_ge(s_hf, HF_STEPS * (t + 1))
                if t >= 1:
                    pe.wait_ge(s_hc, 2 * t)
                for k in range(KD):
                    y = tr(ps[:, 4 + k // 4, (k % 4) * P:(k % 4) * P + n], fb[0:n, FX[t % 2], k * P:(k + 1) * P],
                           ident[0:n, 0:n])
                y.then_inc(s_h, 1)
                pe.wait_ge(s_hc, 2 * (t + 1))
                if t >= 1:
                    pe.wait_ge(s_hg, t)
                if t < TILES - 1:
                    for k in range(KD):
                        for h in range(2):
                            y = mm(ps[0:n, h, :], fbT[:, k, 0:n], wbig[:, k, h * 512:(h + 1) * 512],
                                   start=(k == 0), stop=(k == KD - 1))
                    y.then_inc(s_h, 1)
                else:
                    narrow(0, lambda k: fbT[:, k, 0:32], wbig).then_inc(s_fp, 1)
                    pe.wait_ge(s_fc, 2)
                    narrow_sum(4, fb[:, 11], 1).then_inc(s_h, 1)

        @block.scalar
        def _(act):
            av = nc.scalar.activation
            for b in range(2):
                act.wait_ge(s_ha, b + 1)
                av(hTh[:, B_CA + b], ps[:, 2 * b:2 * b + 2, 0:TH], ACT.Copy).then_inc(s_ht, 1)
            with act.Fori(1, NCV // 2) as i:
                for s in range(2):
                    act.wait_ge(s_ha, 2 * i + s + 1)
                    av(hTh[:, bass.ds(B_CA + 2 * i + s, 1)].rearrange("p a h t -> p (a h) t"),
                       ps[:, 2 * s:2 * s + 2, 0:TH], ACT.Copy).then_inc(s_ht, 1)
            act.wait_ge(s_ht, NCV)
            for c in range(KC):
                av(hT[:, B_CB + c], hT[:, B_CB + c], ACT.Sigmoid).then_inc(s_u, 1)
            def latent(b):
                act.wait_ge(s_ha, NCV + b + 1)
                av(hTh[:, b], ps[:, 2 * (b % 2):2 * (b % 2) + 2, 0:TH], ACT.Copy).then_inc(s_ht, 1)

            for b in range(KKV + 2):
                latent(b)
            act.wait_ge(s_ht, NCV + B_KR + 1)
            av(tmp[64:128, 0], hT[0:64, B_KR], ACT.Copy).then_inc(s_kro, 1)
            act.wait_ge(s_ini, N_INI)
            act.wait_ge(s_ss, 1)
            av(tmph[:, 1], ps[:, 4:6, 0:TH], ACT.Sqrt, bias=eps[:, 0:1], scale=1.0 / KVL).then_inc(s_rt, 1)
            for b in range(KKV + 2, NA - NCV):
                latent(b)
            act.wait_ge(s_ss, 2)
            av(tmph[:, 2], ps[:, 6:8, 0:TH], ACT.Sqrt, bias=eps[:, 0:1], scale=1.0 / QL).then_inc(s_rt, 1)

            def out_q(p, s, x):
                act.wait_ge(s_g, 4 * p + 1 + 2 * x)
                av(qTh[0:64, s, x], ps[0:64, 0:2, 0:TH], ACT.Copy).then_inc(s_ga, 1)

            def out_k(p, s):
                act.wait_ge(s_g, 4 * p + 2)
                for x in range(2):
                    av(kT[0:64, s, x], ps[64 * x:64 * x + 64, 0, :], ACT.Copy).then_inc(s_ga, 1)

            def soft(p, x):
                hh = 2 * p + x
                for n, i in enumerate((0, 2, 1, 3)):
                    act.wait_ge(s_mx, 4 * hh + n + 1)
                    nc.scalar.mul(nb[:, x, i:i + 1], mx[:, x, i:i + 1], -SCALE).then_inc(s_nb, 1)
                    act.wait_ge(s_nb, 4 * hh + n + 1)
                    q = prob[:, x, POFF[i]:POFF[i] + (i + 1) * P]
                    av(q, q, ACT.Exp, bias=nb[:, x, i:i + 1], scale=SCALE, accum_out=rs[:, x, i:i + 1]).then_inc(s_ex, 1)

            def out_p(p, x):
                hh = 2 * p + x
                if not (isinstance(p, int) and p == 0):
                    act.wait_ge(s_o, p)
                for n, (bank, i) in enumerate(((7, 1), (6, 3))):
                    act.wait_ge(s_tp, 3 * hh + n + 2)
                    av(pT[:, x, 0:i + 1, i * P:(i + 1) * P], ps[:, bank, 0:(i + 1) * P].rearrange("p (j q) -> p j q", q=P),
                       ACT.Copy).then_inc(s_ta, 1)

            def out_o(p):
                act.wait_ge(s_o, p + 1)
                dst = oT[:, p, 0:NPR] if isinstance(p, int) else \
                    oT[:, bass.ds(p, 1), 0:NPR].rearrange("p a t -> p (a t)")
                av(dst, ps[:, 7, :], ACT.Copy).then_inc(s_ot, 1)

            def pair(p, s, first=False, last=False):
                q = 1 - s
                if last:
                    act.wait_ge(s_g, 4 * PAIRS)
                    act.dma_start(er[:, 0], a["wgate"][0]).then_inc(s_er[0], 16)
                if not first:
                    out_p(p - 1, 1)
                soft(p, 0)
                if not last:
                    out_q(p + 1, q, 0)
                if not first:
                    out_o(p - 1)
                if not last:
                    out_k(p + 1, q)
                soft(p, 1)
                if last:
                    act.wait_ge(s_s, 3 * HEADS)
                    act.dma_start(er[:, 1], a["wgate"][1]).then_inc(s_er[1], 16)
                    for c in range(KC):
                        act.wait_ge(s_ln, 2 + c)
                        av(sqc(c), aT[:, c], ACT.Square).then_inc(s_sqc, 1)
                out_p(p, 0)
                if not last:
                    out_q(p + 1, q, 1)

            out_q(0, 0, 0)
            out_k(0, 0)
            out_q(0, 0, 1)
            pair(0, 0, first=True)
            pair(1, 1)
            with act.Fori(1, PAIRS // 2 - 1) as i:
                pair(2 * i, 0)
                pair(2 * i + 1, 1)
            pair(PAIRS - 2, 0)
            pair(PAIRS - 1, 1, last=True)
            out_p(PAIRS - 1, 1)
            act.wait_ge(s_cm, 2)
            av(tmph[:, 1], ps[:, 0:2, 0:TH], ACT.Sqrt, bias=eps[:, 1:2], scale=1.0 / CC).then_inc(s_sqc, 1)
            out_o(PAIRS - 1)
            for c in range(KC):
                act.wait_ge(s_ln, 7 + c)
                av(aT[:, c], aT[:, c], ACT.Silu, bias=vec[:, VLB + c:VLB + c + 1],
                   scale=vec[:, VLG + c:VLG + c + 1]).then_inc(s_sqc, 1)

            act.sem_inc(s_da, 1)
            act.sem_inc(s_ske, 1)
            act.wait_ge(s_o, PAIRS)
            act.dma_start(wuv[:], a["wuv"]).then_inc(s_wuv, 16)

            def gate(r, jj, u):
                act.wait_ge(s_d, 4 + 12 * r + 3 * jj + u + 1)
                if u == 0:
                    act.wait_ge(s_dd, 1 + 4 * r + jj)
                    av(sgh, ps[:, 0:2, 0:TH], ACT.Sigmoid).then_inc(s_da, 1)
                else:
                    av(sigBh[:, bass.ds(4 * r + jj, 1)].rearrange("p a h t -> p (a h) t"), ps[:, 0:2, 0:TH],
                       ACT.Sigmoid).then_inc(s_da, 1)

            def next_block(s, j):
                act.dma_start(er[:, s], a["wgate"][j].rearrange("a p k m -> (a p) k m")
                              ).then_inc(s_er[s], 16)

            with act.Fori(0, 2) as r:
                for half in range(2):
                    if half == 1:
                        act.wait_ge(s_rnd, RND * r + 14)
                        av(rsum[:, 4:5], S[:, 4096:4097], ACT.Exp, bias=sm[:, 1:2], scale=SCALE).then_inc(s_pcx, 1)
                        for c in range(4):
                            w = S[:, c * 1024:(c + 1) * 1024]
                            av(w, w, ACT.Exp, bias=sm[:, 1:2], scale=SCALE, accum_out=rsum[:, c:c + 1]).then_inc(s_pcx, 1)
                    for q in range(12):
                        if q % 2 == 1 and q // 2 % 3 != 1:
                            gate(r, 2 * half + q // 6, q // 2 % 3)
                        if q % 6 == 5:
                            s = q // 6
                            if half == 0:
                                next_block(s, bass.ds(4 * r + 2 + s, 1))
                            else:
                                with act.If(r < 1):
                                    next_block(s, slice(4 + s, 5 + s))
                        if half == 0:
                            for g in range((16 * q) // 12, (16 * (q + 1)) // 12):
                                act.wait_ge(s_sk, 17 * r + g + 1)
                                av(S[:, g * 256:(g + 1) * 256], ps[:, 4 + g % 2, 0:256], ACT.Copy).then_inc(s_ske, 1)
                    if half == 0:
                        act.wait_ge(s_sk, 17 * r + 17)
                        av(S[:, 4096:4097], ps[:, 4, 0:1], ACT.Copy).then_inc(s_ske, 1)
            act.wait_ge(s_os, 1)
            av(oT[:, :, NPR:T], ps[:, 4, 0:PAIRS * NS].rearrange("p (k b) -> p k b", k=PAIRS), ACT.Copy).then_inc(s_ose, 1)

            def x1_out(t):
                n = ROWS[t]
                act.wait_ge(s_fx, t + 1)
                if t >= 1:
                    act.wait_ge(s_fl, t)
                for h in range(2):
                    av(x1T[:, 4 * h:4 * h + 4, 0:n], ps[:, 4 + h, :].rearrange("p (k n) -> p k n", k=4)[:, :, 0:n],
                       ACT.Copy).then_inc(s_fe, 1)

            for t in range(TILES):
                act.wait_ge(s_fd, FD * t + 4)
                av(rstd[0:ROWS[t], 0:1], mv[0:ROWS[t], 1:2], ACT.Sqrt, bias=eps[0:ROWS[t], 1:2]).then_inc(s_fa, 1)
                if t >= 1:
                    x1_out(t - 1)
            x1_out(TILES - 1)
            act.wait_ge(s_r, R_EXP)
            av(gg[:], gx[:], ACT.Exp).then_inc(s_ra, 1)
            act.wait_ge(s_r, R_EXP2)
            av(gf, gf, ACT.Exp).then_inc(s_ra, 1)

            def experts(m, p, xs, n):
                act.wait_ge(m.xt, p + 1)
                av(xgT[:, 0:4], ps[:, 0, :].rearrange("p (k n) -> p k n", k=4), ACT.Copy).then_inc(m.xa, 1)
                act.wait_ge(m.h, p + 1)
                av(sgE, ps[:, 2, 0:DE], ACT.Silu).then_inc(m.sg, 1)
                act.wait_ge(m.y, p + 1)
                if not (isinstance(n, int) and n == 0):
                    act.wait_ge(m.yw[xs], 16 * n)
                av(yb[:, xs, 0:512], ps[:, 6, :], ACT.Copy).then_inc(m.ya, 1)
                act.wait_ge(m.ya, p + 1)
                act.wait_ge(m.yd, p + 1)
                rows = ybd[p * P:(p + 1) * P] if isinstance(p, int) else ybd[bass.ds(p * P, P)]
                act.dma_start(rows, yb[:, xs]).then_inc(m.yw[xs], 16)

            for s in range(2):
                experts(moe, s, s, 0)
            with act.Fori(1, EPAIRS // 2) as i:
                for s in range(2):
                    experts(moe, 2 * i + s, s, i)
            act.wait_ge(s_r, R_STEPS)
            act.wait_ge(s_yz, 16)
            blocks = act.value_load(ovi[0:1, 16:17], min_val=0, max_val=OVB)

            def extra(p, s, n):
                experts(moe, p, s, n)
                act.wait_ge(moe.yw[s], 16 * n + 16)
                act.sem_inc(s_own, 1)

            overflow(act, blocks, extra)
            act.wait_ge(moe.yw[0], 16 * EPAIRS // 2)
            act.wait_ge(moe.yw[1], 16 * EPAIRS // 2)
            act.sem_inc(s_ovr, 1)

            def front(t):
                n = ROWS[t]
                act.wait_ge(s_hf, HF_STEPS * t + 6)
                av(rstd[0:n, 0:1], mv[0:n, 1:2], ACT.Sqrt, bias=eps[0:n, 1:2]).then_inc(s_hr, 1)

            def turned(t):
                n = ROWS[t]
                act.wait_ge(s_h, 2 * t + 1)
                for h in range(2):
                    av(fbT[:, 4 * h:4 * h + 4, 0:n], ps[:, 4 + h, :].rearrange("p (k n) -> p k n", k=4)[:, :, 0:n],
                       ACT.Copy).then_inc(s_hc, 1)

            front(0)
            turned(0)
            for t in range(TILES):
                n = ROWS[t]
                if t + 1 < TILES:
                    front(t + 1)
                act.wait_ge(s_h, 2 * t + 2)
                if t >= 1:
                    act.wait_ge(s_hb, HB_STEPS * (t - 1) + 3)
                b = 4 if t == TILES - 1 else 0
                av(fb[0:n, 5], ps[0:n, b:b + 2, :].rearrange("p h n -> p (h n)"), ACT.Sigmoid).then_inc(s_hg, 1)
                if t + 1 < TILES:
                    turned(t + 1)
                act.wait_ge(s_hb, HB_STEPS * t + 1)
                av(fb[0:n, 8], fb[0:n, 5], ACT.Square, accum_out=rms[0:n, 0:1]).then_inc(s_hs, 1)
                act.wait_ge(s_hs, 2 * t + 1)
                av(rms[0:n, 1:2], rms[0:n, 0:1], ACT.Sqrt, bias=eps[0:n, 0:1], scale=1.0 / D).then_inc(s_hs, 1)

        @block.vector
        def _(dve):
            v = nc.vector
            v.memset(zeros, 0.0).then_inc(s_ini, 1)
            v.memset(eps[:, 0:1], RMS_EPS).then_inc(s_ini, 1)
            v.memset(eps[:, 1:2], LN_EPS).then_inc(s_ini, 1)
            v.memset(ext[:, :, 0:CW - 1], 0.0).then_inc(s_ini, 1)
            v.memset(qlat, 0.0).then_inc(s_ini, 1)
            v.memset(qrs, 0.0).then_inc(s_ini, 1)
            def glu():
                for c in range(KC):
                    dve.wait_ge(s_u, c + 1)
                    v.tensor_tensor(ext[:, c, CW - 1:CW - 1 + NPR], hT[:, B_CA + c, 0:NPR], hT[:, B_CB + c, 0:NPR],
                                    ALU.mult).then_inc(s_gl, 1)
                    v.tensor_tensor(exs[:, c, :, CW - 1], hT[:, B_CA + c, NPR:T], hT[:, B_CB + c, NPR:T],
                                    ALU.mult).then_inc(s_gl, 1)

            def conv_s():
                e3 = exw.rearrange("p (b w) -> p b w", b=NS)
                for c in range(KC):
                    w = vec[:, VDW + c * CW:VDW + (c + 1) * CW].unsqueeze(1).to_broadcast([P, NS, CW])
                    dve.wait_ge(s_gl, 2 * c + 2)
                    v.tensor_tensor(e3, exs[:, c], w, ALU.mult).then_inc(s_sc, 1)
                    dve.wait_ge(s_sc, 3 * c + 1)
                    v.tensor_reduce(aT[:, c, NPR:T], e3, AX.X, ALU.add).then_inc(s_sc, 1)
                    dve.wait_ge(s_sc, 3 * c + 2)
                    v.tensor_scalar(aT[:, c, NPR:T], aT[:, c, NPR:T], vec[:, VBD + c:VBD + c + 1], None,
                                    ALU.add).then_inc(s_sc, 1)

            def tap(w):
                at_w = (lambda off, ln: slice(off + w, off + w + ln)) if isinstance(w, int) else \
                    (lambda off, ln: bass.ds(w + off, ln))
                for c in range(KC):
                    win, wt = ext[:, c, at_w(0, NPR)], vec[:, at_w(VDW + c * CW, 1)]
                    if isinstance(w, int) and w == 0:
                        dve.wait_ge(s_gl, 2 * c + 1)
                        y = v.tensor_scalar(aT[:, c, 0:NPR], win, wt, vec[:, VBD + c:VBD + c + 1], ALU.mult, ALU.add)
                    else:
                        dve.wait_ge(s_cv, KC * w - KC + c + 1)
                        y = v.scalar_tensor_tensor(out=aT[:, c, 0:NPR], in0=win, scalar=wt, in1=aT[:, c, 0:NPR],
                                                   op0=ALU.mult, op1=ALU.add)
                    y.then_inc(s_cv, 1)

            dve.wait_ge(s_con, 112)
            dve.wait_ge(s_ini, N_INI)
            glu()
            tap(0)
            conv_s()
            dve.wait_ge(s_sc, 3 * KC)
            dve.wait_ge(s_ht, NCV + KKV)
            h = hT[:, B_CKV:B_CKV + KKV]
            v.tensor_tensor(sq[:, 0:KKV], h, h, ALU.mult).then_inc(s_sq, 1)
            with dve.Fori(1, PRE) as i:
                tap(i)
            dve.wait_ge(s_kro, 1)
            kr = hT[64:128, B_KR]
            v.tensor_tensor(tmp[64:128, 0], tmp[64:128, 0], rsn[64:128], ALU.mult).then_inc(s_nrm, 1)
            v.tensor_tensor(kr, kr, rc[64:128], ALU.mult).then_inc(s_nrm, 1)
            dve.wait_ge(s_nrm, 2)
            v.tensor_tensor(kr, kr, tmp[64:128, 0], ALU.add).then_inc(s_nrm, 1)
            dve.wait_ge(s_rt, 1)
            v.reciprocal(tmp[:, 1], tmp[:, 1]).then_inc(s_nrm, 1)
            dve.wait_ge(s_nrm, 4)
            for c in range(KKV):
                h = hT[:, B_CKV + c]
                v.scalar_tensor_tensor(out=h, in0=h, scalar=vec[:, VKG + c:VKG + c + 1], in1=tmp[:, 1], op0=ALU.mult,
                                       op1=ALU.mult).then_inc(s_nrm, 1)
            dve.wait_ge(s_ht, NA)
            h = hT[:, B_CQ:B_CQ + KQ]
            v.tensor_tensor(sq[:, KKV:KKV + KQ], h, h, ALU.mult).then_inc(s_sq, 1)
            dve.wait_ge(s_rt, 2)
            v.reciprocal(tmp[:, 2], tmp[:, 2]).then_inc(s_nrm, 1)
            dve.wait_ge(s_nrm, 7)
            for c in range(KQ):
                h = hT[:, B_CQ + c]
                v.scalar_tensor_tensor(out=h, in0=h, scalar=vec[:, VQG + c:VQG + c + 1], in1=tmp[:, 2], op0=ALU.mult,
                                       op1=ALU.mult).then_inc(s_nrm, 1)

            def out_q(p, s, x):
                dve.wait_ge(s_g, 4 * p + 1 + 2 * x)
                v.tensor_tensor(qTh[64:128, s, x], ps[64:128, 0:2, 0:TH],
                                rq[64:128].rearrange("p (h t) -> p h t", h=2), ALU.mult).then_inc(s_gd, 1)
                dve.wait_ge(s_gd, 6 * p + 1 + 3 * x)
                dst = qrr[64:128, :, 2 * p + x] if isinstance(p, int) else \
                    qrr[64:128, :, bass.ds(2 * p + x, 1)].rearrange("p b a -> p (b a)")
                v.tensor_copy(dst, qT[64:128, s, x, NPR:T]).then_inc(s_gd, 1)

            def out_v(p, s):
                dve.wait_ge(s_g, 4 * p + 2)
                v.tensor_copy(vf[:, s], ps[:, 1, :]).then_inc(s_gd, 1)

            def out_lat(p):
                dve.wait_ge(s_g, 4 * p + 4)
                for x in range(2):
                    sl = slice(2 * p + x, 2 * p + x + 1) if isinstance(p, int) else bass.ds(2 * p + x, 1)
                    y = v.tensor_copy(qlat[:, :, :, sl].rearrange("p c b a -> p c (b a)"),
                                      ps[:, 0, 16 * x:16 * x + 16].rearrange("p (c b) -> p c b", b=NS))
                y.then_inc(s_gd, 1)

            def masks(p, x):
                hh = 2 * p + x
                if not (isinstance(p, int) and p == 0):
                    dve.wait_ge(s_tp, 3 * (hh - 1))
                for n, i in enumerate((0, 2, 1, 3)):
                    dve.wait_ge(s_s, 3 * hh + (1, 1, 2, 3)[n])
                    dve.sem_inc(s_own, 1)
                    bank, c0 = (2, 3, 2, 4)[i], P if i == 2 else 0
                    w = (i + 1) * P
                    v.tensor_tensor_reduce(prob[:, x, POFF[i]:POFF[i] + w], ps[:, bank, c0:c0 + w], maskw[:, 512 - w:512],
                                           1.0, -BIG, ALU.add, ALU.max, mx[:, x, i:i + 1]).then_inc(s_mx, 1)

            def scale(p, x):
                hh = 2 * p + x
                for n, i in enumerate((0, 2, 1, 3)):
                    dve.wait_ge(s_ex, 4 * hh + n + 1)
                    v.reciprocal(rr[:, x, i:i + 1], rs[:, x, i:i + 1]).then_inc(s_rc, 1)
                    dve.wait_ge(s_rc, 4 * hh + n + 1)
                    q = prob[:, x, POFF[i]:POFF[i] + (i + 1) * P]
                    v.tensor_scalar(q, q, rr[:, x, i:i + 1], None, ALU.mult).then_inc(s_pr, 1)

            def out_p(p, x):
                hh = 2 * p + x
                if not (isinstance(p, int) and p == 0):
                    dve.wait_ge(s_o, p)
                dve.wait_ge(s_tp, 3 * hh + 1)
                for i in (0, 2):
                    c0 = P if i == 2 else 0
                    v.tensor_copy(pT[:, x, 0:i + 1, i * P:(i + 1) * P],
                                  ps[:, 5, c0:c0 + (i + 1) * P].rearrange("p (j q) -> p j q", q=P)).then_inc(s_td, 1)

            def pair(p, s, first=False, last=False):
                q = 1 - s
                masks(p, 0)
                if not first:
                    out_p(p - 1, 1)
                if not last:
                    out_q(p + 1, q, 0)
                if not last:
                    tap(PRE + 3 * p)
                scale(p, 0)
                masks(p, 1)
                if last:
                    dve.wait_ge(s_cm, 1)
                    v.tensor_scalar(tmph[:, 0], ps[:, 0:2, 0:TH], 1.0 / CC, None, ALU.mult).then_inc(s_ln, 1)
                    dve.wait_ge(s_ln, 1)
                    for c in range(KC):
                        v.tensor_tensor(aT[:, c], aT[:, c], tmp[:, 0], ALU.subtract).then_inc(s_ln, 1)
                else:
                    out_v(p + 1, q)
                if not last:
                    tap(PRE + 3 * p + 1)
                out_p(p, 0)
                if not last:
                    out_q(p + 1, q, 1)
                if not last:
                    tap(PRE + 3 * p + 2)
                scale(p, 1)
                if not last:
                    out_lat(p + 1)

            out_q(0, 0, 0)
            out_v(0, 0)
            out_q(0, 0, 1)
            out_lat(0)
            pair(0, 0, first=True)
            pair(1, 1)
            with dve.Fori(1, PAIRS // 2 - 1) as i:
                pair(2 * i, 0)
                pair(2 * i + 1, 1)
            pair(PAIRS - 2, 0)
            pair(PAIRS - 1, 1, last=True)
            out_p(PAIRS - 1, 1)
            dve.wait_ge(s_sqc, KC + 1)
            v.reciprocal(tmp[:, 2], tmp[:, 1]).then_inc(s_ln, 1)
            dve.wait_ge(s_ln, 6)
            for c in range(KC):
                v.tensor_tensor(aT[:, c], aT[:, c], tmp[:, 2], ALU.mult).then_inc(s_ln, 1)

            dve.wait_ge(s_qs, 1)
            v.tensor_copy(qrs[:, :, 0:HEADS], ps[0:32, 2, 0:P].rearrange("p (b h) -> p b h", b=NS)).then_inc(s_qc, 1)
            v.tensor_copy(ckvs, ps[0:NS, 3, 0:KVL]).then_inc(s_qc, 1)
            v.tensor_copy(krs[:], hT[64:96, B_KR, NPR:T]).then_inc(s_qc, 1)
            dve.sem_inc(s_dd, 1)
            dve.sem_inc(s_on, 1)
            dve.sem_inc(s_pte, 1)
            dve.wait_ge(s_qc, 3)
            dve.wait_ge(s_z, 16)
            dve.wait_ge(s_yz, 16)
            dve.wait_ge(s_cm, 2)

            def gated(r, jj):
                dve.wait_ge(s_d, 4 + 12 * r + 3 * jj + 2)
                dve.wait_ge(s_da, 1 + 8 * r + 2 * jj + 1)
                v.tensor_tensor(mixh[:, bass.ds(4 * r + jj, 1)].rearrange("p a h t -> p (a h) t"),
                                ps[:, 2:4, 0:TH], sgh, ALU.mult).then_inc(s_dd, 1)

            with dve.Fori(0, 2) as r:
                now, new = bass.ds(4 * r, 4), bass.ds(NPR + 4 * r, 4)
                ckv = hT[:, B_CKV:B_CKV + KKV]
                v.tensor_copy(qcur[:, 0:2], qlat[0:KR, :, now, :]).then_inc(s_rnd, 1)
                v.tensor_copy(qcur[0:32, 2], qrs[:, now, :]).then_inc(s_rnd, 1)
                v.tensor_copy(knew[:, 0:2], ckv[0:KR, :, new]).then_inc(s_rnd, 1)
                v.tensor_copy(knew[0:32, 2], krs[:, now]).then_inc(s_rnd, 1)
                for c in range(KKV):
                    v.tensor_copy(qcur[32 + 32 * c:64 + 32 * c, 2], qlat[KR:P, c, now, :]).then_inc(s_rnd, 1)
                    v.tensor_copy(knew[32 + 32 * c:64 + 32 * c, 2], ckv[KR:P, c, new]).then_inc(s_rnd, 1)
                for c in range(4):
                    dve.wait_ge(s_ske, 1 + 17 * r + (17 if c == 3 else 4 * c + 4))
                    v.tensor_reduce(smp[:, c:c + 1], S[:, c * 1024:(c + 1) * 1024 + (c == 3)], AX.X,
                                    ALU.max).then_inc(s_rnd, 1)
                    if c % 2 == 0:
                        gated(r, c // 2)
                dve.wait_ge(s_rnd, RND * r + 12)
                v.tensor_reduce(sm[:, 0:1], smp[:], AX.X, ALU.max).then_inc(s_rnd, 1)
                dve.wait_ge(s_rnd, RND * r + 13)
                v.tensor_scalar(sm[:, 1:2], sm[:, 0:1], -SCALE, None, ALU.mult).then_inc(s_rnd, 1)
                dve.wait_ge(s_pcx, 5 * r + 1)
                v.tensor_scalar(pnm[:], con[:, bass.ds(CM8 + NS * r, NS)], rsum[:, 4:5], None, ALU.mult).then_inc(s_rnd, 1)
                dve.wait_ge(s_pt, 18 * r + 1)
                v.tensor_copy(pnT, ps[0:NS, 6, 0:P]).then_inc(s_pte, 1)
                for g in range(16):
                    if g in (5, 13):
                        gated(r, 2 + (g == 13))
                    dve.wait_ge(s_pt, 18 * r + g + 2)
                    dve.wait_ge(s_ov, 2 + 17 * r + (g if g >= 2 else 0))
                    v.tensor_copy(pts[:, g % 2], ps[:, 4 + g % 2, 0:256]).then_inc(s_pte, 1)
                dve.wait_ge(s_pcx, 5 * r + 5)
                v.tensor_reduce(sm[:, 3:4], rsum[:, 0:5], AX.X, ALU.add).then_inc(s_rnd, 1)
                dve.wait_ge(s_rnd, RND * r + 16)
                v.reciprocal(sm[:, 4:5], sm[:, 3:4]).then_inc(s_rnd, 1)
                dve.wait_ge(s_rnd, RND * r + 17)
                dve.wait_ge(s_ov, 2 + 17 * r + 17)
                v.tensor_scalar(olat, ps[:, 7, 0:KVL], sm[:, 4:5], None, ALU.mult).then_inc(s_on, 1)
                dve.wait_ge(s_pt, 18 * r + 18)
                v.tensor_copy(olT[:, :, bass.ds(r, 1)].rearrange("p c a n -> p c (a n)"),
                              ps[:, 6, 0:256].rearrange("p (c n) -> p c n", c=KKV)).then_inc(s_pte, 1)

            def b_block(j, s):
                dve.wait_ge(s_b, j + 1)
                sl = slice(j, j + 1) if isinstance(j, int) else bass.ds(j, 1)
                if not (isinstance(j, int) and j == 0):
                    dve.wait_ge(s_mt, j)
                v.tensor_tensor(sgbh, ps[:, 2 * s:2 * s + 2, 0:TH],
                                sigBh[:, sl].rearrange("p a h t -> p (a h) t"), ALU.mult).then_inc(s_bt, 1)
                dve.wait_ge(s_bt, j + 1)
                m = mixT[:, sl].rearrange("p a t -> p (a t)")
                v.tensor_tensor(m, m, sgb, ALU.add).then_inc(s_mt, 1)

            for s in range(2):
                b_block(s, s)
            with dve.Fori(1, KD // 2) as i:
                for s in range(2):
                    b_block(2 * i + s, s)

            def norm(n, x, stats_sem, base, root_sem, root_n, g, b):
                for hh in range(2):
                    v.bn_stats(bst[0:n, hh], x[:, hh * 512:(hh + 1) * 512]).then_inc(stats_sem, 1)
                dve.wait_ge(stats_sem, base + 2)
                v.bn_aggr(mv[0:n], bst[0:n].rearrange("p h s -> p (h s)")).then_inc(stats_sem, 1)
                dve.wait_ge(root_sem, root_n)
                v.reciprocal(rstd[0:n, 1:2], rstd[0:n, 0:1]).then_inc(stats_sem, 1)
                dve.wait_ge(stats_sem, base + 4)
                v.tensor_scalar(x, x, mv[0:n, 0:1], rstd[0:n, 1:2], ALU.subtract, ALU.mult).then_inc(stats_sem, 1)
                dve.wait_ge(stats_sem, base + 5)
                v.tensor_tensor(x, x, g[0:n], ALU.mult).then_inc(stats_sem, 1)
                dve.wait_ge(stats_sem, base + 6)
                v.tensor_tensor(x, x, b[0:n], ALU.add).then_inc(stats_sem, 1)

            def logits(t):
                n = ROWS[t]
                dve.wait_ge(s_fl, t + 1)
                v.tensor_copy(L[0:n, t, 0:4], ps[0:n, 6, 0:4]).then_inc(s_r, 1)
                v.tensor_copy(L[0:n, t, 8:40], ps[0:n, 6, 4:36]).then_inc(s_r, 1)

            v.memset(L, 0.0).then_inc(s_ini, 1)
            dve.wait_ge(s_ini, N_INI + 1)
            v.memset(L[:, :, 4:8], -BIG).then_inc(s_ini, 1)
            v.memset(one32, 1.0).then_inc(s_ini, 1)
            v.memset(pf[:, 0], 0.0).then_inc(s_ini, 1)
            dve.wait_ge(s_ini, N_INI + 4)
            dve.wait_ge(s_wb, 128)
            for t in range(TILES):
                n = ROWS[t]
                x = x1[0:n, t]
                b = 2 * (t % 2)
                if t == TILES - 1:
                    dve.wait_ge(s_fp, 1)
                    v.tensor_copy(parts, ps[:, 0:2, :].rearrange("p h n -> p (h n)")).then_inc(s_fc, 1)
                    b = 2
                dve.wait_ge(s_f, t + 1)
                v.scalar_tensor_tensor(out=x, in0=x, scalar=ALPHA,
                                       in1=ps[0:n, b:b + 2, :].rearrange("p h n -> p (h n)"),
                                       op0=ALU.mult, op1=ALU.add).then_inc(s_fd, 1)
                dve.wait_ge(s_fd, FD * t + 1)
                norm(n, x, s_fd, FD * t + 1, s_fa, t + 1, lnr[:, 0], lnr[:, 1])
                if t >= 2:
                    logits(t - 2)
            logits(TILES - 2)
            logits(TILES - 1)

            count = [2 * TILES]

            def step(ins):
                ins.then_inc(s_r, 1)
                count[0] += 1
                dve.wait_ge(s_r, count[0])

            dve.wait_ge(s_r, count[0])

            def b3(x, n):
                return x.unsqueeze(2).to_broadcast([P, TILES, n])

            def cb(off, n):
                return con[:, off:off + n].unsqueeze(1).to_broadcast([P, TILES, n])

            for t in range(TILES):
                v.max(gv[:, t], L[:, t, 0:8])
            step(v.tensor_copy(gx, L[:, :, 0:4]))
            for t in range(TILES):
                v.max_index(gi[:, t], gv[:, t], L[:, t, 0:8])
            step(v.tensor_tensor(gx, gx, b3(gv[:, :, 0], 4), ALU.subtract))
            assert count[0] == R_EXP
            step(v.tensor_copy(gf, gi[:, :, 0]))
            step(v.tensor_tensor(ms, cb(CGID, 32), b3(gf, 32), ALU.is_equal))
            step(v.tensor_scalar(ms2, ms, -1.0, BIG, ALU.add, ALU.mult))
            step(v.tensor_tensor(ms, ms, L[:, :, 8:40], ALU.mult))
            step(v.tensor_tensor(ms, ms, ms2, ALU.add))
            for t in range(TILES):
                v.max(ev[:, t], ms[:, t])
            step(v.tensor_copy(ms2, ms))
            for t in range(TILES):
                v.max_index(ei[:, t], ev[:, t], ms2[:, t])
            step(v.tensor_tensor(gf, ev[:, :, 1], ev[:, :, 0], ALU.subtract))
            assert count[0] == R_EXP2, count
            step(v.tensor_copy(ef, ei[:, :, 0:2]))
            for k in range(2):
                step(v.tensor_tensor(oh[:, k], cb(CEID, 32), b3(ef[:, :, k], 32), ALU.is_equal))
            step(v.tensor_tensor(ohs, oh[:, 0], oh[:, 1], ALU.add))
            step(v.tensor_tensor(ohs, ohs, b3(con[:, CVAL:CVAL + TILES], 32), ALU.mult))
            for t in range(TILES):
                step(v.tensor_tensor(pf[:, t + 1], pf[:, t], ohs[:, t], ALU.add))
            assert count[0] == R_RANK, count
            dve.wait_ge(s_ra, 1)
            step(v.tensor_reduce(gv[:, :, 0], gg, AX.X, ALU.add))
            step(v.reciprocal(gv[:, :, 1], gv[:, :, 0]))
            dve.wait_ge(s_ra, 2)
            step(v.tensor_scalar(gv[:, :, 2], gf, 1.0, None, ALU.add))
            step(v.reciprocal(gv[:, :, 3], gv[:, :, 2]))
            step(v.tensor_tensor(gates[:, 0], gv[:, :, 3], gv[:, :, 1], ALU.mult))
            step(v.tensor_tensor(gates[:, 1], gates[:, 0], gf, ALU.mult))
            dve.wait_ge(s_rp, 1)
            v.tensor_copy(cnt, ps[:, 7, 256:288])
            step(v.tensor_copy(pos, ps[:, 7, 0:TILES * 32].rearrange("p (t e) -> p t e", e=32)))
            step(v.tensor_tensor(cmp8, cnt.unsqueeze(2).to_broadcast([P, 32, 8]),
                                 con[:, CTHR:CTHR + 8].unsqueeze(1).to_broadcast([P, 32, 8]), ALU.is_gt))
            step(v.tensor_reduce(nov, cmp8, AX.X, ALU.add))
            step(v.tensor_tensor_scan(oend, one32, nov, 0.0, ALU.mult, ALU.add))
            step(v.tensor_tensor(dsl, oend, nov, ALU.subtract))
            step(v.tensor_scalar(dsl, dsl, float(CAP), float(CAP * (NEXP - 1)), ALU.mult, ALU.add))
            step(v.tensor_tensor(dsl, dsl, con[:, CEB:CEB + 32], ALU.subtract))
            step(v.tensor_scalar(ms, pos, float(CAP), None, ALU.is_ge))
            step(v.tensor_tensor(ms, ms, dsl.unsqueeze(1).to_broadcast([P, TILES, 32]), ALU.mult))
            step(v.tensor_tensor(pos, pos, cb(CEB, 32), ALU.add))
            step(v.tensor_tensor(pos, pos, ms, ALU.add))
            for k in range(2):
                step(v.tensor_tensor(ms, oh[:, k], pos, ALU.mult))
                step(v.tensor_reduce(slotf[:, k], ms, AX.X, ALU.add))
            step(v.tensor_copy(slotu[:], slotf))
            assert count[0] == R_SLOT, count
            step(v.tensor_tensor(ovc, oend[0:1].unsqueeze(1).to_broadcast([1, 16, 32]),
                                 con[0:1, CBLK:CBLK + 16].unsqueeze(2).to_broadcast([1, 16, 32]), ALU.is_le))
            step(v.tensor_reduce(ovf[:, 0:16], ovc, AX.X, ALU.add))
            step(v.tensor_scalar(ovf[:, 0:16], ovf[:, 0:16], float(NEXP - 1), None, ALU.min))
            step(v.tensor_copy(ovf[:, 16:17], oend[0:1, 31:32]))
            step(v.tensor_copy(ovi[:], ovf[:]))
            dve.wait_ge(s_rp, 2)
            step(v.tensor_copy(idx[:], ps[:, 6, 0:SLOTS // P]))
            assert count[0] == R_STEPS, count

            def experts(m, p, xs, n):
                dve.wait_ge(m.xt, p + 1)
                v.tensor_copy(xgT[:, 4:8], ps[:, 1, :].rearrange("p (k n) -> p k n", k=4)).then_inc(m.xd, 1)
                dve.wait_ge(m.sg, p + 1)
                v.tensor_tensor(hs, ps[:, 2, DE:2 * DE], sgE, ALU.mult).then_inc(m.hs, 1)
                dve.wait_ge(m.ht, p + 1)
                v.tensor_copy(htT, ps[:, 4, 0:256].rearrange("p (c n) -> p c n", c=2)).then_inc(m.he, 1)
                dve.wait_ge(m.y, p + 1)
                if not (isinstance(n, int) and n == 0):
                    dve.wait_ge(m.yw[xs], 16 * n)
                v.tensor_copy(yb[:, xs, 512:1024], ps[:, 7, :]).then_inc(m.yd, 1)

            for s in range(2):
                experts(moe, s, s, 0)
            with dve.Fori(1, EPAIRS // 2) as i:
                for s in range(2):
                    experts(moe, 2 * i + s, s, i)
            blocks = dve.value_load(ovi[0:1, 16:17], min_val=0, max_val=OVB)
            overflow(dve, blocks, lambda p, s, n: experts(moe, p, s, n))

            dve.wait_ge(s_plw, 64)

            def front(t):
                n, b = ROWS[t], HF_STEPS * t
                dve.wait_ge(s_gt[t % 2][0], 16 * (t // 2 + 1))
                v.tensor_scalar(fb[0:n, t % 2], fb[0:n, t % 2], gates[0:n, 0, t:t + 1], None, ALU.mult).then_inc(s_hf, 1)
                dve.wait_ge(s_hf, b + 1)
                dve.wait_ge(s_gt[t % 2][1], 16 * (t // 2 + 1))
                v.scalar_tensor_tensor(out=fb[0:n, 11], in0=fb[0:n, 2 + t % 2], scalar=gates[0:n, 1, t:t + 1],
                                       in1=fb[0:n, t % 2], op0=ALU.mult, op1=ALU.add).then_inc(s_hf, 1)
                dve.wait_ge(s_hf, b + 2)
                x = fb[0:n, FX[t % 2]]
                v.scalar_tensor_tensor(out=x, in0=x1[0:n, t], scalar=ALPHA, in1=fb[0:n, 11], op0=ALU.mult,
                                       op1=ALU.add).then_inc(s_hf, 1)
                dve.wait_ge(s_hf, b + 3)
                norm(n, x, s_hf, b + 3, s_hr, t + 1, ln2r[:, 0], ln2r[:, 1])

            front(0)
            for t in range(TILES):
                if t + 1 < TILES:
                    front(t + 1)
                n, b = ROWS[t], HB_STEPS * t
                if t == TILES - 1:
                    dve.wait_ge(s_fp, 2)
                    v.tensor_copy(fb[:, 11], ps[:, 0:2, :].rearrange("p h n -> p (h n)")).then_inc(s_fc, 1)
                dve.wait_ge(s_hg, t + 1)
                p0 = 2 + 4 * (t % 2)
                v.tensor_tensor(fb[0:n, 5], fb[0:n, 5], ps[0:n, p0:p0 + 2, :].rearrange("p h n -> p (h n)"),
                                ALU.mult).then_inc(s_hb, 1)
                dve.wait_ge(s_hs, 2 * t + 2)
                v.reciprocal(rms[0:n, 1:2], rms[0:n, 1:2]).then_inc(s_hb, 1)
                dve.wait_ge(s_hb, b + 2)
                if t >= 2:
                    dve.wait_ge(s_yo[t % 2], 16 * (t // 2))
                y = fb[0:n, 6 + t % 2]
                v.scalar_tensor_tensor(out=y, in0=fb[0:n, 5], scalar=rms[0:n, 1:2], in1=pgr[0:n], op0=ALU.mult,
                                       op1=ALU.mult).then_inc(s_hb, 1)
                dve.wait_ge(s_hb, b + 3)
                v.tensor_tensor(y, y, fb[0:n, FX[t % 2]], ALU.add).then_inc(s_hb, 1)

        @block.gpsimd
        def _(pool):
            gp = nc.gpsimd
            pool.wait_ge(s_nrm, 3)
            for s in range(2):
                for x in range(2):
                    gp.tensor_copy(kT[64:128, s, x], hT[64:128, B_KR, 0:NPR]).then_inc(s_kf, 1)
            numbers = [pool.alloc_register(f"pool_page{j}") for j in range(8 - SPN)]

            def step_pages(r, g):
                pool.load(numbers, pages[0:1, bass.ds(8 * (16 * r + g) + SPN, 8 - SPN)])

            def k_pages(r, g, s):
                for j in range(8 - SPN):
                    pg = pool.snap(numbers[j], min_val=0, max_val=NPOOL - 1)
                    pool.dma_start(kpage(s, SPN + j), a["kT"][bass.ds(pg, 1)].rearrange("a p n -> (a p) n")
                                   ).then_inc(s_kp[s], 16)

            def v_pages(r, g, s):
                for j in range(8 - SPN):
                    pg = pool.snap(numbers[j], min_val=0, max_val=NPOOL - 1)
                    pool.dma_start(vpage(s, SPN + j), a["vc"][bass.ds(pg, 1)].rearrange("a p n -> (a p) n")
                                   ).then_inc(s_vp[s], 16)

            pool.wait_ge(s_con, 112)
            pool.wait_ge(s_ha, NA)
            with pool.Fori(0, 2) as r:
                for g in (1, 0):
                    step_pages(r, g)
                    pool.wait_ge(s_ov, 2 + 17 * r - g)
                    k_pages(r, g, g)
                with pool.Fori(1, 8) as gg:
                    for s in range(2):
                        step_pages(r, 2 * gg + s)
                        pool.wait_ge(s_sk, 17 * r + 2 * gg + s - 1)
                        k_pages(r, 2 * gg + s, s)
                for g in range(3):
                    step_pages(r, g)
                    pool.wait_ge(s_sk, 17 * r + (15 if g == 0 else 16))
                    v_pages(r, g, g)
                with pool.Fori(1, 5) as gg:
                    for s in range(3):
                        step_pages(r, 3 * gg + s)
                        pool.wait_ge(s_ov, 2 + 17 * r + 3 * gg + s - 1)
                        v_pages(r, 3 * gg + s, s)
                step_pages(r, 15)
                pool.wait_ge(s_ov, 2 + 17 * r + 14)
                v_pages(r, 15, 0)


            pool.wait_ge(s_z, 16)
            pool.wait_ge(s_r, R_SLOT)
            for t in range(TILES):
                n = ROWS[t]
                for k in range(2):
                    gp.indirect_dma_start(tokd, bass.IndirectOffsetOnAxis(ap=slotu[0:n, k, t:t + 1], axis=0),
                                         con[0:n, CTOK + t:CTOK + t + 1], None).then_inc(s_tk, 16)
            pool.wait_ge(s_tk, 32 * TILES)
            pool.wait_ge(s_r, R_SLOT + 2)
            gp.dma_start(tokrow, tokd.rearrange("(q p) o -> q (p o)", p=P)).then_inc(s_tl, 16)
            pool.wait_ge(s_r, R_STEPS)
            pool.wait_ge(s_x1, 16 * TILES)

            def gather(m, p, xs):
                sl = slice(p, p + 1) if isinstance(p, int) else bass.ds(p, 1)
                if not (isinstance(p, int) and p < 2):
                    pool.wait_ge(m.xt, p - 1)
                gp.tensor_copy(idc[:, xs:xs + 1], idx[:, sl]).then_inc(m.ic, 1)
                pool.wait_ge(m.ic, p + 1)
                pool.sem_inc(s_own, 1)
                gp.indirect_dma_start(xg[:, xs], None, x1d, bass.IndirectOffsetOnAxis(ap=idc[:, xs:xs + 1], axis=0)
                                      ).then_inc(m.xg[xs], 16)

            for s in range(2):
                gather(moe, s, s)
            with pool.Fori(1, EPAIRS // 2) as i:
                for s in range(2):
                    gather(moe, 2 * i + s, s)
            blocks = pool.value_load(ovi[0:1, 16:17], min_val=0, max_val=OVB)
            overflow(pool, blocks, lambda p, s, n: gather(moe, p, s))
            pool.wait_ge(s_ovr, 1)
            for t in range(TILES):
                n = ROWS[t]
                if t >= 2:
                    pool.wait_ge(s_hf, HF_STEPS * (t - 2) + 2)
                for k in range(2):
                    gp.indirect_dma_start(fb[0:n, 2 * k + t % 2], None, ybd,
                                         bass.IndirectOffsetOnAxis(ap=slotu[0:n, k, t:t + 1], axis=0)
                                         ).then_inc(s_gt[t % 2][k], 16)


def constants():
    con = np.zeros((P, NCON), np.float32)
    q = np.arange(P)
    con[:, CI:CI + P] = np.eye(P)
    con[:, C1:C1 + P] = 1.0
    con[:, CU:CU + P] = q[:, None] < q[None, :]
    con[:, CM + 384:CM + 512] = np.where(q[None, :] <= q[:, None], 0.0, NEG)
    con[:, CTHR:CTHR + 8] = CAP * np.arange(1, 9)
    con[:, CGID:CGID + 32] = np.arange(32) // EPG
    con[:, CEID:CEID + 32] = np.arange(32)
    con[:, CEB:CEB + 32] = CAP * np.arange(32)
    for r in range(2):
        con[:, CM8 + NS * r:CM8 + NS * (r + 1)] = (4 * r + q // 32)[:, None] == np.arange(NS)[None, :]
    for t in range(TILES):
        con[:, CTOK + t] = np.minimum(t * P + q, T - 1)
        con[:, CVAL + t] = t * P + q < T
    con[:, CBLK:CBLK + 16] = np.arange(16)
    for j in range(4):
        for i in range(NS):
            con[32 * j + 24 + i, CSUM + i] = con[32 * j + i, CSUM + NS + i] = 1.0
    for r in range(ROPE):
        con[64 + r, CSEL + r] = con[96 + r, CSEL + r] = 1.0
    half = ROPE // 2
    inv = (1.0 / (10000.0 ** (np.arange(half, dtype=np.float32) / half))).astype(np.float32)
    pos = np.concatenate([np.arange(NPR), np.full(NS, PAGE * NPAGES)]).astype(np.float32)
    ang = (pos[None, :] * inv[:, None]).astype(np.float32)
    c, s = np.cos(ang), np.sin(ang)
    c2, s2 = np.concatenate([c, c]), np.concatenate([-s, s])
    rope = np.zeros((3, P, T), np.float32)
    rope[0, 64:96], rope[0, 96:128] = c2, s2
    rope[1, 64:96] = rope[1, 96:128] = c2
    rope[2, 64:96] = rope[2, 96:128] = s2
    return con, rope


def chunks(w, p=P):
    return w.reshape(-1, p, w.shape[-1]).transpose(1, 0, 2)


def laid_out(i):
    x = np.concatenate([i["x_prompt"].reshape(NPR, D), i["x_sample"].reshape(NS, D)])
    w_in = i["w_in"][0]
    o_kv, o_kr, o_cv = QL, QL + KVL, QL + KVL + ROPE
    o_ga = o_cv + 2 * CC
    kr = w_in[:, o_kr:o_kr + ROPE]
    krs = np.concatenate([kr[:, 16:], kr[:, :16]], 1)
    first = np.concatenate([w_in[:, o_kv:o_kv + KVL], krs, krs, kr, kr, w_in[:, :QL], w_in[:, o_cv:o_cv + 2 * CC]], 1)

    def blocks(w):
        return chunks(w).reshape(P, -1, w.shape[1] // P, P).transpose(2, 0, 1, 3)

    uq = i["w_uq"][0].reshape(QL, HEADS, NOPE + ROPE)
    uq = np.concatenate([uq[..., :NOPE], uq[..., NOPE:], uq[..., NOPE + 16:], uq[..., NOPE:NOPE + 16]], -1)
    uq = uq.reshape(KQ, P, HEADS, P).transpose(2, 1, 0, 3)
    uq = uq.reshape(PAIRS, 2, P, KQ * P).transpose(0, 2, 1, 3).reshape(PAIRS, P, 2 * KQ * P)
    uk, uv = i["w_uk"][0], i["w_uv"][0]

    def by_pair(w):
        return w.reshape(KKV, P, PAIRS, 2 * w.shape[-1]).transpose(2, 1, 0, 3).reshape(PAIRS, P, -1)

    ukt = np.zeros((PAIRS, P, 2, KVL), np.float32)
    ukt[:, :NOPE] = uk.transpose(2, 1, 0).reshape(NOPE, PAIRS, 2, KVL).transpose(1, 0, 2, 3)
    wpair = np.concatenate([uq, by_pair(uk), by_pair(uv), ukt.reshape(PAIRS, P, -1)], -1)
    gates = np.concatenate([blocks(w_in[:, o_ga:o_ga + D]), blocks(i["w_pw2"][0]), blocks(w_in[:, o_ga + D:])], 2)
    vec = np.concatenate([np.asarray(v).reshape(-1, P).T for v in
                          (i["q_norm_g"][0], i["kv_norm_g"][0], i["b_dw"][0], i["conv_ln_g"][0], i["conv_ln_b"][0])]
                         + [i["w_dw"][0].T.reshape(KC, P, CW).transpose(1, 0, 2).reshape(P, KC * CW)], 1)
    state = np.zeros((P, KC, NS, CW), np.float32)
    state[..., :CW - 1] = i["state_conv"][0].transpose(2, 0, 1).reshape(KC, P, NS, CW - 1).transpose(1, 0, 2, 3)
    ex = np.concatenate([i["w_gate"][0], i["w_up"][0]], -1).reshape(NEXP, KD, P, 2 * DE).transpose(0, 2, 1, 3)
    dn = i["w_down"][0].reshape(NEXP, 2, P, D).transpose(0, 2, 1, 3)
    con, rope = constants()
    rows = np.stack([i[n][0] for n in ("ln1_g", "ln1_b", "ln2_g", "ln2_b", "ple_norm_g")])
    ple = np.concatenate([i["p_prompt"][0].reshape(NPR, -1), i["p_sample"][0].reshape(NS, -1)])
    ckv, ckr = i["cache_ckv"][0], i["cache_krope"][0]
    kT = np.concatenate([ckv[..., :KR], ckv[..., P:P + KR], ckr, ckv[..., KR:P], ckv[..., P + KR:]], 2).transpose(0, 2, 1)
    steps = i["page_table"].reshape(2, 4, NPAGES // 2, 2).transpose(0, 2, 1, 3)
    out = {
        "xT": chunks(x.T), "x": x, "w1": np.roll(blocks(first), NCV, axis=0), "wpair": wpair, "wgate": gates, "wo": blocks(i["w_o_attn"][0]),
        "wuv": chunks(uv.reshape(KVL, -1)), "w_out": chunks(i["w_out"][0]),
        "w_rt": chunks(np.concatenate([i["w_group"][0], i["w_router"][0]], 1)),
        "wexp": np.concatenate([ex.reshape(NEXP, P, -1), dn.reshape(NEXP, P, -1)], -1),
        "w_plg": chunks(i["w_ple_gate"][0]), "w_plp": chunks(i["w_ple_proj"][0]), "plT": chunks(ple.T),
        "kT": kT.reshape(NPOOL, 3, KR, PAGE).transpose(0, 2, 1, 3).reshape(NPOOL, KR, 3 * PAGE), "vc": ckv,
        "state": state, "vec": vec, "con": con, "rope": rope,
        "lnrows": np.broadcast_to(rows[None], (P, 5, D)), "pages": steps.reshape(1, -1),
    }
    return {n: np.ascontiguousarray(v) for n, v in out.items()}


OUTS = {"y": (T, D), "ckv": (P, KKV, T), "krope": (ROPE, T), "conv_p": (P, KC, CW - 1), "conv_s": (P, KC, NS, CW)}


def kernel(**inputs):
    import concourse.bacc as bacc
    from concourse.bass_utils import run_bass_kernel_spmd

    arrays = laid_out({n: np.asarray(v) for n, v in inputs.items()})
    nc = bacc.Bacc("TRN2", target_bir_lowering=False, num_devices=1)
    a = {n: nc.dram_tensor(f"in_{n}", v.shape, mybir.dt.from_np(v.dtype), kind="ExternalInput").ap()
         for n, v in arrays.items()}
    o = {n: nc.dram_tensor(f"out_{n}", s, F32, kind="ExternalOutput").ap() for n, s in OUTS.items()}
    decoder_layer(nc, a, o)
    r = run_bass_kernel_spmd(nc, [{f"in_{n}": v for n, v in arrays.items()}], core_ids=[0]).results[0]
    y, ckv, kr, cp, cs = (r[f"out_{n}"] for n in ("y", "ckv", "krope", "conv_p", "conv_s"))
    ckv = ckv.transpose(2, 1, 0).reshape(T, KVL)
    kr = kr.T
    cp = cp.transpose(2, 1, 0).reshape(CW - 1, CC)
    cs = cs[..., 1:].transpose(2, 3, 1, 0).reshape(NS, CW - 1, CC)
    return (y[:NPR].reshape(1, NPR, D), y[NPR:].reshape(NS, 1, D),
            ckv[:NPR].reshape(1, 1, NPR, KVL), kr[:NPR].reshape(1, 1, NPR, ROPE), cp.reshape(1, 1, CW - 1, CC),
            ckv[NPR:].reshape(1, NS, 1, KVL), kr[NPR:].reshape(1, NS, 1, ROPE), cs.reshape(1, NS, CW - 1, CC))
```
